# Optimizing a Trainium2 kernel written in Bass

```python
import jax, jax.numpy as jnp
from jax import lax
import numpy as np
import math

D_MODEL = 1024
BATCH = 1
SEQ = 512
DEPTH = 1

HEAD_DIM = D_MODEL // 16
RET_HEADS = 8
NSA_HEADS = 8
NSA_KV_GROUPS = 2
HEADS_PER_GROUP = NSA_HEADS // NSA_KV_GROUPS
RET_WIDTH = RET_HEADS * HEAD_DIM
NSA_WIDTH = NSA_HEADS * HEAD_DIM
MIX_WIDTH = RET_WIDTH + NSA_WIDTH
KV_WIDTH = NSA_KV_GROUPS * HEAD_DIM
RET_CHUNK = 128
RET_ROPE_BASE = 10000.0
NSA_ROPE_BASE = 500000.0
ROPE_DIM = HEAD_DIM // 4
CMP_BLOCK = 32
CMP_STRIDE = 16
CMP_HIDDEN = 256
SLC_BLOCK = 64
SLC_TOPK = 16
WINDOW = 512
NSA_QBLK = 64
NEG = -1e30
BIG = 1e9
EPS = 1e-6
SPLITS = (RET_WIDTH, RET_WIDTH, RET_WIDTH, RET_WIDTH, NSA_WIDTH, 6 * KV_WIDTH, 3 * NSA_HEADS, NSA_WIDTH)
PROJ_WIDTH = sum(SPLITS)


def rmsnorm(x, g):
    xf = x.astype(jnp.float32)
    y = xf * lax.rsqrt(jnp.mean(xf * xf, axis=-1, keepdims=True) + EPS) * g.astype(jnp.float32)
    return y.astype(x.dtype)

def rotary(x, pos, base, rot_dim):
    half = rot_dim // 2
    inv = jnp.power(base, -jnp.arange(half, dtype=jnp.float32) / half)
    ang = pos.astype(jnp.float32)[..., None] * inv
    cos = jnp.cos(ang)[:, :, None, :]
    sin = jnp.sin(ang)[:, :, None, :]
    x1 = x[..., :half].astype(jnp.float32)
    x2 = x[..., half:rot_dim].astype(jnp.float32)
    out = jnp.concatenate([(x1 * cos - x2 * sin).astype(x.dtype),
                           (x1 * sin + x2 * cos).astype(x.dtype),
                           x[..., rot_dim:]], axis=-1)
    return out

def masked_softmax(s, mask):
    s = jnp.where(mask, s.astype(jnp.float32), NEG)
    return jax.nn.softmax(s, axis=-1) * mask

def retention(q, k, v, pos):
    B, S, H, Dh = q.shape
    q = rotary(q, pos, RET_ROPE_BASE, Dh).astype(jnp.float32) * (Dh ** -0.5)
    k = rotary(k, pos, RET_ROPE_BASE, Dh).astype(jnp.float32)
    v = v.astype(jnp.float32)
    log_g = jnp.log1p(-jnp.power(2.0, -5.0 - jnp.arange(H, dtype=jnp.float32)))
    C = RET_CHUNK
    N = S // C
    qc = q.reshape(B, N, C, H, Dh)
    kc = k.reshape(B, N, C, H, Dh)
    vc = v.reshape(B, N, C, H, Dh)
    idx = jnp.arange(C, dtype=jnp.float32)
    diff = idx[:, None] - idx[None, :]
    decay = jnp.where(diff[None] >= 0, jnp.exp(jnp.maximum(diff, 0.0)[None] * log_g[:, None, None]), 0.0)
    scores = jnp.einsum('bnihd,bnjhd->bnhij', qc, kc) * decay
    inner = jnp.einsum('bnhij,bnjhe->bnihe', scores, vc)
    zeta = jnp.exp((C - 1 - idx)[None, :] * log_g[:, None])
    kv_chunk = jnp.einsum('bnjhd,hj,bnjhe->nbhde', kc, zeta, vc)
    chunk_decay = jnp.exp(C * log_g)[None, :, None, None]

    def step(R, kv):
        return R * chunk_decay + kv, R

    _, R_prev = lax.scan(step, jnp.zeros((B, H, Dh, Dh), jnp.float32), kv_chunk)
    xi = jnp.exp((idx + 1.0)[None, :] * log_g[:, None])
    cross = jnp.einsum('bnihd,nbhde,hi->bnihe', qc, R_prev, xi)
    o = (inner + cross).reshape(B, S, H, Dh)
    mu = jnp.mean(o, axis=-1, keepdims=True)
    var = jnp.mean(jnp.square(o - mu), axis=-1, keepdims=True)
    return (o - mu) * lax.rsqrt(var + 1e-5)

def compress(t, pe, w1, w2):
    B, S, G, Dh = t.shape
    Nc = (S - CMP_BLOCK) // CMP_STRIDE + 1
    cidx = np.arange(Nc)[:, None] * CMP_STRIDE + np.arange(CMP_BLOCK)[None, :]
    blocks = t[:, cidx] + pe[None, None, :, None, :].astype(t.dtype)
    flat = blocks.transpose(0, 1, 3, 2, 4).reshape(B, Nc, G, CMP_BLOCK * Dh)
    return jax.nn.silu(flat @ w1) @ w2

def nsa(q, kv_all, gate_logits, pos, pe_k, w1_k, w2_k, pe_v, w1_v, w2_v):
    B, S, Hq, Dh = q.shape
    G, hpg = NSA_KV_GROUPS, HEADS_PER_GROUP
    kv = kv_all.reshape(B, S, 6, G, Dh)
    k_c, v_c, k_s, v_s, k_w, v_w = [kv[:, :, i] for i in range(6)]
    q = rotary(q, pos, NSA_ROPE_BASE, ROPE_DIM) * (Dh ** -0.5)
    k_s = rotary(k_s, pos, NSA_ROPE_BASE, ROPE_DIM)
    k_w = rotary(k_w, pos, NSA_ROPE_BASE, ROPE_DIM)
    Nc = (S - CMP_BLOCK) // CMP_STRIDE + 1
    NS = S // SLC_BLOCK
    topk = min(SLC_TOPK, NS)
    cmp_start = np.arange(Nc) * CMP_STRIDE
    cmp_end = cmp_start + CMP_BLOCK - 1
    slc_start = np.arange(NS) * SLC_BLOCK
    overlap = jnp.asarray(((cmp_start[:, None] <= slc_start[None, :] + SLC_BLOCK - 1) &
                           (cmp_end[:, None] >= slc_start[None, :])).astype(np.float32))
    kc = rotary(compress(k_c, pe_k, w1_k, w2_k), pos[:, cmp_end], NSA_ROPE_BASE, ROPE_DIM)
    vc = compress(v_c, pe_v, w1_v, w2_v)
    kcT = kc.transpose(0, 2, 1, 3)
    vcT = vc.transpose(0, 2, 1, 3)
    qg = q.reshape(B, S, G, hpg, Dh).transpose(0, 2, 3, 1, 4)
    ks_blk = k_s.reshape(B, NS, SLC_BLOCK, G, Dh).transpose(0, 3, 1, 2, 4)
    vs_blk = v_s.reshape(B, NS, SLC_BLOCK, G, Dh).transpose(0, 3, 1, 2, 4)
    pad = ((0, 0), (0, 0), (WINDOW, 0), (0, 0))
    kw_pad = jnp.pad(k_w.transpose(0, 2, 1, 3), pad)
    vw_pad = jnp.pad(v_w.transpose(0, 2, 1, 3), pad)
    bidx = jnp.arange(B)[:, None, None, None]
    gidx = jnp.arange(G)[None, :, None, None]
    blk_ids = jnp.arange(NS)

    def block(bi):
        t0 = bi * NSA_QBLK
        qb = lax.dynamic_slice_in_dim(qg, t0, NSA_QBLK, axis=3)
        tq = t0 + jnp.arange(NSA_QBLK)
        s = jnp.einsum('bghqd,bgnd->bghqn', qb, kcT)
        p_cmp = masked_softmax(s, cmp_end[None, :] <= tq[:, None])
        o_cmp = jnp.einsum('bghqn,bgnd->bghqd', p_cmp, vcT.astype(jnp.float32))
        imp = jnp.einsum('bghqn,ns->bgqs', p_cmp, overlap)
        cur = tq // SLC_BLOCK
        valid = blk_ids[None, :] <= cur[:, None]
        forced = (blk_ids[None, :] == 0) | (blk_ids[None, :] == cur[:, None]) | (blk_ids[None, :] == cur[:, None] - 1)
        score = jnp.where(forced, BIG, jnp.where(valid, imp, NEG))
        top_val, top_idx = lax.top_k(score, topk)
        kg = ks_blk[bidx, gidx, top_idx]
        vg = vs_blk[bidx, gidx, top_idx]
        s = jnp.einsum('bghqd,bgqnkd->bghqnk', qb, kg).reshape(B, G, hpg, NSA_QBLK, topk * SLC_BLOCK)
        tok = top_idx[..., None] * SLC_BLOCK + jnp.arange(SLC_BLOCK)
        m = (tok <= tq[None, None, :, None, None]) & (top_val > 0.5 * NEG)[..., None]
        p_slc = masked_softmax(s, m.reshape(B, G, 1, NSA_QBLK, topk * SLC_BLOCK))
        o_slc = jnp.einsum('bghqm,bgqmd->bghqd', p_slc,
                           vg.reshape(B, G, NSA_QBLK, topk * SLC_BLOCK, Dh).astype(jnp.float32))
        kwb = lax.dynamic_slice_in_dim(kw_pad, t0, WINDOW + NSA_QBLK, axis=2)
        vwb = lax.dynamic_slice_in_dim(vw_pad, t0, WINDOW + NSA_QBLK, axis=2)
        kp = t0 - WINDOW + jnp.arange(WINDOW + NSA_QBLK)
        mw = (kp[None, :] >= 0) & (kp[None, :] <= tq[:, None]) & (tq[:, None] - kp[None, :] < WINDOW)
        s = jnp.einsum('bghqd,bgkd->bghqk', qb, kwb)
        p_win = masked_softmax(s, mw)
        o_win = jnp.einsum('bghqk,bgkd->bghqd', p_win, vwb.astype(jnp.float32))
        return o_cmp, o_slc, o_win

    o_cmp, o_slc, o_win = lax.map(block, jnp.arange(S // NSA_QBLK))
    to_bshd = lambda o: o.transpose(1, 0, 4, 2, 3, 5).reshape(B, S, Hq, Dh)
    g = jax.nn.sigmoid(gate_logits.astype(jnp.float32)).reshape(B, S, Hq, 3)
    o = g[..., 0:1] * to_bshd(o_cmp) + g[..., 1:2] * to_bshd(o_slc) + g[..., 2:3] * to_bshd(o_win)
    return o

def first_inputs(seed: int = 0) -> dict:
    key = jax.random.key(seed)
    ks = jax.random.split(key, 20)
    f32 = jnp.float32
    nrm = lambda k, shape, scale: jax.random.normal(k, shape, f32) * scale
    x = jax.random.normal(ks[0], (BATCH, SEQ, D_MODEL), f32)
    c = jax.random.normal(ks[1], (BATCH, D_MODEL), f32)
    start = jax.random.randint(ks[2], (BATCH, 1), 0, 1024, dtype=jnp.int32)
    positions = start + jnp.arange(SEQ, dtype=jnp.int32)[None, :]
    return {
        "x": x,
        "c": c,
        "positions": positions,
        "w_ada": nrm(ks[3], (DEPTH, D_MODEL, 3 * D_MODEL), 0.5 * D_MODEL ** -0.5),
        "b_ada": nrm(ks[4], (DEPTH, 3 * D_MODEL), 0.02),
        "g_pre": 1.0 + nrm(ks[5], (DEPTH, D_MODEL), 0.05),
        "g_post": 1.0 + nrm(ks[6], (DEPTH, D_MODEL), 0.05),
        "w_in": nrm(ks[7], (DEPTH, D_MODEL, PROJ_WIDTH), D_MODEL ** -0.5),
        "w_out": nrm(ks[8], (DEPTH, MIX_WIDTH, D_MODEL), MIX_WIDTH ** -0.5),
        "cmp_pe_k": nrm(ks[9], (DEPTH, CMP_BLOCK, HEAD_DIM), 0.1),
        "cmp_w1_k": nrm(ks[10], (DEPTH, CMP_BLOCK * HEAD_DIM, CMP_HIDDEN), (CMP_BLOCK * HEAD_DIM) ** -0.5),
        "cmp_w2_k": nrm(ks[11], (DEPTH, CMP_HIDDEN, HEAD_DIM), CMP_HIDDEN ** -0.5),
        "cmp_pe_v": nrm(ks[12], (DEPTH, CMP_BLOCK, HEAD_DIM), 0.1),
        "cmp_w1_v": nrm(ks[13], (DEPTH, CMP_BLOCK * HEAD_DIM, CMP_HIDDEN), (CMP_BLOCK * HEAD_DIM) ** -0.5),
        "cmp_w2_v": nrm(ks[14], (DEPTH, CMP_HIDDEN, HEAD_DIM), CMP_HIDDEN ** -0.5),
    }

def first_block(x, c, positions, w_ada, b_ada, g_pre, g_post, w_in, w_out,
              cmp_pe_k, cmp_w1_k, cmp_w2_k, cmp_pe_v, cmp_w1_v, cmp_w2_v):
    B, S, _ = x.shape
    offsets = np.cumsum(SPLITS)[:-1].tolist()
    for l in range(DEPTH):
        mod = jax.nn.silu(c) @ w_ada[l] + b_ada[l]
        shift, scale, gate = jnp.split(mod, 3, axis=-1)
        h = rmsnorm(x, g_pre[l]) * (1.0 + scale[:, None, :]) + shift[:, None, :]
        proj = h @ w_in[l]
        rq, rk, rv, rg, nq, nkv, ngl, ng = jnp.split(proj, offsets, axis=-1)
        hd = lambda t, H: t.reshape(B, S, H, HEAD_DIM)
        ret = retention(hd(rq, RET_HEADS), hd(rk, RET_HEADS), hd(rv, RET_HEADS), positions)
        ret = ret.reshape(B, S, RET_WIDTH) * jax.nn.silu(rg.astype(jnp.float32))
        att = nsa(hd(nq, NSA_HEADS), nkv, ngl, positions,
                  cmp_pe_k[l], cmp_w1_k[l], cmp_w2_k[l], cmp_pe_v[l], cmp_w1_v[l], cmp_w2_v[l])
        att = att.reshape(B, S, NSA_WIDTH) * jax.nn.silu(ng.astype(jnp.float32))
        mixed = jnp.concatenate([ret, att], axis=-1).astype(x.dtype)
        y = rmsnorm(mixed @ w_out[l], g_post[l])
        x = x + gate[:, None, :].astype(x.dtype) * y
    return x


MLA_HEADS = 8
QK_NOPE = 64
QK_ROPE = 32
QK_HEAD = QK_NOPE + QK_ROPE
V_HEAD = 64
Q_LORA = 256
KV_LORA = 128
ROPE_THETA = 10000.0
Q_BLOCK = 128
RWKV_HEADS = 8
RWKV_HEAD = 64
RWKV_DIM = RWKV_HEADS * RWKV_HEAD
DECAY_LORA = 64
AAA_LORA = 64
GATE_LORA = 128
GN_EPS = 64e-5
PEER_HEADS = 8
N_KEYS = 128
N_EXPERTS = N_KEYS * N_KEYS
D_KEY = 256
HALF_KEY = D_KEY // 2
TOPK_HALF = 16
TOPK = 16
PEER_BLOCK = 64
N_BRANCH = 2
MLA_IN = Q_LORA + KV_LORA + QK_ROPE
RWKV_IN = 3 * RWKV_DIM + DECAY_LORA + AAA_LORA + GATE_LORA
GATE_IN = N_BRANCH * D_MODEL
IN_DIM = MLA_IN + RWKV_IN + GATE_IN
N_MOD = 6


def rms_norm(x, g, eps=EPS):
    xf = x.astype(jnp.float32)
    y = xf * lax.rsqrt(jnp.mean(xf * xf, axis=-1, keepdims=True) + eps)
    return (y * g.astype(jnp.float32)).astype(x.dtype)

def modulate(h, shift, scale):
    return h * (1.0 + scale[:, None, :]) + shift[:, None, :]

def rope(x, positions):
    half = x.shape[-1] // 2
    inv_freq = ROPE_THETA ** (-jnp.arange(half, dtype=jnp.float32) / half)
    ang = positions.astype(jnp.float32)[..., None] * inv_freq
    cos = jnp.cos(ang)[:, :, None, :]
    sin = jnp.sin(ang)[:, :, None, :]
    xf = x.astype(jnp.float32)
    x1, x2 = xf[..., :half], xf[..., half:]
    return jnp.concatenate([x1 * cos - x2 * sin, x1 * sin + x2 * cos], axis=-1).astype(x.dtype)

def causal_block_attention(q, k, v):
    B, S, H, Dq = q.shape
    nb = S // Q_BLOCK
    scale = Dq ** -0.5
    qb = q.reshape(B, nb, Q_BLOCK, H, Dq).transpose(1, 0, 2, 3, 4)
    kpos = jnp.arange(S)

    def one_block(args):
        i, q_blk = args
        s = jnp.einsum('bqhd,bkhd->bhqk', q_blk, k).astype(jnp.float32) * scale
        qpos = i * Q_BLOCK + jnp.arange(Q_BLOCK)
        mask = kpos[None, :] <= qpos[:, None]
        s = jnp.where(mask[None, None], s, -jnp.inf)
        p = jax.nn.softmax(s, axis=-1).astype(v.dtype)
        return jnp.einsum('bhqk,bkhd->bqhd', p, v)

    out = lax.map(one_block, (jnp.arange(nb), qb))
    return out.transpose(1, 0, 2, 3, 4).reshape(B, S, H, v.shape[-1])

def mla_branch(q_a, kv_a, k_rope_raw, positions, q_a_norm, w_uq, kv_a_norm, w_ukv, q_norm, k_norm, w_o_mla):
    B, S, _ = q_a.shape
    cq = rms_norm(q_a, q_a_norm)
    q = (cq @ w_uq).reshape(B, S, MLA_HEADS, QK_HEAD)
    ckv = rms_norm(kv_a, kv_a_norm)
    kv = (ckv @ w_ukv).reshape(B, S, MLA_HEADS, QK_NOPE + V_HEAD)
    k_nope, v = kv[..., :QK_NOPE], kv[..., QK_NOPE:]
    q_nope = rms_norm(q[..., :QK_NOPE], q_norm[:QK_NOPE])
    q_pe = rope(rms_norm(q[..., QK_NOPE:], q_norm[QK_NOPE:]), positions)
    k_nope = rms_norm(k_nope, k_norm[:QK_NOPE])
    k_pe = rope(rms_norm(k_rope_raw[:, :, None, :], k_norm[QK_NOPE:]), positions)
    k_pe = jnp.broadcast_to(k_pe, (B, S, MLA_HEADS, QK_ROPE))
    qh = jnp.concatenate([q_nope, q_pe], axis=-1)
    kh = jnp.concatenate([k_nope, k_pe], axis=-1)
    o = causal_block_attention(qh, kh, v)
    return o.reshape(B, S, MLA_HEADS * V_HEAD) @ w_o_mla

def token_shift(p, mu):
    prev = jnp.pad(p, ((0, 0), (1, 0), (0, 0)))[:, :-1]
    return p + (prev - p) * mu

def rwkv7_scan(r, decay, k, v, kk, a):
    B, S, H, N = r.shape
    b = kk * a

    def step(state, inp):
        r_t, w_t, k_t, v_t, kk_t, b_t = inp
        sa = jnp.einsum('bhvk,bhk->bhv', state, -kk_t)
        state = (state * w_t[:, :, None, :] + sa[..., None] * b_t[:, :, None, :]
                 + v_t[..., None] * k_t[:, :, None, :])
        y = jnp.einsum('bhvk,bhk->bhv', state, r_t)
        return state, y

    xs = tuple(t.transpose(1, 0, 2, 3) for t in (r, decay, k, v, kk, b))
    s0 = jnp.zeros((B, H, N, N), jnp.float32)
    _, y = lax.scan(step, s0, xs)
    return y.transpose(1, 0, 2, 3)

def rwkv7_branch(p, mu_shift, w_decay_up, decay_base, w_aaa_up, aaa_base, w_gate_up,
                 k_k, k_a, r_k, ln_x_w, ln_x_b, w_o_rwkv):
    B, S, _ = p.shape
    p = token_shift(p, mu_shift)
    splits = [RWKV_DIM, 2 * RWKV_DIM, 3 * RWKV_DIM, 3 * RWKV_DIM + DECAY_LORA,
              3 * RWKV_DIM + DECAY_LORA + AAA_LORA]
    r, k, v, wd, ad, gd = jnp.split(p, splits, axis=-1)
    w = -jax.nn.softplus(-(decay_base + jnp.tanh(wd) @ w_decay_up)) - 0.5
    decay = jnp.exp(-jnp.exp(w.astype(jnp.float32)))
    a = jax.nn.sigmoid(aaa_base + ad @ w_aaa_up)
    g = jax.nn.sigmoid(gd) @ w_gate_up

    def heads(t):
        return t.reshape(B, S, RWKV_HEADS, RWKV_HEAD).astype(jnp.float32)

    kk = heads(k * k_k)
    kk = kk / jnp.maximum(jnp.linalg.norm(kk, axis=-1, keepdims=True), 1e-12)
    a_h = heads(a)
    k_h = heads(k) * (1.0 + (a_h - 1.0) * k_a.reshape(RWKV_HEADS, RWKV_HEAD).astype(jnp.float32))
    r_h, v_h = heads(r), heads(v)
    y = rwkv7_scan(r_h, heads(decay), k_h, v_h, kk, a_h)
    mu = jnp.mean(y, axis=-1, keepdims=True)
    var = jnp.mean(jnp.square(y - mu), axis=-1, keepdims=True)
    y = (y - mu) * lax.rsqrt(var + GN_EPS)
    y = y * ln_x_w.reshape(RWKV_HEADS, RWKV_HEAD) + ln_x_b.reshape(RWKV_HEADS, RWKV_HEAD)
    y = y + jnp.sum(r_h * k_h * r_k, axis=-1, keepdims=True) * v_h
    y = y.reshape(B, S, RWKV_DIM).astype(p.dtype) * g
    return y @ w_o_rwkv

def token_mixer(h, positions, w_in, mu_shift, q_a_norm, w_uq, kv_a_norm, w_ukv, q_norm, k_norm, w_o_mla,
                w_decay_up, decay_base, w_aaa_up, aaa_base, w_gate_up, k_k, k_a, r_k, ln_x_w, ln_x_b,
                w_o_rwkv, w_out):
    proj = h @ w_in
    q_a, kv_a, k_rope_raw, rwkv_in, gate_logits = jnp.split(
        proj, [Q_LORA, Q_LORA + KV_LORA, MLA_IN, MLA_IN + RWKV_IN], axis=-1)
    o_mla = mla_branch(q_a, kv_a, k_rope_raw, positions, q_a_norm, w_uq, kv_a_norm, w_ukv,
                       q_norm, k_norm, w_o_mla)
    o_rwkv = rwkv7_branch(rwkv_in, mu_shift, w_decay_up, decay_base, w_aaa_up, aaa_base, w_gate_up,
                          k_k, k_a, r_k, ln_x_w, ln_x_b, w_o_rwkv)
    g_mla, g_rwkv = jnp.split(jax.nn.sigmoid(gate_logits), 2, axis=-1)
    return (g_mla * o_mla + g_rwkv * o_rwkv) @ w_out

def peer_ffn(h, w_query, sub_keys1, sub_keys2, expert_down, expert_up):
    B, S, D = h.shape
    q = (h @ w_query).reshape(B, S, PEER_HEADS, 2, HALF_KEY)
    s1 = jnp.einsum('bshd,nd->bshn', q[..., 0, :], sub_keys1).astype(jnp.float32)
    s2 = jnp.einsum('bshd,nd->bshn', q[..., 1, :], sub_keys2).astype(jnp.float32)
    v1, i1 = lax.top_k(s1, TOPK_HALF)
    v2, i2 = lax.top_k(s2, TOPK_HALF)
    cand = (v1[..., :, None] + v2[..., None, :]).reshape(B, S, PEER_HEADS, TOPK_HALF * TOPK_HALF)
    cand_idx = (i1[..., :, None] * N_KEYS + i2[..., None, :]).reshape(B, S, PEER_HEADS, TOPK_HALF * TOPK_HALF)
    top_v, pos = lax.top_k(cand, TOPK)
    expert_idx = jnp.take_along_axis(cand_idx, pos, axis=-1)
    gates = jax.nn.softmax(top_v, axis=-1).astype(h.dtype)
    nb = S // PEER_BLOCK
    hb = h.reshape(B, nb, PEER_BLOCK, D).transpose(1, 0, 2, 3)
    idxb = expert_idx.reshape(B, nb, PEER_BLOCK, PEER_HEADS, TOPK).transpose(1, 0, 2, 3, 4)
    gb = gates.reshape(B, nb, PEER_BLOCK, PEER_HEADS, TOPK).transpose(1, 0, 2, 3, 4)

    def one_block(args):
        h_blk, idx_blk, g_blk = args
        u = jnp.take(expert_down, idx_blk, axis=0)
        act = jax.nn.gelu(jnp.einsum('bpd,bphkd->bphk', h_blk, u))
        vv = jnp.take(expert_up, idx_blk, axis=0)
        return jnp.einsum('bphk,bphkd->bpd', g_blk * act, vv)

    out = lax.map(one_block, (hb, idxb, gb))
    return out.transpose(1, 0, 2, 3).reshape(B, S, D)

def second_inputs(seed: int = 0) -> dict:
    key = jax.random.key(seed)
    ks = jax.random.split(key, 40)
    f32 = jnp.float32

    def nrm(k, shape, scale):
        return jax.random.normal(k, (DEPTH,) + shape, f32) * scale

    def gain(k, shape):
        return 1.0 + 0.1 * jax.random.normal(k, (DEPTH,) + shape, f32)

    x = jax.random.normal(ks[0], (BATCH, SEQ, D_MODEL), f32)
    c = jax.random.normal(ks[1], (BATCH, D_MODEL), f32)
    offsets = jax.random.randint(ks[2], (BATCH, 1), 0, 1024, dtype=jnp.int32)
    positions = offsets + jnp.arange(SEQ, dtype=jnp.int32)[None, :]
    return {
        "x": x, "c": c, "positions": positions,
        "w_ada": nrm(ks[3], (D_MODEL, N_MOD * D_MODEL), 0.3 * D_MODEL ** -0.5),
        "b_ada": nrm(ks[4], (N_MOD * D_MODEL,), 0.05),
        "norm_mix": gain(ks[5], (D_MODEL,)),
        "w_in": nrm(ks[6], (D_MODEL, IN_DIM), D_MODEL ** -0.5),
        "mu_shift": jax.random.uniform(ks[7], (DEPTH, RWKV_IN), f32),
        "q_a_norm": gain(ks[8], (Q_LORA,)),
        "w_uq": nrm(ks[9], (Q_LORA, MLA_HEADS * QK_HEAD), Q_LORA ** -0.5),
        "kv_a_norm": gain(ks[10], (KV_LORA,)),
        "w_ukv": nrm(ks[11], (KV_LORA, MLA_HEADS * (QK_NOPE + V_HEAD)), KV_LORA ** -0.5),
        "q_norm": gain(ks[12], (QK_HEAD,)),
        "k_norm": gain(ks[13], (QK_HEAD,)),
        "w_o_mla": nrm(ks[14], (MLA_HEADS * V_HEAD, D_MODEL), (MLA_HEADS * V_HEAD) ** -0.5),
        "w_decay_up": nrm(ks[15], (DECAY_LORA, RWKV_DIM), 0.1),
        "decay_base": jax.random.uniform(ks[16], (DEPTH, RWKV_DIM), f32, -6.0, 2.0),
        "w_aaa_up": nrm(ks[17], (AAA_LORA, RWKV_DIM), 0.1),
        "aaa_base": nrm(ks[18], (RWKV_DIM,), 0.5),
        "w_gate_up": nrm(ks[19], (GATE_LORA, RWKV_DIM), GATE_LORA ** -0.5),
        "k_k": 0.85 + nrm(ks[20], (RWKV_DIM,), 0.1),
        "k_a": gain(ks[21], (RWKV_DIM,)),
        "r_k": nrm(ks[22], (RWKV_HEADS, RWKV_HEAD), 0.1),
        "ln_x_w": gain(ks[23], (RWKV_DIM,)),
        "ln_x_b": nrm(ks[24], (RWKV_DIM,), 0.02),
        "w_o_rwkv": nrm(ks[25], (RWKV_DIM, D_MODEL), RWKV_DIM ** -0.5),
        "w_out": nrm(ks[26], (D_MODEL, D_MODEL), D_MODEL ** -0.5),
        "norm_ffn": gain(ks[27], (D_MODEL,)),
        "w_query": nrm(ks[28], (D_MODEL, PEER_HEADS * D_KEY), D_MODEL ** -0.5),
        "sub_keys1": nrm(ks[29], (N_KEYS, HALF_KEY), HALF_KEY ** -0.5),
        "sub_keys2": nrm(ks[30], (N_KEYS, HALF_KEY), HALF_KEY ** -0.5),
        "expert_down": nrm(ks[31], (N_EXPERTS, D_MODEL), D_MODEL ** -0.5),
        "expert_up": nrm(ks[32], (N_EXPERTS, D_MODEL), PEER_HEADS ** -0.5),
    }

def second_block(x, c, positions, w_ada, b_ada, norm_mix, w_in, mu_shift, q_a_norm, w_uq, kv_a_norm, w_ukv,
              q_norm, k_norm, w_o_mla, w_decay_up, decay_base, w_aaa_up, aaa_base, w_gate_up, k_k, k_a, r_k,
              ln_x_w, ln_x_b, w_o_rwkv, w_out, norm_ffn, w_query, sub_keys1, sub_keys2, expert_down, expert_up):
    for l in range(DEPTH):
        mod = jax.nn.silu(c) @ w_ada[l] + b_ada[l]
        sh1, sc1, gt1, sh2, sc2, gt2 = jnp.split(mod, N_MOD, axis=-1)
        h = modulate(rms_norm(x, norm_mix[l]), sh1, sc1)
        mix = token_mixer(h, positions, w_in[l], mu_shift[l], q_a_norm[l], w_uq[l], kv_a_norm[l], w_ukv[l],
                          q_norm[l], k_norm[l], w_o_mla[l], w_decay_up[l], decay_base[l], w_aaa_up[l],
                          aaa_base[l], w_gate_up[l], k_k[l], k_a[l], r_k[l], ln_x_w[l], ln_x_b[l],
                          w_o_rwkv[l], w_out[l])
        x = x + gt1[:, None, :] * mix
        h = modulate(rms_norm(x, norm_ffn[l]), sh2, sc2)
        x = x + gt2[:, None, :] * peer_ffn(h, w_query[l], sub_keys1[l], sub_keys2[l], expert_down[l], expert_up[l])
    return x


def setup_inputs(seed=0):
    out = dict(first_inputs(seed))
    for name, value in second_inputs(seed + 1).items():
        if name != "x":
            out[name + "_2"] = value
    return out


def reference(
    x, c, positions, w_ada, b_ada, g_pre, g_post, w_in, w_out, cmp_pe_k, cmp_w1_k, cmp_w2_k,
    cmp_pe_v, cmp_w1_v, cmp_w2_v, c_2, positions_2, w_ada_2, b_ada_2, norm_mix_2, w_in_2,
    mu_shift_2, q_a_norm_2, w_uq_2, kv_a_norm_2, w_ukv_2, q_norm_2, k_norm_2, w_o_mla_2,
    w_decay_up_2, decay_base_2, w_aaa_up_2, aaa_base_2, w_gate_up_2, k_k_2, k_a_2, r_k_2,
    ln_x_w_2, ln_x_b_2, w_o_rwkv_2, w_out_2, norm_ffn_2, w_query_2, sub_keys1_2, sub_keys2_2,
    expert_down_2, expert_up_2,
):
    x = first_block(
        x, c, positions, w_ada, b_ada, g_pre, g_post, w_in, w_out, cmp_pe_k, cmp_w1_k, cmp_w2_k,
        cmp_pe_v, cmp_w1_v, cmp_w2_v,
    )
    return second_block(
        x, c_2, positions_2, w_ada_2, b_ada_2, norm_mix_2, w_in_2, mu_shift_2, q_a_norm_2,
        w_uq_2, kv_a_norm_2, w_ukv_2, q_norm_2, k_norm_2, w_o_mla_2, w_decay_up_2, decay_base_2,
        w_aaa_up_2, aaa_base_2, w_gate_up_2, k_k_2, k_a_2, r_k_2, ln_x_w_2, ln_x_b_2,
        w_o_rwkv_2, w_out_2, norm_ffn_2, w_query_2, sub_keys1_2, sub_keys2_2, expert_down_2,
        expert_up_2,
    )


_drawn_inputs = setup_inputs


def setup_inputs(seed=0):
    import zlib

    import numpy as np

    out = dict(_drawn_inputs(seed))
    spreads = {}
    factors = {'g_post': 3.475,
     'cmp_pe_k': 8.0,
     'cmp_w1_k': 3.345,
     'cmp_w2_k': 3.394,
     'cmp_pe_v': 8.0,
     'norm_mix_2': 5.172,
     'q_a_norm_2': 64.0,
     'w_uq_2': 19.383,
     'kv_a_norm_2': 64.0,
     'q_norm_2': 64.0,
     'k_norm_2': 64.0,
     'w_decay_up_2': 64.0,
     'w_aaa_up_2': 3.54,
     'aaa_base_2': 5.076,
     'k_k_2': 64.0,
     'k_a_2': 7.406,
     'r_k_2': 4.053,
     'ln_x_w_2': 64.0,
     'ln_x_b_2': 200.0,
     'norm_ffn_2': 37.6,
     'w_ukv_2': 4.844,
     'w_o_mla_2': 4.837,
     'decay_base_2': 8.0,
     'w_query_2': 8.0,
     'sub_keys1_2': 8.0,
     'sub_keys2_2': 8.0,
     'expert_down_2': 8.0,
     'expert_up_2': 8.0}
    for name, (base, spread) in spreads.items():
        noise = np.random.default_rng([zlib.crc32(name.encode()), seed]).standard_normal(out[name].shape)
        drawn = base * np.exp(spread * noise) if base else spread * noise
        out[name] = __import__('jax').numpy.asarray(drawn.astype(out[name].dtype))
    for name, factor in factors.items():
        out[name] = (out[name] * factor).astype(out[name].dtype)
    return out
```

```python
from contextlib import ExitStack

import numpy as np

import concourse.bass as bass
from concourse import mybir

F32 = mybir.dt.float32
BF16 = mybir.dt.bfloat16
I32 = mybir.dt.int32
U32 = mybir.dt.uint32
ALU = mybir.AluOpType
ACT = mybir.ActivationFunctionType
AXX = mybir.AxisListType.X
ADD, SUB, MUL, MAX, MIN, EQ, POW = (ALU.add, ALU.subtract, ALU.mult, ALU.max, ALU.min, ALU.is_equal, ALU.pow)

P = 128
NT = 4
D = 1024
NJ = 8
H = 8
PW1 = 3864
PW2 = 4256
RW = 1792
NE = 16384
GC = 8
NG = NE // P // GC
EM05 = float(np.exp(-0.5))


def constants():
    f = np.float32
    i = np.arange(128)
    c = {}
    c["ident"] = np.eye(128, dtype=f)
    c["caus"] = np.where(i[None, :] <= i[:, None], 0.0, -1e30).astype(f)
    c["iota"] = np.broadcast_to(i.astype(f), (128, 128))
    c["bd"] = (i[:, None] // 64 == i[None, :] // 64).astype(f)
    inv = [np.power(f(b), -np.arange(n, dtype=f) / f(n)).astype(f)
           for b, n in ((10000.0, 32), (500000.0, 8), (10000.0, 16))]
    c["inv"] = np.broadcast_to(np.concatenate(inv), (128, 56))
    c["nhalf"] = np.full((128, 32), -0.5, f)
    cst = np.ascontiguousarray(np.concatenate([c[k] for k in CST], axis=1), f)

    d = {}
    lg = np.log1p(-np.power(2.0, -5.0 - np.arange(H))).astype(f)
    diff = (i[None, :] - i[:, None]).astype(f)
    dec = np.where(diff[:, None, :] >= 0, np.exp(np.maximum(diff, 0)[:, None, :] * lg[None, :, None]), 0) * 0.125
    d["dec"] = dec.astype(f).reshape(128, 1024)
    d["zeta"] = np.exp((127 - i).astype(f)[:, None] * lg[None, :])
    d["xi"] = np.exp((i + 1).astype(f)[:, None] * lg[None, :]) * f(0.125)
    cd = np.exp(f(128) * lg)
    d["cd"] = np.concatenate([np.where(c["bd"] > 0, np.repeat(cd[2 * p:2 * p + 2], 64)[:, None], 0) for p in range(4)], 1)
    t = np.arange(512).reshape(4, 128)
    n = np.arange(32)
    ok = (n[None, None, :] * 16 + 31 <= t[:, :, None]) & (n < 31)
    ok = ok.transpose(1, 0, 2).reshape(128, 128)
    d["cneg"] = np.where(ok, 0.0, -1e30)
    d["cmul"] = ok.astype(f)
    d["hsel"] = 0.5 * (i[:, None] // 32 == np.arange(4)[None, :])
    c1 = np.ascontiguousarray(np.concatenate([d[k].astype(f) for k in C1], axis=1), f)

    e = {}
    same = i[:, None] // 64 == i[None, :] // 64
    e["tri"] = ((i[:, None] <= i[None, :]) & same).astype(f)
    e["mm"] = np.concatenate([((i[:, None] < i[None, :]) & same), ((i[:, None] <= i[None, :]) & same)], 1)

    def lev(l):
        b = 1 << (l - 1)
        t, s = i[:, None], i[None, :]
        return ((t // (2 * b) == s // (2 * b)) & (t // b % 2 == 1) & (s // b % 2 == 0)).astype(f)

    e["m1"] = lev(1)
    e["mt"] = np.concatenate([lev(l).T for l in range(1, 7)], 1)
    e["sel"] = (i[:, None] // 64 == np.arange(2)[None, :])
    c2 = np.ascontiguousarray(np.concatenate([e[k].astype(f) for k in C2], axis=1), f)
    return cst, c1, c2


CST = {"ident": 128, "caus": 128, "iota": 128, "bd": 128, "inv": 56, "nhalf": 32}
C1 = {"dec": 1024, "zeta": 8, "xi": 8, "cd": 512, "cneg": 128, "cmul": 128, "hsel": 4}
C2 = {"tri": 128, "mm": 256, "m1": 128, "mt": 768, "sel": 2}


class Queue:

    def __init__(self, sem):
        self.sem, self.n, self.items, self.seen = sem, 0, [], {}

    @property
    def t(self):
        return (self.sem, self.n)

    def wait(self, *toks):
        for sem, n in toks:
            if self.seen.get(id(sem), 0) < n:
                self.seen[id(sem)] = n
                self.items.append(lambda e, sem=sem, n=n: e.wait_ge(sem, n))

    def do(self, fn, *toks, inc=True):
        self.wait(*toks)
        if inc:
            self.n += 1
            self.items.append(lambda e: fn(e).then_inc(self.sem, 1))
        else:
            self.items.append(fn)
        return (self.sem, self.n)

    def dma(self, line, out, in_, *toks, **kw):
        self.wait(*toks)
        line[1] += 16
        self.items.append(lambda e: e.dma_start(out, in_, **kw).then_inc(line[0], 16))
        return (line[0], line[1])

    def emit(self, e):
        for f in self.items:
            f(e)


class Ring:

    def __init__(self, n):
        self.free, self.i = [[] for _ in range(n)], 0

    def take(self):
        k = self.i % len(self.free)
        self.i += 1
        toks, self.free[k] = self.free[k], None
        assert toks is not None, "buffer taken before it was given back"
        return k, toks

    def give(self, k, *toks):
        self.free[k] = list(toks)


class Space:
    def __init__(self, ap, base, size):
        self.ap, self.at, self.end = ap, base, base + size

    def get(self, *shape):
        n = int(np.prod(shape))
        assert self.at + n <= self.end, (self.at, n, self.end)
        v = self.ap[:, self.at:self.at + n]
        self.at += n
        if len(shape) == 1:
            return v
        names = "abcd"[:len(shape)]
        return v.rearrange(f"p ({' '.join(names)}) -> p {' '.join(names)}",
                           **{names[k]: shape[k] for k in range(len(shape))})

    def fork(self, n):
        assert self.at + n <= self.end
        s = Space(self.ap, self.at, n)
        self.at += n
        return s

    def rest(self):
        return Space(self.ap, self.at, self.end - self.at)


def bx(ap, axis, shape):
    return ap.unsqueeze(axis).to_broadcast(list(shape))


def build(nc, A, out, tap=None, stop=None):
    ctx = ExitStack()
    with ctx:
        def sem(name):
            return ctx.enter_context(nc.semaphore(name))

        def line(name):
            return [sem(name), 0]

        PE, V, S, G, SP = [Queue(sem(n)) for n in ("pe", "dve", "act", "pool", "sp")]
        QS = (PE, V, S, G)
        alln = 53208
        NCST = sum(CST.values())
        arena = ctx.enter_context(nc.sbuf_tensor("arena", [P, alln], F32))
        root = Space(arena[:, :], 0, alln)
        cst = root.get(NCST)
        C = {}
        o = 0
        for k, n in CST.items():
            C[k] = cst[:, o:o + n]
            o += n
        ident = C["ident"]
        nhalf = C["nhalf"]
        identb = root.get(64).bitcast(BF16)
        cmaskb = root.get(64).bitcast(BF16)
        hT = root.get(NJ, 512)
        gt1_2 = root.get(D)
        gt2_2 = root.get(D)
        colm = root.get(64)
        ccol = root.get(16)
        trig = root.get(9, 2, 32)
        NW = 3
        wslot = [root.get(4096) for _ in range(NW)]
        wring = Ring(NW)
        wline = [line(f"w{i}") for i in range(NW)]
        phase = root.rest()
        banks = [ctx.enter_context(nc.psum_tensor(f"ps{i}", [P, 512], F32)) for i in range(8)]
        ps, po = Ring(6), Ring(2)

        class Bank:
            def __init__(self, ring=ps):
                self.ring = ring
                self.k, self.w = ring.take()
                self.ap = banks[self.k + (0 if ring is ps else 6)][:, :]

            def v(self, n, m, parts=P):
                return self.ap[0:parts, 0:n * m].rearrange("p (a b) -> p a b", a=n)

            def give(self, *toks):
                self.ring.give(self.k, *toks)

        lines = iter([line(f"d{i}") for i in range(40)])
        ldone = []

        def load(out_, in_, *toks, q=SP, ln=None):
            return q.dma(ln or next(lines), out_, in_, *toks)

        def wload(*pairs):
            k, w = wring.take()
            for view, src in pairs:
                t = SP.dma(wline[k], view(wslot[k]), src, *w)
            return k, t

        def wblock(src, n):
            k, t = wload((lambda s: s[:, 0:NJ * n].rearrange("p (j n) -> p j n", j=NJ),
                          src.rearrange("(j p) n -> p j n", p=P)))
            return k, t, wslot[k][:, 0:NJ * n].rearrange("p (j n) -> p j n", j=NJ)

        def dbg(name, ap, *toks):
            if tap is not None:
                dst = tap(name, ap)
                t = load(dst, ap, *toks, ln=line("t_" + name))
                ldone.append(t)
                for q in QS:
                    q.wait(t)

        def barrier():
            toks = [q.t for q in QS]
            for q in QS:
                q.wait(*[t for t in toks if t[0] is not q.sem])
                q.wait(q.t)
            return toks

        def pow_nhalf(ap, n, *toks):
            return G.do(lambda e: e.tensor_tensor(ap, ap, nhalf[:, 0:n], POW), *toks)

        def tt(q, out_, a, b, op, *toks):
            return q.do(lambda e: e.tensor_tensor(out_, a, b, op), *toks)

        def ts(q, out_, a, s1, s2, op0, op1, *toks):
            if op1 is None:
                return q.do(lambda e: e.tensor_scalar(out_, a, s1, None, op0), *toks)
            return q.do(lambda e: e.tensor_scalar(out_, a, s1, s2, op0, op1), *toks)

        def stt(out_, a, s, b, op0, op1, *toks):
            return V.do(lambda e: e.scalar_tensor_tensor(out=out_, in0=a, scalar=s, in1=b, op0=op0, op1=op1), *toks)

        def red(out_, a, op, *toks, negate=None):
            return V.do(lambda e: e.tensor_reduce(out_, a, AXX, op, negate=negate), *toks)

        def act(out_, a, f, *toks, **kw):
            return S.do(lambda e: e.activation(out_, a, f, **kw), *toks)

        def cp(q, out_, a, *toks):
            if q is S:
                return act(out_, a, ACT.Copy, *toks)
            return q.do(lambda e: e.tensor_copy(out_, a), *toks)

        def mm(out_, l, r, start, stop, *toks, inc=False):
            return PE.do(lambda e: e.matmul(out_, l, r, start=start, stop=stop), *toks, inc=inc)

        def tr(out_, in_, *toks, inc=False):
            n = in_.shape[0]
            return PE.do(lambda e: e.transpose(out_, in_, ident[0:n, 0:n]), *toks, inc=inc)

        t_cst = load(cst, A["cst"])
        ct = phase.get(32)
        gcols = phase.get(24 + 8 + 48 + 8 + 8)
        b1c, gp1, b2c, gp2, gp3 = (gcols[:, 0:24], gcols[:, 24:32], gcols[:, 32:80], gcols[:, 80:88], gcols[:, 88:96])
        ln0 = next(lines)
        for dst, src in ((ct[:, 0:8], A["c"]), (ct[:, 8:16], A["c_2"]), (b1c, A["b_ada_c"]), (gp1, A["g_pre"]),
                         (b2c, A["b_ada_2_c"]), (gp2, A["norm_mix_2"]), (gp3, A["norm_ffn_2"])):
            t_cols = load(dst, src, ln=ln0)
        posi = phase.get(16)
        pos = phase.get(16)
        t_pos = load(posi[:, 0:9].bitcast(I32), A["pos"])
        G1 = phase.get(D)
        ln1 = next(lines)
        load(G1, A["b_ada_r"][2 * D:3 * D].partition_broadcast(P), ln=ln1)
        load(gt1_2, A["b_ada_2_r"][2 * D:3 * D].partition_broadcast(P), ln=ln1)
        load(gt2_2, A["b_ada_2_r"][5 * D:6 * D].partition_broadcast(P), ln=ln1)
        t_rows = (ln1[0], ln1[1])

        cp(V, identb, ident, t_cst)
        t_mb = cp(V, cmaskb, C["caus"])
        act(ct[:, 16:32], ct[:, 0:16], ACT.Tanh, t_cols, scale=0.5)
        stt(ccol, ct[:, 16:32], 1.0, ct[:, 0:16], ADD, MUL, S.t)
        t_cc = ts(V, ccol, ccol, 0.5, None, MUL, None, V.t)

        def trig_tables():
            ang = phase_tmp.get(9, 32)
            kk = phase_tmp.get(9, 32)
            r = phase_tmp.get(9, 32)
            nsat = phase_tmp.get(5, 16)
            cp(V, pos[:, 0:9], posi[:, 0:9].bitcast(I32), t_pos)
            inv = C["inv"]
            tt(V, ang[:, 0:4, :], bx(pos[:, 0:4], 2, (P, 4, 32)), bx(inv[:, 0:32], 1, (P, 4, 32)), MUL, V.t)
            tt(V, ang[:, 4, 0:8], pos[:, 4:5].to_broadcast([P, 8]), inv[:, 32:40], MUL)
            tt(V, ang[:, 4, 8:16], pos[:, 4:5].to_broadcast([P, 8]), inv[:, 32:40], MUL)
            tt(V, ang[:, 4, 16:32], pos[:, 4:5].to_broadcast([P, 16]), inv[:, 40:56], MUL)
            tt(V, ang[:, 5:9, 0:16], bx(pos[:, 5:9], 2, (P, 4, 16)), bx(inv[:, 40:56], 1, (P, 4, 16)), MUL)
            tt(V, ang[:, 5:9, 16:24], bx(pos[:, 0:4], 2, (P, 4, 8)), bx(inv[:, 32:40], 1, (P, 4, 8)), MUL)
            tt(V, ang[:, 5:9, 24:32], bx(pos[:, 0:4], 2, (P, 4, 8)), bx(inv[:, 32:40], 1, (P, 4, 8)), MUL)
            pi2 = 2 * np.pi
            m1 = 6.28125
            m2 = float(np.float32(np.round((pi2 - m1) * 2 ** 21) / 2 ** 21))
            m3 = float(np.float32(pi2 - m1 - m2))
            big = 12582912.0
            for w, shift in ((0, 0.25), (1, 0.0)):
                ts(V, kk, ang, float(np.float32(1 / pi2)), shift, MUL, ADD, V.t)
                ts(V, kk, kk, big, None, ADD, None, V.t)
                ts(V, kk, kk, big, None, SUB, None, V.t)
                stt(r, kk, -m1, ang, MUL, ADD, V.t)
                stt(r, kk, -m2, r, MUL, ADD, V.t)
                stt(r, kk, -m3, r, MUL, ADD, V.t)
                if shift:
                    ts(V, r, r, float(np.pi / 2), None, ADD, None, V.t)
                ts(V, r, r, float(np.float32(3.1415925)), -float(np.float32(3.1415925)), MIN, MAX, V.t)
                act(trig[:, :, w, :], r, ACT.Sin, V.t)
                V.wait(S.t)
            return S.t

        phase_tmp = phase.rest()
        xt = phase_tmp.get(NT, D)
        t_x = load(xt, A["x"].rearrange("(t p) d -> p t d", p=P))
        t_trig = trig_tables()
        cosr = lambda k: trig[:, k, 0, :]
        sinr = lambda k: trig[:, k, 1, :]

        side = []
        side_every = [1, 0]

        def fill():
            side_every[1] += 1
            if side and side_every[1] % side_every[0] == 0:
                side.pop(0)()

        def drain_side():
            while side:
                side.pop(0)()

        def mod_cols(src, which, base, cc, halves=(0, 1)):
            for half in halves:
                k, t, w = wblock(src[:, which * D + half * 512:which * D + half * 512 + 512], 512)
                b = Bank()
                PE.wait(t, t_cc, *b.w)
                for n in range(4):
                    for j in range(NJ):
                        mm(b.ap[:, n:n + 1], w[:, j, n * P:(n + 1) * P], ccol[:, cc * 8 + j:cc * 8 + j + 1],
                           j == 0, j == NJ - 1, inc=(n == 3 and j == NJ - 1))
                wring.give(k, PE.t)
                cp(V, colm[:, base + 4 * half:base + 4 * half + 4], b.ap[:, 0:4], PE.t)
                b.give(V.t)
            return V.t

        def mod_row(src, which, dst, cc, mulrow=None, halves=(0, 1)):
            for half in halves:
                k, t, w = wblock(src[:, which * D + half * 512:which * D + half * 512 + 512], 512)
                b = Bank()
                PE.wait(t, t_scb, *b.w)
                for j in range(NJ):
                    mm(b.ap, scb[:, cc, j, :], w[:, j, :], j == 0, j == NJ - 1, inc=(j == NJ - 1))
                wring.give(k, PE.t)
                d_ = dst[:, half * 512:half * 512 + 512]
                tt(V, d_, b.ap, d_, ADD, PE.t, t_rows)
                b.give(V.t)
                if mulrow is not None:
                    tt(V, d_, d_, mulrow[:, half * 512:half * 512 + 512], MUL, V.t)
            return V.t

        def finish_cols(base, bcol, bat, gp):
            sh, sc = colm[:, base:base + 8], colm[:, base + 8:base + 16]
            tt(V, sh, sh, bcol[:, bat:bat + 8], ADD, V.t, t_cols)
            tt(V, sc, sc, bcol[:, bat + 8:bat + 16], ADD, V.t)
            return stt(sc, sc, 1.0, gp, ADD, MUL, V.t)

        mod_cols(A["w_ada"], 0, 0, 0)
        mod_cols(A["w_ada"], 1, 8, 0)
        t_col1 = finish_cols(0, b1c, 0, gp1)

        def make_hT(xt, ready, base, tcol, spare, after=()):
            xh, ss = spare
            S.wait(*ready, *after)
            V.wait(*after)
            for t_ in range(NT):
                act(xh[:, t_, :], xt[:, t_, :], ACT.Square, accum_out=ss[:, t_:t_ + 1])
            ts(V, ss[:, 4:8], ss[:, 0:4], 1.0 / D, 1e-6, MUL, ADD, S.t)
            tp = pow_nhalf(ss[:, 4:8], 4, V.t)
            xd = []
            for t_ in range(NT):
                if t_ % 2:
                    xd.append(ts(V, xh[:, t_, :], xt[:, t_, :], ss[:, 4 + t_:5 + t_], None, MUL, None, tp, S.t, *ready))
                else:
                    xd.append(act(xh[:, t_, :], xt[:, t_, :], ACT.Copy, tp, S.t, scale=ss[:, 4 + t_:5 + t_]))
            for j in range(NJ):
                b = Bank()
                PE.wait(*b.w, *xd)
                for t_ in range(NT):
                    tr(b.ap[:, t_ * P:(t_ + 1) * P], xh[:, t_, j * P:(j + 1) * P], inc=(t_ == NT - 1))
                sc, sh = colm[:, base + 8 + j:base + 9 + j], colm[:, base + j:base + j + 1]
                if j % 2:
                    act(hT[:, j, :], b.ap, ACT.Identity, PE.t, tcol, scale=sc, bias=sh)
                    b.give(S.t)
                else:
                    ts(V, hT[:, j, :], b.ap, sc, sh, MUL, ADD, PE.t, tcol)
                    b.give(V.t)
            return (S.t, V.t)

        xh1 = phase_tmp.get(NT, D)
        ss1 = phase_tmp.get(16)
        hready = make_hT(xt, (t_x,), 0, t_col1, (xh1, ss1))
        t_hT_free = None
        dbg("hT", hT, *hready)
        bt = barrier()

        ph = Space(phase.ap, phase.at, phase.end - phase.at)
        c1 = ph.get(sum(C1.values()))
        t_c1 = load(c1, A["c1"], *bt, q=G)
        K1 = {}
        o = 0
        for k, n in C1.items():
            K1[k] = c1[:, o:o + n]
            o += n
        pe_t = ph.get(2, 16)
        w2s = ph.get(2, 2, 64)
        ln2 = next(lines)
        load(pe_t[:, 0, :], A["cmp_pe_k"], *bt, q=G, ln=ln2)
        load(pe_t[:, 1, :], A["cmp_pe_v"], q=G, ln=ln2)
        load(w2s[:, 0], A["cmp_w2_k"].rearrange("(j p) n -> p j n", p=P), q=G, ln=ln2)
        t_cw = load(w2s[:, 1], A["cmp_w2_v"].rearrange("(j p) n -> p j n", p=P), q=G, ln=ln2)

        mix = ph.get(NT, D)
        nqT = ph.get(4, 512)
        gl = ph.get(NT, 24)
        vs = ph.get(2, NT, 128)
        KT = ph.get(2, 2, 512)
        kc2 = [ph.get(2, 529), ph.get(2, 529)]
        tmp = ph.get(3, 512)
        retsp = ph.rest()
        rqT = ph.get(4, 512)
        rkT = ph.get(4, 512)
        rk = ph.get(NT, 512)
        rv = ph.get(NT, 512)
        t_kz = G.do(lambda e: e.memset(kc2[0], 0.0))
        t_kz = G.do(lambda e: e.memset(kc2[1], 0.0))

        def proj(w, n, t_, b, c0=0):
            for j in range(NJ):
                mm(b.ap[:, 0:n], hT[:, j, t_ * P:(t_ + 1) * P], w[:, j, c0:c0 + n], j == 0, j == NJ - 1,
                   inc=(j == NJ - 1))
            return PE.t

        tring = Ring(3)

        def turn(src_tok, src, dst_of, evac, *w):
            b = Bank()
            PE.wait(src_tok, *b.w)
            for p in range(4):
                tr(b.ap[:, p * P:(p + 1) * P], src[:, p * P:(p + 1) * P], inc=(p == 3))
            cp(evac, dst_of, b.v(4, P), PE.t, *w)
            b.give(evac.t)
            return PE.t, evac.t

        def rope_full(b, dst, t_, tk, w):
            k2, w2 = tring.take()
            u = tmp[:, k2, :].rearrange("p (h d) -> p h d", h=H)
            s = b.v(H, 64)
            c_ = bx(cosr(t_), 1, (P, H, 32))
            s_ = bx(sinr(t_), 1, (P, H, 32))
            V.wait(tk, t_trig, *w, *w2)
            tt(V, dst[:, :, 0:32], s[:, :, 0:32], c_, MUL)
            tt(V, dst[:, :, 32:64], s[:, :, 32:64], c_, MUL)
            tt(V, u[:, :, 0:32], s[:, :, 32:64], s_, MUL)
            r = tt(V, u[:, :, 32:64], s[:, :, 0:32], s_, MUL)
            tt(G, dst[:, :, 0:32], dst[:, :, 0:32], u[:, :, 0:32], SUB, r)
            r2 = tt(G, dst[:, :, 32:64], dst[:, :, 32:64], u[:, :, 32:64], ADD)
            tring.give(k2, r2)
            return r, r2

        def rope_part(x, n, half, cosa, sina, tk, parts=P):
            k2, w2 = tring.take()
            u = tmp[0:parts, k2, 0:n * 4 * half].rearrange("p (a n h) -> p a n h", a=4, n=n)
            c_ = bx(cosa, 1, (parts, n, half))
            s_ = bx(sina, 1, (parts, n, half))
            x1, x2 = x[:, :, 0:half], x[:, :, half:2 * half]
            G.wait(tk, t_trig, *w2)
            tt(G, u[:, 0], x1, c_, MUL)
            tt(G, u[:, 1], x2, s_, MUL)
            tt(G, u[:, 2], x1, s_, MUL)
            a = tt(G, u[:, 3], x2, c_, MUL)
            tt(G, x1, u[:, 0], u[:, 1], SUB, a)
            r = tt(G, x2, u[:, 2], u[:, 3], ADD)
            tring.give(k2, r)
            return r

        rot = ph.get(2, 512)
        rring = Ring(2)

        def after_proj_rot(which):
            k, t, w = wblock(A["w_in"][:, which * 512:which * 512 + 512], 512)
            PE.wait(t, *hready, t_cst)
            pend = []
            tk_ = []
            for t_ in range(NT):
                b = Bank()
                PE.wait(*b.w)
                tk = proj(w, 512, t_, b)
                if t_ == NT - 1:
                    wring.give(k, tk)
                if which == 0:
                    k3, w3 = rring.take()
                    dst = rot[:, k3, :].rearrange("p (h d) -> p h d", h=H)
                    r, r2 = rope_full(b, dst, t_, tk, w3)
                    b.give(r)
                    pend.append((k3, rot[:, k3, :], r2, t_))
                else:
                    dst = rk[:, t_, :].rearrange("p (h d) -> p h d", h=H)
                    r, r2 = rope_full(b, dst, t_, tk, [])
                    b.give(r)
                    pend.append((None, rk[:, t_, :], r2, t_))
                while len(pend) > 1 or (pend and t_ == NT - 1):
                    k3, src, r2, tx = pend.pop(0)
                    a, b_ = turn(r2, src, (rqT if which == 0 else rkT)[:, :, tx * P:(tx + 1) * P], S)
                    if k3 is not None:
                        rring.give(k3, a)
                    tk_.append(b_)
            return tk_

        t_rq = after_proj_rot(0)
        t_rk = after_proj_rot(1)
        k, t, w = wblock(A["w_in"][:, 1024:1536], 512)
        PE.wait(t)
        t_rv = []
        for t_ in range(NT):
            b = Bank()
            PE.wait(*b.w)
            tk = proj(w, 512, t_, b)
            t_rv.append(cp(S, rv[:, t_, :], b.ap, tk))
            b.give(S.t)
        wring.give(k, tk)

        def silu2(w, off, tk_list):
            for t_ in range(NT):
                b = Bank()
                PE.wait(*b.w)
                tk = proj(w, 512, t_, b)
                k2, w2 = tring.take()
                act(tmp[:, k2, :], b.ap, ACT.Tanh, tk, *w2, scale=0.5)
                r = stt(mix[:, t_, off:off + 512], tmp[:, k2, :], 1.0, b.ap, ADD, MUL, S.t)
                b.give(r)
                tring.give(k2, r)
                tk_list.append(r)
            return tk

        k, t, w = wblock(A["w_in"][:, 1536:2048], 512)
        PE.wait(t)
        t_sg1 = []
        wring.give(k, silu2(w, 0, t_sg1))

        PTr = ph.get(2, 512)
        ptr_ring = Ring(2)
        R = ph.get(4, P)
        kz = ph.get(512)
        oo = ph.get(512)
        o2 = ph.get(512)
        st = ph.get(64)
        h3 = lambda ap: ap.rearrange("p (h d) -> p h d", h=H)

        def retention(t_, last):
            sl = slice(t_ * P, (t_ + 1) * P)
            pts = []
            for e in range(2):
                b = Bank()
                PE.wait(*b.w, t_rq[t_], t_rk[t_])
                rows = slice(64 * e, 64 * e + 64)
                for p in range(4):
                    mm(b.ap[:, p * P:(p + 1) * P], rkT[rows, p, sl], rqT[rows, p, sl], True, True, inc=(p == 3))
                k2, w2 = ptr_ring.take()
                dst = PTr[:, k2, :].rearrange("p (h i) -> p h i", h=4)
                dec = K1["dec"].rearrange("p (a e i) -> p e a i", a=4, e=2)[:, e]
                tt(V, dst, b.v(4, P), dec, MUL, PE.t, t_c1, *w2)
                b.give(V.t)
                pts.append((k2, dst, V.t))
            bi = Bank()
            PE.wait(*bi.w, t_rv[t_], *[x[2] for x in pts])
            for h in range(H):
                mm(bi.ap[:, h * 64:h * 64 + 64], pts[h % 2][1][:, h // 2, :], rv[:, t_, h * 64:h * 64 + 64],
                   True, True, inc=(h == 7))
            t_in = PE.t
            for x in pts:
                ptr_ring.give(x[0], PE.t)
            if t_ > 0:
                bc = Bank()
                PE.wait(*bc.w, last["R"])
                for p in range(4):
                    mm(bc.ap[:, p * P:(p + 1) * P], rqT[:, p, sl], R[:, p, :], True, True, inc=(p == 3))
                last["Rread"] = PE.t
                tt(V, h3(o2), bc.v(H, 64), bx(K1["xi"], 2, (P, H, 64)), MUL, PE.t, *last["o2"])
                bc.give(V.t)
                tt(V, h3(oo), bi.v(H, 64), h3(o2), ADD, V.t, t_in, *last["oo"])
            else:
                cp(V, oo, bi.ap, t_in, *last["oo"])
            bi.give(V.t)
            t_oo = V.t
            if t_ < NT - 1:
                tt(G, h3(kz), h3(rk[:, t_, :]), bx(K1["zeta"], 2, (P, H, 64)), MUL, t_rk[t_], t_c1, *last["kz"])
                bk = Bank()
                PE.wait(*bk.w, G.t)
                for p in range(4):
                    mm(bk.ap[:, p * P:(p + 1) * P], kz[:, p * P:(p + 1) * P], rv[:, t_, p * P:(p + 1) * P],
                       True, True, inc=(p == 3))
                last["kz"] = [PE.t]
                bdb = bx(C["bd"], 1, (P, 4, P))
                if t_ == 0:
                    tt(V, R, bk.v(4, P), bdb, MUL, PE.t)
                else:
                    a = tt(G, R, R, K1["cd"].rearrange("p (a b) -> p a b", a=4), MUL, last["Rread"], last["R"])
                    tt(V, o2.rearrange("p (a b) -> p a b", a=4), bk.v(4, P), bdb, MUL, PE.t, t_oo)
                    tt(V, R, R, o2.rearrange("p (a b) -> p a b", a=4), ADD, V.t, a)
                bk.give(V.t)
                last["R"] = V.t
                last["o2"] = [V.t]
            red(st[:, 0:8], h3(oo), ADD, t_oo, *last["st"])
            ts(V, st[:, 0:8], st[:, 0:8], -1.0 / 64, None, MUL, None, V.t)
            a = tt(V, h3(oo), h3(oo), bx(st[:, 0:8], 2, (P, H, 64)), ADD, V.t)
            tt(G, kq, oo, oo, MUL, a, *last["kq"])
            red(st[:, 8:16], h3(kq), ADD, G.t)
            last["kq"] = [V.t]
            ts(V, st[:, 8:16], st[:, 8:16], 4.0 / 64, 4e-5, MUL, ADD, V.t)
            b_ = pow_nhalf(st[:, 8:16], 8, V.t)
            m = mix[:, t_, 0:512]
            tt(G, h3(m), h3(m), bx(st[:, 8:16], 2, (P, H, 64)), MUL, b_, t_sg1[t_])
            tt(V, m, m, oo, MUL, G.t)
            last["oo"] = [V.t]
            last["st"] = [G.t]
            return V.t

        kq = ph.get(512)
        last = {"o2": [], "oo": [], "kz": [], "R": None, "Rread": None, "st": [], "kq": []}

        k, t, w = wblock(A["w_in"][:, 2048:2560], 512)
        PE.wait(t)
        t_nq = []
        t_mix1 = []
        for t_ in range(NT):
            b = Bank()
            PE.wait(*b.w)
            tk = proj(w, 512, t_, b)
            k3, w3 = rring.take()
            a = act(rot[:, k3, :], b.ap, ACT.Copy, tk, *w3, scale=0.125)
            b.give(a)
            r2 = rope_part(rot[:, k3, :].rearrange("p (h d) -> p h d", h=H), H, 8,
                           trig[:, 5 + t_, 0, 16:24], trig[:, 5 + t_, 1, 16:24], a)
            if t_ == NT - 1:
                wring.give(k, tk)
            t_mix1.append(retention(t_, last))
            pt_, e_ = turn(r2, rot[:, k3, :], nqT[:, :, t_ * P:(t_ + 1) * P], S)
            rring.give(k3, pt_)
            t_nq.append(e_)

        if stop == "ret":
            for t_ in range(NT):
                dbg(f"ret{t_}", mix[:, t_, 0:512], *t_mix1)

        ka, ta, wa = wblock(A["w_in"][:, 2560:3072], 512)
        kb, tb, wb = wblock(A["w_in"][:, 3072:3352], 280)
        PE.wait(ta, tb)
        kvd = ph.get(1, 4, 4, 64)
        kvr = Ring(1)
        t_kt = []
        for t_ in range(NT):
            b = Bank()
            b2 = Bank()
            PE.wait(*b.w, *b2.w)
            proj(wa, 512, t_, b)
            tk1 = PE.t
            tk = proj(wb, 280, t_, b2)
            k3, w3 = kvr.take()
            kv = kvd[:, k3]
            S.wait(tk1, *w3)
            for kind, src in ((0, b.ap[:, 0:128]), (1, b.ap[:, 128:256]), (2, b.ap[:, 256:384])):
                cp(S, kv[:, kind].rearrange("p (g u) d -> p g u d", g=2),
                   bx(src.rearrange("p (g d) -> p g d", g=2), 2, (P, 2, 2, 64)))
            cp(S, vs[:, 0, t_, :], b.ap[:, 384:512])
            b.give(S.t)
            S.wait(tk)
            cp(S, kv[:, 3].rearrange("p (g u) d -> p g u d", g=2),
               bx(b2.ap[:, 0:128].rearrange("p (g d) -> p g d", g=2), 2, (P, 2, 2, 64)))
            cp(S, vs[:, 1, t_, :], b2.ap[:, 128:256])
            act(gl[:, t_, :], b2.ap[:, 256:280], ACT.Tanh, scale=0.5)
            b2.give(S.t)
            ca, sa = trig[:, 5 + t_, 0, 16:24], trig[:, 5 + t_, 1, 16:24]
            rope_part(kv[:, 2], 4, 8, ca, sa, S.t)
            r = rope_part(kv[:, 3], 4, 8, ca, sa, S.t)
            if t_ == NT - 1:
                wring.give(ka, tk)
                wring.give(kb, tk)
            for kinds in ((0, 1), (2, 3)):
                bb = Bank()
                PE.wait(*bb.w, r)
                for x, kind in enumerate(kinds):
                    for g in range(2):
                        tr(bb.ap[:, (x * 2 + g) * P:(x * 2 + g + 1) * P],
                           kv[:, kind, 2 * g:2 * g + 2, :].rearrange("p u d -> p (u d)"), inc=(x == 1 and g == 1))
                s4 = bb.ap.rearrange("p (x g t) -> p x g t", x=2, g=2)
                if kinds[0] == 0:
                    V.wait(t_kz)
                    for x in range(2):
                        cp(V, kc2[x][0:64, :, 1 + t_ * P:1 + (t_ + 1) * P], s4[0:64, x], PE.t)
                        cp(V, kc2[x][64:128, :, t_ * P:(t_ + 1) * P], s4[64:128, x])
                    bb.give(V.t)
                else:
                    cp(S, KT[:, :, :, t_ * P:(t_ + 1) * P], s4, PE.t)
                    bb.give(S.t)
            kvr.give(k3, PE.t)
            t_kt.append((V.t, S.t))
        t_gl = ts(G, gl, gl, 1.0, None, ADD, None, S.t)
        k, t, w = wblock(A["w_in"][:, 3352:3864], 512)
        PE.wait(t)
        t_sg2 = []
        wring.give(k, silu2(w, 512, t_sg2))
        t_h1 = PE.t

        bt = barrier()
        a1 = retsp
        fl = a1.get(2048)
        flat = [fl[:, x * 1024:x * 1024 + 1024].rearrange("p (m g n) -> p m g n", m=16, g=2) for x in range(2)]
        hid = a1.get(2, 256)
        hidT = a1.get(2, 2, 64)
        hv4 = a1.get(2, 2, 4, 32)
        kcs = a1.get(2, 64)
        kcT = a1.get(64)
        vcbd = a1.get(2, 4, 64)
        ht = a1.get(256)
        ring3 = [(a1.get(512), a1.get(512)) for _ in range(3)]
        sc8 = a1.get(8, 32)
        pt8 = a1.get(2, P)
        sm = a1.get(2, 64)
        att = a1.get(NT, 512)
        au = a1.get(2, 512)
        for x in range(2):
            for g in range(2):
                for aa in range(2):
                    src = kc2[x][:, g, 1 + 16 * aa:1 + 16 * aa + 512].rearrange(
                        "p (n b two) -> p b n two", n=32, b=8, two=2)[:, :, :, 0]
                    tt(V, flat[x][:, 8 * aa:8 * aa + 8, g, :], src,
                       bx(pe_t[:, x, 8 * aa:8 * aa + 8], 2, (P, 8, 32)), ADD, t_cw)
        t_flat = V.t
        for x, nm in enumerate(("cmp_w1_k", "cmp_w1_v")):
            k, t = wload((lambda s: s.rearrange("p (m n) -> p m n", m=16),
                          A[nm].rearrange("(m p) n -> p m n", p=P)))
            w = wslot[k].rearrange("p (m n) -> p m n", m=16)
            b = Bank()
            PE.wait(t, t_flat, *b.w)
            for m in range(16):
                mm(b.ap[0:64, 0:256], flat[x][:, m].rearrange("p g n -> p (g n)"), w[:, m, :], m == 0, m == 15,
                   inc=(m == 15))
            wring.give(k, PE.t)
            act(ht[0:64, :], b.ap[0:64, 0:256], ACT.Tanh, PE.t, V.t, scale=0.5)
            r = stt(hid[0:64, x, :], ht[0:64, :], 1.0, b.ap[0:64, 0:256], ADD, MUL, S.t)
            b.give(r)
            b = Bank()
            PE.wait(r, *b.w)
            for j in range(2):
                tr(b.ap[:, j * 64:j * 64 + 64], hid[0:64, x, j * P:(j + 1) * P], inc=(j == 1))
            if x == 0:
                cp(V, hidT[:, 0], b.v(2, 64), PE.t)
            else:
                for j in range(2):
                    for g in range(2):
                        s_ = b.ap[:, j * 64 + g * 32:j * 64 + g * 32 + 32]
                        cp(V, hv4[:, j, g], bx(s_, 1, (P, 4, 32)), PE.t)
            b.give(V.t)
            b = Bank()
            PE.wait(V.t, *b.w)
            if x == 0:
                for j in range(2):
                    mm(b.ap[0:64, 0:64], hidT[:, 0, j], w2s[:, 0, j], j == 0, j == 1, inc=(j == 1))
                act(kcs[0:64], bx(b.ap[0:64, 0:64], 1, (64, 2, 64)), ACT.Copy, PE.t, scale=0.5)
                b.give(S.t)
                r = rope_part(kcs[0:64], 2, 8, trig[0:64, 4, 0, 0:8], trig[0:64, 4, 1, 0:8], S.t, 64)
                b = Bank()
                PE.wait(r, *b.w)
                tr(b.ap[:, 0:64], kcs[0:64].rearrange("p u d -> p (u d)"), inc=True)
                t_kct = cp(V, kcT, b.ap[:, 0:64], PE.t)
                b.give(V.t)
            else:
                for g in range(2):
                    for j in range(2):
                        mm(b.ap[:, g * 64:g * 64 + 64], hv4[:, j, g].rearrange("p a n -> p (a n)"), w2s[:, 1, j],
                           j == 0, j == 1, inc=(j == 1 and g == 1))
                for g in range(2):
                    t_vc = tt(V, vcbd[:, g], bx(b.ap[:, g * 64:g * 64 + 64], 1, (P, 4, 64)),
                              bx(K1["hsel"], 2, (P, 4, 64)), MUL, PE.t)
                b.give(V.t)

        def attention(t_, heads, qf, kf, vf, ob, sums, nmx, scale, ring, bufs, ready, vready):
            n = (t_ + 1) * P
            stg = [None] * len(heads)

            def scores(i):
                h = heads[i]
                b = Bank()
                PE.wait(*b.w, *ready)
                mm(b.ap[:, 0:n], qf(h), kf(h, n), True, False)
                mm(b.ap[:, t_ * P:n], identb, cmaskb, False, True, inc=True)
                kx, wx = ring.take()
                Pb, Tb = bufs[kx]
                red(nmx[:, i:i + 1], b.ap[:, 0:n], MAX, PE.t, negate=True)
                if scale != 1.0:
                    ts(V, nmx[:, i:i + 1], nmx[:, i:i + 1], scale, None, MUL, None, V.t)
                act(Pb[:, 0:n], b.ap[:, 0:n], ACT.Exp, V.t, *wx, bias=nmx[:, i:i + 1], scale=scale,
                    accum_out=sums[:, i:i + 1])
                b.give(S.t)
                stg[i] = [kx, Pb, Tb, S.t]

            def turns(i):
                kx, Pb, Tb, te = stg[i]
                b = Bank()
                PE.wait(*b.w, te)
                for kb in range(t_ + 1):
                    tr(b.ap[:, kb * P:(kb + 1) * P], Pb[:, kb * P:(kb + 1) * P], inc=(kb == t_))
                q = V if i % 2 else S
                cp(q, Tb[:, 0:n], b.ap[:, 0:n], PE.t)
                b.give(q.t)
                stg[i].append(q.t)

            def pv(i):
                kx, Pb, Tb, te, tc = stg[i]
                PE.wait(tc, *vready)
                for kb in range(t_ + 1):
                    mm(ob.ap[:, heads[i] * 64:heads[i] * 64 + 64], Tb[:, kb * P:(kb + 1) * P], vf(heads[i], kb),
                       kb == 0, kb == t_, inc=(kb == t_))
                ring.give(kx, PE.t)

            for i in range(len(heads) + 2):
                fill()
                if i < len(heads):
                    scores(i)
                if 1 <= i <= len(heads):
                    turns(i - 1)
                if i >= 2:
                    pv(i - 2)
            return PE.t

        G1b = a1.get(D)
        scb = fl.rearrange("p (a j n) -> p a j n", a=2, j=NJ)
        xt = a1.get(NT, D)
        t_rows = load(G1b, A["g_post"].partition_broadcast(P), *bt, q=G)
        t_x = load(xt, A["x"].rearrange("(t p) d -> p t d", p=P), q=G)
        t_scb = cp(V, scb, bx(ccol.rearrange("p (a j) -> p a j", a=2), 3, (P, 2, NJ, P)), V.t)
        for half in ((0,), (1,)):
            side.append(lambda half=half: mod_row(A["w_ada"], 2, G1, 0, G1b, half))
        for which, base in ((0, 16), (1, 24), (3, 32), (4, 40)):
            for half in ((0,), (1,)):
                side.append(lambda which=which, base=base, half=half: mod_cols(A["w_ada_2"], which, base, 1, half))
        for which, dst in ((2, gt1_2), (5, gt2_2)):
            for half in ((0,), (1,)):
                side.append(lambda which=which, dst=dst, half=half: mod_row(A["w_ada_2"], which, dst, 1, None, half))
        side_every[0] = 5
        aring = Ring(3)
        smr = Ring(2)
        aur = Ring(2)
        t_att = []
        sc_free = []
        for t_ in range(NT):
            sl = slice(t_ * P, (t_ + 1) * P)
            kS, wS = smr.take()
            sv = sm[:, kS, :]
            for e in range(2):
                b = Bank()
                PE.wait(*b.w, t_nq[t_], t_kct)
                rows = slice(64 * e, 64 * e + 64)
                for p in range(4):
                    g = (2 * p + e) // 4
                    mm(b.ap[:, p * 32:p * 32 + 32], nqT[rows, p, sl], kcT[rows, g * 32:g * 32 + 32], True, True,
                       inc=(p == 3))
                tt(V, sc8.rearrange("p (a e) n -> p e a n", e=2)[:, e], b.v(4, 32),
                   bx(K1["cneg"][:, t_ * 32:t_ * 32 + 32], 1, (P, 4, 32)), ADD, PE.t, *sc_free)
                b.give(V.t)
            red(sv[:, 0:8], sc8, MAX, V.t, *wS)
            tt(V, sc8, sc8, bx(sv[:, 0:8], 2, (P, 8, 32)), SUB, V.t)
            act(sc8, sc8, ACT.Exp, V.t)
            red(sv[:, 8:16], sc8, ADD, S.t)
            tt(V, sc8, sc8, bx(K1["cmul"][:, t_ * 32:t_ * 32 + 32], 1, (P, 8, 32)), MUL, V.t)
            b = Bank()
            PE.wait(*b.w, V.t)
            for g in range(2):
                tr(b.ap[:, g * P:(g + 1) * P], sc8[:, 4 * g:4 * g + 4, :].rearrange("p h n -> p (h n)"), inc=(g == 1))
            sc_free = [PE.t]
            cp(V, pt8, b.v(2, P), PE.t)
            b.give(V.t)
            ob = Bank(po)
            PE.wait(V.t, t_vc, *ob.w)
            for g in range(2):
                mm(ob.ap[:, g * 256:g * 256 + 256], pt8[:, g], vcbd[:, g].rearrange("p a d -> p (a d)"), True, True,
                   inc=(g == 1))
            V.do(lambda e, sv=sv: e.reciprocal(sv[:, 8:16], sv[:, 8:16]))
            gv = gl[:, t_, :].rearrange("p (h c) -> p h c", c=3)
            stt(sv[:, 8:16], sv[:, 8:16], 0.25, gv[:, :, 0], MUL, MUL, V.t, t_gl)
            tt(V, h3(att[:, t_, :]), ob.v(H, 64), bx(sv[:, 8:16], 2, (P, H, 64)), MUL, V.t, PE.t)
            ob.give(V.t)
            tlast = V.t
            for kind in range(2):
                ob = Bank(po)
                PE.wait(*ob.w)
                o_ = 16 + 24 * kind
                attention(
                    t_, list(range(H)),
                    lambda h: nqT[64 * (h % 2):64 * (h % 2) + 64, h // 2, sl],
                    lambda h, n: KT[64 * (h % 2):64 * (h % 2) + 64, kind, h // 4, 0:n],
                    lambda h, kb: vs[:, kind, kb, (h // 4) * 64:(h // 4) * 64 + 64],
                    ob, sv[:, o_:o_ + 8], sv[:, o_ + 8:o_ + 16], 1.0, aring, ring3,
                    [t_nq[t_], *t_kt[t_]], [])
                V.do(lambda e, sv=sv, o_=o_: e.reciprocal(sv[:, o_ + 16:o_ + 24], sv[:, o_:o_ + 8]), S.t)
                stt(sv[:, o_ + 16:o_ + 24], sv[:, o_ + 16:o_ + 24], 0.25, gv[:, :, 1 + kind], MUL, MUL, V.t)
                ka_, wa_ = aur.take()
                tt(V, h3(au[:, ka_, :]), ob.v(H, 64), bx(sv[:, o_ + 16:o_ + 24], 2, (P, H, 64)), MUL, V.t, PE.t, *wa_)
                ob.give(V.t)
                tt(G, att[:, t_, :], att[:, t_, :], au[:, ka_, :], ADD, V.t, tlast)
                tlast = G.t
                aur.give(ka_, G.t)
            smr.give(kS, V.t)
            tt(G, mix[:, t_, 512:1024], mix[:, t_, 512:1024], att[:, t_, :], MUL, G.t, t_sg2[t_])
            t_att.append(G.t)
        if tap is not None:
            dbg("mix", mix, *t_att, *t_mix1)

        drain_side()
        t_G1 = V.t
        t_col2 = finish_cols(16, b2c, 0, gp2)
        t_col3 = finish_cols(32, b2c, 24, gp3)

        def transpose_into_hT(src, n, toks):
            for j in range(n):
                b = Bank()
                PE.wait(*b.w, *toks)
                for t_ in range(NT):
                    tr(b.ap[:, t_ * P:(t_ + 1) * P], src[:, t_, j * P:(j + 1) * P], inc=(t_ == NT - 1))
                q = V if j % 2 else S
                cp(q, hT[:, j, :], b.ap, PE.t, t_h1)
                b.give(q.t)
            return (S.t, V.t)

        mtok = transpose_into_hT(mix, NJ, (*t_att, *t_mix1))
        ws = [wblock(A["w_out"][:, n * 512:n * 512 + 512], 512) for n in range(2)]
        ysp = a1.get(NT, D) if False else att
        y2 = mix
        ss2 = sm
        for t_ in range(NT):
            for n in range(2):
                k, t, w = ws[n]
                b = Bank()
                PE.wait(*b.w, t, *mtok)
                proj(w, 512, t_, b)
                act(au[:, 0, :], b.ap, ACT.Square, PE.t, V.t, G.t, accum_out=ss2[:, 0, 8 + 2 * t_ + n:9 + 2 * t_ + n])
                tt(V, y2[:, t_, n * 512:n * 512 + 512], b.ap, G1[:, n * 512:n * 512 + 512], MUL, S.t, t_G1)
                b.give(V.t)
        for n in range(2):
            wring.give(ws[n][0], PE.t)
        t_h2 = PE.t
        red(ss2[:, 0, 0:4], ss2[:, 0, 8:16].rearrange("p (t n) -> p t n", n=2), ADD, S.t, V.t)
        ts(V, ss2[:, 0, 0:4], ss2[:, 0, 0:4], 1.0 / D, 1e-6, MUL, ADD, V.t)
        tp = pow_nhalf(ss2[:, 0, 0:4], 4, V.t)
        for t_ in range(NT):
            t_x1 = stt(xt[:, t_, :], y2[:, t_, :], ss2[:, 0, t_:t_ + 1], xt[:, t_, :], MUL, ADD, tp, V.t, t_x)
        dbg("x1", xt, t_x1)
        t_xsp = load(A["xs"].rearrange("(t p) d -> p t d", p=P), xt, t_x1, q=S)

        hready = make_hT(xt, (t_x1,), 16, t_col2, (mix, sm[:, 0, :]), (V.t, t_h2))
        dbg("h2T", hT, *hready)
        bt = barrier()
        for q in QS:
            q.wait(t_xsp)
        if stop in ("b1", "ret"):
            return finish(nc, ctx, (PE, V, S, G, SP), ldone)

        ph = root.rest()
        omla = ph.get(NT, 512)
        m2 = ph.rest()
        nrm = m2.get(2, 96)
        qan = m2.get(4)
        ln3 = next(lines)
        load(nrm[:, 0, :], A["q_norm_2"].partition_broadcast(P), *bt, t_xsp, q=G, ln=ln3)
        load(nrm[:, 1, :], A["k_norm_2"].partition_broadcast(P), q=G, ln=ln3)
        load(qan[:, 0:2], A["q_a_norm_2"], q=G, ln=ln3)
        t_nrm = load(qan[:, 2:3], A["kv_a_norm_2"], q=G, ln=ln3)
        mqT = m2.get(H, 512)
        mkT = m2.get(H, 512)
        mv = m2.get(NT, 512)
        lat = m2.get(NT, 416)
        lT = m2.get(3, 512)
        qk = m2.get(2, 2, H, 96)
        sq = m2.get(2, H, 96)
        mst = m2.get(NT, 64)
        ring3 = [(m2.get(512), m2.get(512)) for _ in range(3)]
        tmp = m2.get(3, 512)
        pst = m2.get(2, 512)
        tring = Ring(3)
        psr = Ring(2)
        k, t, w = wblock(A["w_in_2"][:, 0:416], 416)
        PE.wait(t, *hready)
        for t_ in range(NT):
            b = Bank()
            PE.wait(*b.w)
            proj(w, 416, t_, b)
            cp(S, lat[:, t_, :], b.ap[:, 0:416], PE.t)
            b.give(S.t)
        wring.give(k, PE.t)
        t_l = S.t
        for t_ in range(NT):
            act(sq.rearrange("p a h d -> p (a h d)")[:, 0:256], lat[:, t_, 0:256], ACT.Square, t_l, S.t,
                accum_out=mst[:, t_, 0:1])
            act(sq.rearrange("p a h d -> p (a h d)")[:, 256:384], lat[:, t_, 256:384], ACT.Square, S.t,
                accum_out=mst[:, t_, 1:2])
            act(sq.rearrange("p a h d -> p (a h d)")[:, 384:416], lat[:, t_, 384:416], ACT.Square, S.t,
                accum_out=mst[:, t_, 2:3])
        ts(V, mst[:, :, 0:1], mst[:, :, 0:1], 1.0 / 256, 1e-6, MUL, ADD, S.t)
        ts(V, mst[:, :, 1:2], mst[:, :, 1:2], 1.0 / 128, 1e-6, MUL, ADD)
        ts(V, mst[:, :, 2:3], mst[:, :, 2:3], 1.0 / 32, 1e-6, MUL, ADD)
        tp = G.do(lambda e: e.tensor_tensor(mst[:, :, 0:3], mst[:, :, 0:3],
                                            nhalf[:, 0:12].rearrange("p (a b) -> p a b", a=4), POW), V.t)
        for t_ in range(NT):
            ts(V, lat[:, t_, 0:256], lat[:, t_, 0:256], mst[:, t_, 0:1], None, MUL, None, tp)
            ts(V, lat[:, t_, 256:384], lat[:, t_, 256:384], mst[:, t_, 1:2], None, MUL, None)
            stt(lat[:, t_, 384:416], lat[:, t_, 384:416], mst[:, t_, 2:3], nrm[:, 1, 64:96], MUL, MUL, t_nrm)
        t_lv = V.t
        for t_ in range(NT):
            t_kr = rope_part(lat[:, t_, 384:416].unsqueeze(1), 1, 16, trig[:, 5 + t_, 0, 0:16],
                             trig[:, 5 + t_, 1, 0:16], t_lv)
        for j in range(3):
            b = Bank()
            PE.wait(*b.w, t_lv)
            for t_ in range(NT):
                tr(b.ap[:, t_ * P:(t_ + 1) * P], lat[:, t_, j * P:(j + 1) * P], inc=(t_ == NT - 1))
            ts(V, lT[:, j, :], b.ap, qan[:, j:j + 1], None, MUL, None, PE.t)
            b.give(V.t)
        t_lT = V.t
        k, t = wload((lambda s: s[:, 0:1536].rearrange("p (j n) -> p j n", j=2),
                      A["w_uq_2"].rearrange("(j p) n -> p j n", p=P)),
                     (lambda s: s[:, 1536:2560], A["w_ukv_2"]))
        wuq = wslot[k][:, 0:1536].rearrange("p (j n) -> p j n", j=2)
        wkv = wslot[k][:, 1536:2560]
        qkr = Ring(2)
        sqf = []
        t_mq = []
        for t_ in range(NT):
            sl = slice(t_ * P, (t_ + 1) * P)
            kx, wx = qkr.take()
            q_, k_ = qk[:, kx, 0], qk[:, kx, 1]
            S.wait(*wx)
            G.wait(*wx)
            V.wait(*wx)
            for n in range(2):
                b = Bank()
                PE.wait(*b.w, t_lT, t)
                for j in range(2):
                    mm(b.ap[:, 0:384], lT[:, j, sl], wuq[:, j, n * 384:(n + 1) * 384], j == 0, j == 1, inc=(j == 1))
                cp(S, q_[:, 4 * n:4 * n + 4, :], b.v(4, 96), PE.t)
                b.give(S.t)
                b = Bank()
                PE.wait(*b.w)
                mm(b.ap, lT[:, 2, sl], wkv[:, n * 512:(n + 1) * 512], True, True, inc=True)
                cp(V, k_[:, 4 * n:4 * n + 4, 0:64], b.v(4, P)[:, :, 0:64], PE.t)
                cp(V, mv[:, t_, n * 256:n * 256 + 256].rearrange("p (h d) -> p h d", h=4), b.v(4, P)[:, :, 64:128])
                b.give(V.t)
            ms = mst[:, t_, 8:32]
            tt(G, sq[:, 0], q_, q_, MUL, S.t, *sqf)
            tt(G, sq[:, 1, :, 0:64], k_[:, :, 0:64], k_[:, :, 0:64], MUL, V.t)
            red(ms[:, 0:8], sq[:, 0, :, 0:64], ADD, G.t)
            red(ms[:, 8:16], sq[:, 1, :, 0:64], ADD)
            red(ms[:, 16:24], sq[:, 0, :, 64:96], ADD)
            sqf = [V.t]
            ts(V, ms[:, 0:16], ms[:, 0:16], 1.0 / 64, 1e-6, MUL, ADD, V.t)
            ts(V, ms[:, 16:24], ms[:, 16:24], 1.0 / 32, 1e-6, MUL, ADD)
            pow_nhalf(ms, 24, V.t)
            tt(V, q_[:, :, 0:64], q_[:, :, 0:64], bx(ms[:, 0:8], 2, (P, H, 64)), MUL, G.t)
            tt(V, q_[:, :, 64:96], q_[:, :, 64:96], bx(ms[:, 16:24], 2, (P, H, 32)), MUL)
            tt(V, k_[:, :, 0:64], k_[:, :, 0:64], bx(ms[:, 8:16], 2, (P, H, 64)), MUL)
            tt(V, q_, q_, bx(nrm[:, 0, :], 1, (P, H, 96)), MUL, V.t, t_nrm)
            tq = V.t
            tt(V, k_[:, :, 0:64], k_[:, :, 0:64], bx(nrm[:, 1, 0:64], 1, (P, H, 64)), MUL)
            tk_ = V.t
            cp(G, k_[:, :, 64:96], bx(lat[:, t_, 384:416], 1, (P, H, 32)), t_kr)
            r = rope_part(q_[:, :, 64:96], H, 16, trig[:, 5 + t_, 0, 0:16], trig[:, 5 + t_, 1, 0:16], tq)
            for which, src, dst in ((0, q_, mqT), (1, k_, mkT)):
                for n in range(2):
                    b = Bank()
                    PE.wait(*b.w, r, tk_)
                    for hh in range(4):
                        tr(b.ap[0:96, hh * P:(hh + 1) * P], src[:, 4 * n + hh, :], inc=(hh == 3))
                    cp(S, dst[0:96, 4 * n:4 * n + 4, sl], b.v(4, P, 96), PE.t)
                    b.give(S.t)
            qkr.give(kx, PE.t)
            t_mq.append((S.t, V.t))
        wring.give(k, PE.t)

        psd = A["ps"]
        zrow = m2.get(RW // 16)
        G.do(lambda e: e.memset(zrow, 0.0))
        ln4 = [next(lines) for _ in range(3)]
        t_ps = [(x[0], 0) for x in ln4]
        t_ps[2] = load(psd[0:1, :].rearrange("a (p n) -> (a p) n", p=16), zrow[0:16, :], G.t, q=S, ln=ln4[2])
        pjobs = []
        for blk, (c0, n) in enumerate(((416, 512), (928, 512), (1440, 512), (1952, 256))):
            k, t, w = wblock(A["w_in_2"][:, c0:c0 + n], n)

            def job(t_, k=k, t=t, w=w, c0=c0, n=n):
                b = Bank()
                PE.wait(t, *b.w)
                proj(w, n, t_, b)
                if t_ == NT - 1:
                    wring.give(k, PE.t)
                kx, wx = psr.take()
                cp(S, pst[:, kx, 0:n], b.ap[:, 0:n], PE.t, *wx)
                b.give(S.t)
                t2 = S.dma(ln4[kx], psd[1 + t_ * P:1 + (t_ + 1) * P, c0 - 416:c0 - 416 + n], pst[:, kx, 0:n], S.t)
                psr.give(kx, t2)
                t_ps[kx] = t2
            for t_ in range(NT):
                job(t_)

        aring = Ring(3)
        SC = float(np.float32(96 ** -0.5))
        for t_ in range(NT):
            sl = slice(t_ * P, (t_ + 1) * P)
            ob = Bank(po)
            PE.wait(*ob.w)
            attention(t_, list(range(H)), lambda h: mqT[0:96, h, sl], lambda h, n: mkT[0:96, h, 0:n],
                      lambda h, kb: mv[:, kb, h * 64:h * 64 + 64], ob, mst[:, t_, 32:40], mst[:, t_, 40:48], SC,
                      aring, ring3, t_mq[t_], [])
            V.do(lambda e, t_=t_: e.reciprocal(mst[:, t_, 48:56], mst[:, t_, 32:40]), S.t)
            tt(V, h3(omla[:, t_, :]), ob.v(H, 64), bx(mst[:, t_, 48:56], 2, (P, H, 64)), MUL, V.t, PE.t)
            ob.give(V.t)
        dbg("omla", omla, V.t)
        bt = barrier()
        if stop == "mla":
            return finish(nc, ctx, (PE, V, S, G, SP), ldone)

        r2 = Space(m2.ap, root.at + NT * 512, m2.end - root.at - NT * 512)
        K2 = {}
        c2 = r2.get(sum(C2.values()))
        o = 0
        for kx, n in C2.items():
            K2[kx] = c2[:, o:o + n]
            o += n
        rows = r2.get(RW + 7 * 512)
        ln5 = next(lines)
        load(c2, A["c2"], *bt, *t_ps, q=G, ln=ln5)
        o = 0
        RWS = []
        for nm, n in (("mu_shift_2", RW), ("decay_base_2", 512), ("aaa_base_2", 512), ("k_k_2", 512), ("k_a_2", 512),
                      ("r_k_2", 512), ("ln_x_w_2", 512), ("ln_x_b_2", 512)):
            t_row = load(rows[:, o:o + n], A[nm].partition_broadcast(P), q=G, ln=ln5)
            RWS.append(rows[:, o:o + n])
            o += n
        mu, dbase, abase, kkw, kaw, rkw, lnw, lnb = RWS
        pp = r2.get(RW)
        pr = r2.get(RW)
        tl = [r2.get(512) for _ in range(9)]
        X1 = r2.get(4, 2, P)
        BK = r2.get(4, 2, P)
        MM = r2.get(2, 4, 4, P)
        Xb = [r2.get(4, P) for _ in range(2)]
        XTb = [r2.get(4, P) for _ in range(2)]
        T1b = [r2.get(4, P) for _ in range(2)]
        AMb = [r2.get(4, P) for _ in range(2)]
        T_ = [r2.get(4, P) for _ in range(3)]
        PCm = r2.get(2, 4, P)
        pcc = r2.get(4, 2)
        rst = r2.get(64)
        orw = [r2.get(512) for _ in range(1)]
        k, t_up = wload((lambda s: s[0:64, 0:512], A["w_decay_up_2"]), (lambda s: s[64:128, 0:512], A["w_aaa_up_2"]),
                        (lambda s: s[:, 512:1024], A["w_gate_up_2"]))
        kup = k
        wup = wslot[k]
        ln6 = next(lines)
        v4 = lambda ap: ap.rearrange("p (a b) -> p a b", a=4)
        G.do(lambda e: e.memset(T_[0], 0.0))
        t_T = G.t
        cur = 0
        c_ = 0
        orT = r2.get(4, 512) if False else None
        olist = []
        oro = A["orw"]
        for t_ in range(NT):
            bt = [q.t for q in QS]
            load(pp, psd[1 + t_ * P:1 + (t_ + 1) * P, :], *bt, *t_ps, q=S, ln=ln6)
            t_in = load(pr, psd[t_ * P:(t_ + 1) * P, :], q=S, ln=ln6)
            tt(G, pr, pr, pp, SUB, t_in)
            tt(V, pr, pr, mu, MUL, G.t, t_row)
            tt(G, pr, pr, pp, ADD, V.t)
            t_p = G.t
            r_, k_, v_ = pr[:, 0:512], pr[:, 512:1024], pr[:, 1024:1536]
            wd, gd = pr[:, 1536:1600], pr[:, 1664:1792]
            act(wd, wd, ACT.Tanh, t_p)
            act(gd, gd, ACT.Tanh, scale=0.5)
            ts(V, gd, gd, 0.5, 0.5, MUL, ADD, S.t)
            b = Bank()
            PE.wait(*b.w, V.t, t_p)
            for j in range(2):
                tr(b.ap[:, j * P:(j + 1) * P], pr[:, 1536 + j * P:1536 + (j + 1) * P], inc=(j == 1))
            loT = pp[:, 0:256].rearrange("p (a b) -> p a b", a=2)
            cp(V, loT, b.v(2, P), PE.t)
            b.give(V.t)
            b0, b1, b2 = Bank(), Bank(), Bank()
            PE.wait(*b0.w, *b1.w, *b2.w, V.t, t_up)
            mm(b0.ap, loT[0:64, 0], wup[0:64, 0:512], True, True, inc=True)
            mm(b1.ap, loT[64:128, 0], wup[64:128, 0:512], True, True, inc=True)
            mm(b2.ap, loT[:, 1], wup[:, 512:1024], True, True, inc=True)
            if t_ == NT - 1:
                wring.give(kup, PE.t)
            L, a_, g_, kk, kh, e1, e2, bt_, y_ = tl
            tt(V, L, b0.ap, dbase, ADD, PE.t, t_row)
            b0.give(V.t)
            tt(V, a_, b1.ap, abase, ADD)
            b1.give(V.t)
            cp(S, g_, b2.ap, PE.t)
            b2.give(S.t)
            act(L, L, ACT.Tanh, V.t, scale=0.5)
            act(a_, a_, ACT.Tanh, scale=0.5)
            ts(V, L, L, -0.5 * EM05, -0.5 * EM05, MUL, ADD, S.t)
            t_L = V.t
            bc = Bank()
            PE.wait(*bc.w, t_L)
            mm(bc.ap, K2["tri"], L, True, True, inc=True)
            t_cum = PE.t
            bp = Bank()
            PE.wait(*bp.w)
            for p in range(4):
                mm(bp.ap[:, 2 * p:2 * p + 2], L[:, p * P:(p + 1) * P], K2["sel"], True, True, inc=(p == 3))
            t_pc = PE.t
            ts(V, a_, a_, 0.5, 0.5, MUL, ADD)
            tt(V, kk, k_, kkw, MUL, t_row, t_p)
            tt(G, e1, kk, kk, MUL, V.t)
            red(rst[:, 0:8], h3(e1), ADD, G.t)
            ts(V, rst[:, 0:8], rst[:, 0:8], 1e-24, None, MAX, None, V.t)
            pow_nhalf(rst[:, 0:8], 8, V.t)
            tt(V, h3(kk), h3(kk), bx(rst[:, 0:8], 2, (P, H, 64)), MUL, G.t)
            t_kk = V.t
            stt(bt_, kk, -1.0, a_, MUL, MUL, V.t)
            stt(kh, a_, -1.0, kaw, ADD, MUL, V.t)
            stt(kh, kh, 1.0, k_, ADD, MUL, V.t)
            t_kh = V.t
            tt(V, e2, r_, kh, MUL, V.t)
            tt(V, e2, e2, rkw, MUL, V.t)
            red(rst[:, 8:16], h3(e2), ADD, V.t)
            t_e2 = V.t
            act(e1, bc.ap, ACT.Exp, t_cum, V.t)
            tt(V, r_, r_, e1, MUL, S.t)
            t_Rp = V.t
            act(e1, bc.ap, ACT.Exp, V.t, scale=-1.0)
            tt(V, L, bc.ap, L, SUB, S.t, t_pc)
            bc.give(V.t)
            act(e2, L, ACT.Exp, V.t)
            act(pcc, bp.v(4, 2), ACT.Exp, t_pc)
            bp.give(S.t)
            tt(V, kk, kk, e2, MUL, S.t)
            tt(V, kh, kh, e1, MUL)
            tt(V, bt_, bt_, e1, MUL)
            t_all = V.t
            for c in range(2):
                tt(G, PCm[:, c], bx(C["bd"], 1, (P, 4, P)), bx(pcc[:, :, c], 2, (P, 4, P)), MUL, S.t)
            t_PC = G.t
            for n, (src, dst) in enumerate(((kk, X1[:, :, 0]), (r_, X1[:, :, 1]), (bt_, BK[:, :, 0]), (kh, BK[:, :, 1]))):
                turn(t_all, src, dst, V if n % 2 else S)
            t_X = (V.t, S.t)
            mk = bx(K2["mm"], 1, (P, 2, 256))
            for e in range(2):
                rw = slice(64 * e, 64 * e + 64)
                for p in range(4):
                    b = Bank()
                    PE.wait(*b.w, *t_X)
                    x1 = X1[rw, p].rearrange("p a b -> p (a b)")
                    mm(b.ap[:, 0:256], BK[rw, p, 0, :], x1, True, True)
                    mm(b.ap[:, 256:512], BK[rw, p, 1, :], x1, True, True, inc=True)
                    tt(V, MM[:, e, p].rearrange("p (a b) c -> p a (b c)", a=2), b.v(2, 256), mk, MUL, PE.t)
                    b.give(V.t)
            t_MM = V.t
            for e in range(2):
                rw = slice(64 * e, 64 * e + 64)
                b = Bank()
                PE.wait(*b.w)
                for p in range(4):
                    mm(b.ap[:, p * P:(p + 1) * P], X1[rw, p, 0, :], BK[rw, p, 0, :], True, True, inc=(p == 3))
                tt(V, Xb[e], b.v(4, P), bx(K2["m1"], 1, (P, 4, P)), MUL, PE.t)
                b.give(V.t)
                tt(V, Xb[e], Xb[e], bx(ident, 1, (P, 4, P)), ADD, V.t)
                tt(G, XTb[e], MM[:, e, :, 0, :], bx(K2["mt"][:, 0:P], 1, (P, 4, P)), MUL, t_MM)
                tt(G, XTb[e], XTb[e], bx(ident, 1, (P, 4, P)), ADD, G.t)
            xt_t = [[V.t, G.t], [V.t, G.t]]
            am_w = [[], []]
            for l in range(1, 6):
                am = []
                for e in range(2):
                    am.append(tt(G, AMb[e], MM[:, e, :, 0, :], bx(K2["mt"][:, l * P:(l + 1) * P], 1, (P, 4, P)), MUL,
                                 *am_w[e]))
                t1 = []
                for e in range(2):
                    b = Bank()
                    PE.wait(*b.w, am[e], *xt_t[e])
                    for p in range(4):
                        mm(b.ap[:, p * P:(p + 1) * P], AMb[e][:, p], Xb[e][:, p], True, True, inc=(p == 3))
                    am_w[e] = [PE.t]
                    cp(S, T1b[e], b.v(4, P), PE.t)
                    b.give(S.t)
                    t1.append(S.t)
                for e in range(2):
                    ba = Bank() if l < 5 else None
                    bb = Bank()
                    PE.wait(*bb.w, t1[e])
                    if ba:
                        PE.wait(*ba.w)
                        for p in range(4):
                            mm(ba.ap[:, p * P:(p + 1) * P], XTb[e][:, p], T1b[e][:, p], True, True, inc=(p == 3))
                    for p in range(4):
                        mm(bb.ap[:, p * P:(p + 1) * P], T1b[e][:, p], XTb[e][:, p], True, True, inc=(p == 3))
                    if ba:
                        tt(V, Xb[e], Xb[e], ba.v(4, P), ADD, PE.t)
                        ba.give(V.t)
                    tt(V, XTb[e], XTb[e], bb.v(4, P), ADD, PE.t)
                    bb.give(V.t)
                    xt_t[e] = [V.t]
            BV, U, WT, SA = T1b[0].rearrange("p a b -> p (a b)"), T1b[1].rearrange("p a b -> p (a b)"), \
                AMb[0], AMb[1].rearrange("p a b -> p (a b)")
            hs = lambda h: slice(h * 64, h * 64 + 64)
            b = Bank()
            PE.wait(*b.w, V.t, t_p)
            for h in range(H):
                mm(b.ap[:, hs(h)], MM[:, h % 2, h // 2, 2, :], v_[:, hs(h)], True, True, inc=(h == 7))
            cp(S, BV, b.ap, PE.t)
            b.give(S.t)
            b = Bank()
            PE.wait(*b.w, S.t)
            for h in range(H):
                mm(b.ap[:, hs(h)], XTb[h % 2][:, h // 2], BV[:, hs(h)], True, True, inc=(h == 7))
            cp(S, U, b.ap, PE.t)
            b.give(S.t)
            t_U = S.t
            b = Bank()
            PE.wait(*b.w)
            for e in range(2):
                for p in range(4):
                    h = 2 * p + e
                    mm(b.ap[64 * e:64 * e + 64, p * P:(p + 1) * P], kk[:, hs(h)], XTb[e][:, p], True, True,
                       inc=(e == 1 and p == 3))
            cp(S, WT, b.v(4, P), PE.t)
            b.give(S.t)
            t_WT = S.t
            by = Bank(po)
            for c in range(2):
                rw = slice(64 * c, 64 * c + 64)
                Tc, Tn = T_[cur], T_[(cur + 1) % 3]
                b = Bank()
                PE.wait(*b.w, t_WT, t_T)
                for p in range(4):
                    mm(b.ap[rw, p * P:(p + 1) * P], WT[:, p, rw], Tc[:, p], True, True, inc=(p == 3))
                tt(V, SA[rw, :], b.ap[rw, :], U[rw, :], ADD, PE.t, t_U)
                b.give(V.t)
                t_sa = V.t
                b = Bank()
                PE.wait(*b.w, *by.w, t_sa)
                for p in range(4):
                    mm(by.ap[rw, p * P:(p + 1) * P], X1[:, p, 1, rw], Tc[:, p], True, True, inc=(p == 3))
                t_by = PE.t
                for p in range(4):
                    cs = slice(p * P, (p + 1) * P)
                    mm(b.ap[:, cs], kh[rw, cs], v_[rw, cs], True, False)
                    mm(b.ap[:, cs], bt_[rw, cs], SA[rw, cs], False, True, inc=(p == 3))
                tt(V, Tn, Tc, b.v(4, P), ADD, PE.t)
                b.give(V.t)
                tt(V, Tn, Tn, PCm[:, c], MUL, V.t, t_PC)
                t_T = V.t
                cur = (cur + 1) % 3
            b = Bank()
            PE.wait(*b.w, t_sa)
            for h in range(H):
                mm(b.ap[:, hs(h)], MM[:, h % 2, h // 2, 1, :], SA[:, hs(h)], True, False)
                mm(b.ap[:, hs(h)], MM[:, h % 2, h // 2, 3, :], v_[:, hs(h)], False, True, inc=(h == 7))
            cp(S, y_, by.ap, t_by)
            by.give(S.t)
            tt(V, y_, y_, b.ap, ADD, PE.t, S.t)
            b.give(V.t)
            red(rst[:, 16:24], h3(y_), ADD, V.t)
            ts(V, rst[:, 16:24], rst[:, 16:24], -1.0 / 64, None, MUL, None, V.t)
            tt(V, h3(y_), h3(y_), bx(rst[:, 16:24], 2, (P, H, 64)), ADD, V.t)
            tt(G, e1, y_, y_, MUL, V.t)
            red(rst[:, 24:32], h3(e1), ADD, G.t)
            ts(V, rst[:, 24:32], rst[:, 24:32], 1.0 / 64, 64e-5, MUL, ADD, V.t)
            pow_nhalf(rst[:, 24:32], 8, V.t)
            tt(V, h3(y_), h3(y_), bx(rst[:, 24:32], 2, (P, H, 64)), MUL, G.t)
            tt(V, y_, y_, lnw, MUL, V.t)
            tt(V, y_, y_, lnb, ADD, V.t)
            tt(G, h3(v_), h3(v_), bx(rst[:, 8:16], 2, (P, H, 64)), MUL, PE.t, V.t)
            tt(V, y_, y_, v_, ADD, G.t)
            tt(V, y_, y_, g_, MUL, V.t)
            if tap is not None:
                dbg(f"y{t_}", y_, V.t)
            t_o = load(oro[t_ * P:(t_ + 1) * P, :], y_, V.t, q=S, ln=ln6)
            for q in QS:
                q.wait(t_o)
        bt = barrier()
        if stop == "rwkv":
            return finish(nc, ctx, (PE, V, S, G, SP), ldone)

        ph = Space(m2.ap, root.at + NT * 512, m2.end - root.at - NT * 512)
        xt = ph.get(NT, D)
        mix = ph.get(NT, D)
        orr = ph.get(NT, 512)
        oT = ph.get(2, 4, 512)
        tg = ph.get(2, 512)
        ss3 = ph.get(16)
        ln7 = next(lines)
        t_or = load(orr, oro.rearrange("(t p) d -> p t d", p=P), *bt, q=S, ln=ln7)
        t_x2 = load(xt, A["xs"].rearrange("(t p) d -> p t d", p=P), q=S, ln=next(lines))
        for which, src, w_ in ((0, omla, ()), (1, orr, (t_or,))):
            for j in range(4):
                b = Bank()
                PE.wait(*b.w, *w_)
                for t_ in range(NT):
                    tr(b.ap[:, t_ * P:(t_ + 1) * P], src[:, t_, j * P:(j + 1) * P], inc=(t_ == NT - 1))
                q = V if j % 2 else S
                cp(q, oT[:, which, j, :], b.ap, PE.t)
                b.give(q.t)
        t_oT = (S.t, V.t)
        gring = Ring(2)
        for which, nm in ((0, "w_o_mla_2"), (1, "w_o_rwkv_2")):
            k, t = wload((lambda s: s.rearrange("p (j n) -> p j n", j=4), A[nm].rearrange("(j p) n -> p j n", p=P)))
            w = wslot[k].rearrange("p (j n) -> p j n", j=4)
            for n in range(2):
                kg, tg_, wg = wblock(A["w_in_2"][:, 2208 + which * D + n * 512:2208 + which * D + n * 512 + 512], 512)
                for t_ in range(NT):
                    b = Bank()
                    PE.wait(*b.w, tg_)
                    proj(wg, 512, t_, b)
                    kx, wx = gring.take()
                    act(tg[:, kx, :], b.ap, ACT.Tanh, PE.t, *wx, scale=0.5)
                    b.give(S.t)
                    b = Bank()
                    PE.wait(*b.w, t, *t_oT)
                    for j in range(4):
                        mm(b.ap, oT[:, which, j, t_ * P:(t_ + 1) * P], w[:, j, n * 512:n * 512 + 512], j == 0, j == 3,
                           inc=(j == 3))
                    dst = mix[:, t_, n * 512:n * 512 + 512]
                    if which == 0:
                        stt(dst, tg[:, kx, :], 1.0, b.ap, ADD, MUL, PE.t, S.t)
                        b.give(V.t)
                        gring.give(kx, V.t)
                    else:
                        stt(tg[:, kx, :], tg[:, kx, :], 1.0, b.ap, ADD, MUL, PE.t, S.t)
                        b.give(V.t)
                        tt(G, dst, dst, tg[:, kx, :], ADD, V.t)
                        gring.give(kx, G.t)
                wring.give(kg, PE.t)
            wring.give(k, PE.t)
        t_h1 = PE.t
        mtok = transpose_into_hT(mix, NJ, (G.t, V.t))
        ws = [wblock(A["w_out_2"][:, n * 512:n * 512 + 512], 512) for n in range(2)]
        for t_ in range(NT):
            for n in range(2):
                k, t, w = ws[n]
                b = Bank()
                PE.wait(*b.w, t, *mtok)
                proj(w, 512, t_, b)
                stt(mix[:, t_, n * 512:n * 512 + 512], b.ap, 0.5, gt1_2[:, n * 512:n * 512 + 512], MUL, MUL, PE.t)
                b.give(V.t)
                tt(G, xt[:, t_, n * 512:n * 512 + 512], xt[:, t_, n * 512:n * 512 + 512],
                   mix[:, t_, n * 512:n * 512 + 512], ADD, V.t, t_x2)
        for n in range(2):
            wring.give(ws[n][0], PE.t)
        t_x3 = G.t
        dbg("x2", xt, t_x3)
        hready = make_hT(xt, (t_x3,), 32, t_col3, (mix, ss3), (G.t, PE.t))
        dbg("h3T", hT, *hready)
        bt = barrier()
        t_xsp = load(A["xs"].rearrange("(t p) d -> p t d", p=P), xt, *bt, q=S, ln=next(lines))
        for q in QS:
            q.wait(t_xsp)

        ph = root.rest()
        NA = 5
        Ab = [ph.get(GC, 512) for _ in range(3)]
        early = ph.rest()
        hk = ph.rest()
        Ab += [hk.get(GC, 512) for _ in range(2)]
        late = hk.rest()
        hkT = hk.get(3, 512)
        gspace = hk.rest()
        hkE = early.get(3, 512)
        qT = early.get(16, 512)
        sk = early.get(2, P)
        ln8 = next(lines)
        load(sk[:, 0, :], A["sub_keys1_2"], *bt, t_xsp, q=G, ln=ln8)
        t_sk = load(sk[:, 1, :], A["sub_keys2_2"], q=G, ln=ln8)
        for n in range(4):
            k, t, w = wblock(A["w_query_2"][:, n * 512:n * 512 + 512], 512)
            PE.wait(t, *hready)
            for m in range(4):
                b = Bank()
                PE.wait(*b.w)
                for j in range(NJ):
                    mm(b.ap, w[:, j, m * P:(m + 1) * P], hT[:, j, :], j == 0, j == NJ - 1, inc=(j == NJ - 1))
                cp(S, qT[:, 4 * n + m, :], b.ap, PE.t)
                b.give(S.t)
            wring.give(k, PE.t)
        t_qT = S.t

        Aring = Ring(NA)
        upq = []

        def up_start(g):
            st_ = {"toks": []}

            def piece(m):
                if m == 0:
                    st_["a"], st_["wa"] = Aring.take()
                if m % 4 == 0:
                    st_["k"], st_["t"] = wload((lambda s: s, A["down"][g * (GC // 4) + m // 4]))
                k, t = st_["k"], st_["t"]
                w = wslot[k].rearrange("p (j n) -> p j n", j=NJ)
                b = Bank()
                PE.wait(*b.w, t)
                for j in range(NJ):
                    mm(b.ap, w[:, j, (m % 4) * P:(m % 4 + 1) * P], hT[:, j, :], j == 0, j == NJ - 1,
                       inc=(j == NJ - 1))
                if m % 4 == 3:
                    wring.give(k, PE.t)
                act(Ab[st_["a"]][:, m, :], b.ap, ACT.Gelu_apprx_tanh, PE.t, *st_["wa"])
                b.give(S.t)
                st_["toks"].append(S.t)

            for m in range(GC):
                side.append(lambda m=m: piece(m))
            upq.append(st_)

        for g in range(3):
            up_start(g)
        side_every[0] = 2
        sb_ = early.get(2, 16, P)
        sbr = Ring(2)
        v16 = early.get(16, 16)
        i16 = early.get(16, 16).bitcast(U32)
        if16 = early.get(16, 16)
        cand = early.get(H, 256)
        cv = early.get(H, 16)
        ci = early.get(H, 16).bitcast(U32)
        cif = early.get(4, H, 16)
        eq = early.get(H, 16, 16)
        e3 = early.get(3, P)
        NEGF = -3.0e38
        s_free = []
        for t_ in range(NT):
            kx, wx = sbr.take()
            sc = sb_[:, kx]
            fill()
            for n in range(4):
                b = Bank()
                PE.wait(*b.w, t_qT, t_sk)
                for m in range(4):
                    mm(b.ap[:, m * P:(m + 1) * P], qT[:, 4 * n + m, t_ * P:(t_ + 1) * P], sk[:, m % 2, :], True, True,
                       inc=(m == 3))
                cp(S, sc[:, 4 * n:4 * n + 4, :], b.v(4, P), PE.t, *wx)
                b.give(S.t)
            V.wait(S.t)
            def top16(n, src, vals, idx):
                def mx(m, o):
                    s_, v_ = src(m), vals(m)[:, o:o + 8]
                    return V.do(lambda e: e.max(v_, s_), tk[m])

                def ix(m, o):
                    s_, v_, i_ = src(m), vals(m)[:, o:o + 8], idx(m)[:, o:o + 8]
                    return V.do(lambda e: e.max_index(i_, v_, s_), tk[m])

                def rp(m, o):
                    s_, v_ = src(m), vals(m)[:, 0:8]
                    return V.do(lambda e: e.match_replace(s_, v_, s_, NEGF), tk[m])

                tk = [V.t] * n
                for f, o in ((mx, 0), (ix, 0), (rp, 0), (mx, 8), (ix, 8)):
                    tk = [f(m, o) for m in range(n)]
                    fill()

            top16(16, lambda m: sc[:, m, :], lambda m: v16[:, m, :], lambda m: i16[:, m, :])
            sbr.give(kx, V.t)
            cp(V, if16, i16, V.t)
            vv = v16.rearrange("p (h w) k -> p h w k", w=2)
            ii = if16.rearrange("p (h w) k -> p h w k", w=2)
            tcd = V.t
            for h in range(H):
                cd = cand[:, h, :].rearrange("p (a b) -> p a b", a=16)
                tt(V, cd, bx(vv[:, h, 0], 2, (P, 16, 16)), bx(vv[:, h, 1], 1, (P, 16, 16)), ADD, tcd)
            top16(8, lambda h: cand[:, h, :], lambda h: cv[:, h, :], lambda h: ci[:, h, :])
            cu = cif[:, 3].bitcast(U32)
            V.do(lambda e: e.tensor_scalar(cu, ci, 4, None, ALU.logical_shift_right), V.t)
            cp(V, cif[:, 0], cu, V.t)
            V.do(lambda e: e.tensor_scalar(cu, ci, 15, None, ALU.bitwise_and), V.t)
            cp(V, cif[:, 1], cu, V.t)
            io = C["iota"][:, 0:16]
            for w_ in range(2):
                te0 = V.t
                te = [tt(V, eq[:, h], bx(cif[:, w_, h], 2, (P, 16, 16)), bx(io, 1, (P, 16, 16)), EQ, te0)
                      for h in range(H)]
                for h in range(H):
                    tt(V, eq[:, h], eq[:, h], bx(ii[:, h, w_], 1, (P, 16, 16)), MUL, te[h])
                red(e3[:, w_, :].rearrange("p (h k) -> p h k", h=H), eq, ADD, V.t, *s_free)
                fill()
            cpm = cif[:, 2, :, 0]
            cp(V, cpm, cv[:, :, 0], V.t)
            tt(V, cv, cv, bx(cpm, 2, (P, H, 16)), SUB, V.t)
            act(cv, cv, ACT.Exp, V.t)
            red(cpm, cv, ADD, S.t)
            V.do(lambda e: e.reciprocal(cpm, cpm), V.t)
            tt(V, e3[:, 2, :].rearrange("p (h k) -> p h k", h=H), cv, bx(cpm, 2, (P, H, 16)), MUL, V.t)
            b = Bank()
            PE.wait(*b.w, V.t)
            for w_ in range(3):
                tr(b.ap[:, w_ * P:(w_ + 1) * P], e3[:, w_, :], inc=(w_ == 2))
            s_free = [PE.t]
            cp(S, hkE[:, :, t_ * P:(t_ + 1) * P], b.ap[:, 0:384].rearrange("p (a b) -> p a b", a=3), PE.t)
            b.give(S.t)

        drain_side()
        bt = barrier()
        t_hk = cp(V, hkT, hkE)
        V.wait(t_hk)
        G.wait(t_hk)
        bt = [t_hk, *bt]
        S.wait(t_hk)
        PE.wait(t_hk)
        NOH = 8
        TB = 64
        ls = gspace
        stg = ls.get(P, TB)
        oh = [(ls.get(P), ls.get(P)) for _ in range(NOH)]
        ohr = Ring(NOH)
        gd_ = A["gd"]
        lng = next(lines)
        sfree = []
        iota = C["iota"]
        up_start(3)
        up_start(4)
        for tb in range(512 // TB):
            for q4 in range(TB // 4):
                if q4 % 8 == 3 and side:
                    side.pop(0)()
                b = Bank()
                PE.wait(*b.w)
                for u in range(4):
                    tok = tb * TB + q4 * 4 + u
                    kx, wx = ohr.take()
                    o1, o2_ = oh[kx]
                    q = G if u % 2 == 0 else V
                    q.wait(*wx)
                    V.wait(*wx)
                    a = ts(q, o2_, iota, hkT[:, 1, tok:tok + 1], None, EQ, None)
                    c = ts(V, o1, iota, hkT[:, 0, tok:tok + 1], hkT[:, 2, tok:tok + 1], EQ, MUL)
                    mm(b.ap[:, u * P:(u + 1) * P], o2_, o1, True, True, a, c, inc=True)
                    ohr.give(kx, PE.t)
                src = b.v(4, P).rearrange("p u a -> p a u")
                cp(S, stg[:, :, q4 * 4:q4 * 4 + 4], src, PE.t, *sfree)
                b.give(S.t)
            t_g = S.dma(lng, gd_[tb].rearrange("b a t -> b (a t)"), stg.rearrange("p a t -> p (a t)"), S.t)
            sfree = [t_g]
        drain_side()
        for q in (V, G, S, SP):
            q.wait(t_g)
        bt = [q.t for q in QS]
        SP.wait(*bt)
        V.wait(*bt)
        G.wait(*bt)
        S.wait(*bt)

        ls = late
        Y = ls.get(NT, D)
        Gb = [ls.get(8, GC, TB) for _ in range(2)]
        gline = [line("g0"), line("g1")]
        gring = Ring(2)

        def gates(g, ka_, toks):
            kg, wg = gring.take()
            for half in range(2):
                t = SP.dma(gline[kg], Gb[kg][:, 4 * half:4 * half + 4], gd_[4 * half:4 * half + 4, :, g * GC:(g + 1) * GC, :].rearrange("b p a t -> p b (a t)").rearrange(
                    "p b (a t) -> p b a t", a=GC), *wg)
            for m in range(GC):
                a = Ab[ka_][:, m, :].rearrange("p (b t) -> p b t", b=8)
                r = tt(V if m % 4 else G, a, a, Gb[kg][:, :, m, :], MUL, t, toks[m])
            gring.give(kg, V.t, G.t)
            return V.t, G.t

        def down_sum(g, ka_, toks):
            ups = [wload((lambda s: s, A["up"][g * (GC // 4) + blk])) for blk in range(GC // 4)]
            for t_ in range(NT):
                for n in range(2):
                    b = Bank()
                    PE.wait(*b.w, *toks, *[u[1] for u in ups])
                    for m in range(GC):
                        w = wslot[ups[m // 4][0]].rearrange("p (m n) -> p m n", m=4)
                        mm(b.ap, Ab[ka_][:, m, t_ * P:(t_ + 1) * P], w[:, m % 4, n * 512:n * 512 + 512],
                           m == 0, m == GC - 1, inc=(m == GC - 1))
                    y = Y[:, t_, n * 512:n * 512 + 512]
                    if g == 0:
                        cp(V, y, b.ap, PE.t)
                    else:
                        tt(V, y, y, b.ap, ADD, PE.t, V.t)
                    b.give(V.t)
            for u in ups:
                wring.give(u[0], PE.t)
            Aring.give(ka_, PE.t)

        gt = gates(0, upq[0]["a"], upq[0]["toks"])
        for g in range(NG):
            nxt = gates(g + 1, upq[g + 1]["a"], upq[g + 1]["toks"]) if g + 1 < NG else None
            down_sum(g, upq[g]["a"], gt)
            gt = nxt
            if g + NA < NG:
                up_start(g + NA)
                drain_side()
        lno = next(lines)
        xo = Gb[0].rearrange("p a b c -> p (a b c)").rearrange("p (t d) -> p t d", t=NT)
        t_xl = load(xo, A["xs"].rearrange("(t p) d -> p t d", p=P), V.t, G.t, q=S, ln=next(lines))
        for t_ in range(NT):
            tt(V, Y[:, t_, :], Y[:, t_, :], gt2_2, MUL, V.t)
            tt(V, Y[:, t_, :], Y[:, t_, :], xo[:, t_, :], ADD, V.t, t_xl)
            to = SP.dma(lno, out[t_ * P:(t_ + 1) * P, :], Y[:, t_, :], V.t)
        ldone.append(to)
        return finish(nc, ctx, (PE, V, S, G, SP), ldone)


def finish(nc, ctx, queues, ldone):
    PE, V, S, G, SP = queues
    SP.wait(*ldone)
    block = ctx.enter_context(nc.Block())

    @block.sync
    def _(e):
        SP.emit(e)

    @block.gpsimd
    def _(e):
        G.emit(e)

    @block.scalar
    def _(e):
        S.emit(e)

    @block.vector
    def _(e):
        V.emit(e)

    @block.tensor
    def _(e):
        PE.emit(e)


def layout(inputs):
    f = lambda n: np.asarray(inputs[n])
    col = lambda a, n: np.ascontiguousarray(a.reshape(n, 128).T)
    m = {}
    m["cst"], m["c1"], m["c2"] = constants()
    m["x"] = f("x")[0]
    m["c"] = col(f("c")[0], 8)
    m["c_2"] = col(f("c_2")[0], 8)
    p1, p2 = f("positions")[0], f("positions_2")[0]
    ce = p1[31::16]
    ce = np.concatenate([ce, ce[-1:]])
    ce = np.concatenate([ce, ce, ce, ce])
    m["pos"] = np.ascontiguousarray(np.concatenate([p1.reshape(4, 128), ce[None], p2.reshape(4, 128)]).T)
    m["w_ada"], m["w_ada_2"] = f("w_ada")[0], f("w_ada_2")[0]
    m["b_ada_c"], m["b_ada_2_c"] = col(f("b_ada")[0], 24), col(f("b_ada_2")[0], 48)
    m["b_ada_r"], m["b_ada_2_r"] = f("b_ada")[0], f("b_ada_2")[0]
    for n in ("g_pre", "norm_mix_2", "norm_ffn_2"):
        m[n] = col(f(n)[0], 8)
    m["g_post"] = f("g_post")[0]
    for n in ("w_in", "w_out", "cmp_w1_k", "cmp_w1_v", "cmp_w2_k", "cmp_w2_v", "w_in_2", "w_uq_2", "w_ukv_2",
              "w_o_mla_2", "w_decay_up_2", "w_aaa_up_2", "w_gate_up_2", "w_o_rwkv_2", "w_out_2", "w_query_2",
              "mu_shift_2", "decay_base_2", "aaa_base_2", "k_k_2", "k_a_2", "ln_x_w_2", "ln_x_b_2",
              "q_norm_2", "k_norm_2"):
        m[n] = f(n)[0]
    m["r_k_2"] = f("r_k_2")[0].reshape(512)
    for n in ("cmp_pe_k", "cmp_pe_v"):
        m[n] = col(f(n)[0].reshape(-1), 16)
    m["q_a_norm_2"] = col(f("q_a_norm_2")[0], 2)
    m["kv_a_norm_2"] = col(f("kv_a_norm_2")[0], 1)
    for n in ("sub_keys1_2", "sub_keys2_2"):
        m[n] = f(n)[0].T
    m["down"] = f("expert_down_2")[0].reshape(32, 512, 8, 128).transpose(0, 3, 2, 1).reshape(32, 128, 4096)
    m["up"] = f("expert_up_2")[0].reshape(32, 4, 128, 1024).transpose(0, 2, 1, 3).reshape(32, 128, 4096)
    return {k: np.ascontiguousarray(v) for k, v in m.items()}


def program(nc, shapes, tap=None, stop=None):
    A = {}
    for name, (shape, dt) in shapes.items():
        A[name] = nc.dram_tensor("in_" + name, shape, dt, kind="ExternalInput").ap()
    for name, shape in (("xs", (512, D)), ("ps", (513, RW)), ("orw", (512, 512)), ("gd", (8, P, P, 64))):
        A[name] = nc.dram_tensor("scratch_" + name, shape, F32, kind="Internal").ap()
    out = nc.dram_tensor("out_0", (512, D), F32, kind="ExternalOutput").ap()
    build(nc, A, out, tap, stop)


def kernel(**inputs):
    import concourse.bacc as bacc
    from concourse.bass_utils import run_bass_kernel_spmd

    arrays = layout(inputs)
    nc = bacc.Bacc("TRN2", target_bir_lowering=False, num_devices=1)
    program(nc, {k: (v.shape, mybir.dt.from_np(v.dtype)) for k, v in arrays.items()})
    r = run_bass_kernel_spmd(nc, [{"in_" + k: v for k, v in arrays.items()}], core_ids=[0])
    return r.results[0]["out_0"].reshape(1, 512, 1024)
```

```python
from contextlib import ExitStack

import numpy as np

import concourse.bass as bass
from concourse import mybir

F32 = mybir.dt.float32
F32R = mybir.dt.float32r
BF16 = mybir.dt.bfloat16
I32 = mybir.dt.int32
U32 = mybir.dt.uint32
ALU = mybir.AluOpType
ACT = mybir.ActivationFunctionType
AXX = mybir.AxisListType.X
ADD, SUB, MUL, MAX, MIN, EQ, POW = (ALU.add, ALU.subtract, ALU.mult, ALU.max, ALU.min, ALU.is_equal, ALU.pow)

P = 128
NT = 4
D = 1024
NJ = 8
H = 8
PW1 = 3864
PW2 = 4256
RW = 1792
NE = 16384
NU = NE // 512
NE_ = 16
EM05 = float(np.exp(-0.5))


def constants():
    f = np.float32
    i = np.arange(128)
    c = {}
    c["ident"] = np.eye(128, dtype=f)
    c["caus"] = np.where(i[None, :] <= i[:, None], 0.0, -1e30).astype(f)
    c["iota"] = np.broadcast_to(i.astype(f), (128, 128))
    c["bd"] = (i[:, None] // 64 == i[None, :] // 64).astype(f)
    inv = [np.power(f(b), -np.arange(n, dtype=f) / f(n)).astype(f)
           for b, n in ((10000.0, 32), (500000.0, 8), (10000.0, 16))]
    c["inv"] = np.broadcast_to(np.concatenate(inv), (128, 56))
    c["nhalf"] = np.full((128, 32), -0.5, f)
    cst = np.ascontiguousarray(np.concatenate([c[k] for k in CST], axis=1), f)

    d = {}
    lg = np.log1p(-np.power(2.0, -5.0 - np.arange(H))).astype(f)
    diff = (i[None, :] - i[:, None]).astype(f)
    dec = np.where(diff[:, None, :] >= 0, np.exp(np.maximum(diff, 0)[:, None, :] * lg[None, :, None]), 0) * 0.125
    d["dec"] = dec.astype(f).reshape(128, 1024)
    d["zeta"] = np.exp((127 - i).astype(f)[:, None] * lg[None, :])
    d["xi"] = np.exp((i + 1).astype(f)[:, None] * lg[None, :]) * f(0.125)
    cd = np.exp(f(128) * lg)
    d["cd"] = np.concatenate([np.where(c["bd"] > 0, np.repeat(cd[2 * p:2 * p + 2], 64)[:, None], 0) for p in range(4)], 1)
    t = np.arange(512).reshape(4, 128)
    n = np.arange(32)
    ok = (n[None, None, :] * 16 + 31 <= t[:, :, None]) & (n < 31)
    ok = ok.transpose(1, 0, 2).reshape(128, 128)
    d["cneg"] = np.where(ok, 0.0, -1e30)
    d["cmul"] = ok.astype(f)
    d["hsel"] = 0.5 * (i[:, None] // 32 == np.arange(4)[None, :])
    c1 = np.ascontiguousarray(np.concatenate([d[k].astype(f) for k in C1], axis=1), f)

    e = {}
    same = i[:, None] // 64 == i[None, :] // 64
    e["tri"] = ((i[:, None] <= i[None, :]) & same).astype(f)
    e["mm"] = np.concatenate([((i[:, None] < i[None, :]) & same), ((i[:, None] <= i[None, :]) & same)], 1)

    def lev(l):
        b = 1 << (l - 1)
        t, s = i[:, None], i[None, :]
        return ((t // (2 * b) == s // (2 * b)) & (t // b % 2 == 1) & (s // b % 2 == 0)).astype(f)

    e["m1"] = lev(1)
    e["mt"] = np.concatenate([lev(l).T for l in range(1, 7)], 1)
    e["sel"] = (i[:, None] // 64 == np.arange(2)[None, :])
    c2 = np.ascontiguousarray(np.concatenate([e[k].astype(f) for k in C2], axis=1), f)
    return cst, c1, c2


CST = {"ident": 128, "caus": 128, "iota": 128, "bd": 128, "inv": 56, "nhalf": 32}
C1 = {"dec": 1024, "zeta": 8, "xi": 8, "cd": 512, "cneg": 128, "cmul": 128, "hsel": 4}
C2 = {"tri": 128, "mm": 256, "m1": 128, "mt": 768, "sel": 2}


class Queue:

    def __init__(self, sem):
        self.sem, self.n, self.items, self.seen = sem, 0, [], {}

    @property
    def t(self):
        return (self.sem, self.n)

    def wait(self, *toks):
        for sem, n in toks:
            if self.seen.get(id(sem), 0) < n:
                self.seen[id(sem)] = n
                self.items.append(lambda e, sem=sem, n=n: e.wait_ge(sem, n))

    def do(self, fn, *toks, inc=True):
        self.wait(*toks)
        if inc:
            self.n += 1
            self.items.append(lambda e: fn(e).then_inc(self.sem, 1))
        else:
            self.items.append(fn)
        return (self.sem, self.n)

    def dma(self, line, out, in_, *toks, **kw):
        self.wait(*toks)
        line[1] += 16
        self.items.append(lambda e: e.dma_start(out, in_, **kw).then_inc(line[0], 16))
        return (line[0], line[1])

    def emit(self, e):
        for f in self.items:
            f(e)


class Ring:

    def __init__(self, n):
        self.free, self.i = [[] for _ in range(n)], 0

    def take(self):
        k = self.i % len(self.free)
        self.i += 1
        toks, self.free[k] = self.free[k], None
        assert toks is not None, "buffer taken before it was given back"
        return k, toks

    def give(self, k, *toks):
        self.free[k] = list(toks)


class Space:
    def __init__(self, ap, base, size):
        self.ap, self.at, self.end = ap, base, base + size

    def get(self, *shape):
        n = int(np.prod(shape))
        assert self.at + n <= self.end, (self.at, n, self.end)
        v = self.ap[:, self.at:self.at + n]
        self.at += n
        if len(shape) == 1:
            return v
        names = "abcd"[:len(shape)]
        return v.rearrange(f"p ({' '.join(names)}) -> p {' '.join(names)}",
                           **{names[k]: shape[k] for k in range(len(shape))})

    def fork(self, n):
        assert self.at + n <= self.end
        s = Space(self.ap, self.at, n)
        self.at += n
        return s

    def rest(self):
        return Space(self.ap, self.at, self.end - self.at)


def bx(ap, axis, shape):
    return ap.unsqueeze(axis).to_broadcast(list(shape))


def build(nc, A, out, tap=None, stop=None):
    ctx = ExitStack()
    with ctx:
        def sem(name):
            return ctx.enter_context(nc.semaphore(name))

        def line(name):
            return [sem(name), 0]

        PE, V, S, G, SP = [Queue(sem(n)) for n in ("pe", "dve", "act", "pool", "sp")]
        QS = (PE, V, S, G)
        alln = 53208
        NCST = sum(CST.values())
        nlow = 19816
        nph = alln - nlow
        hT_at, wslot_at, hi_at = 728, 7528, alln - 3 * 4096
        a_at, m_at = nlow + 8192, nlow + 16384
        cuts = [0, hT_at, hT_at + 4096, wslot_at, wslot_at + 4096, wslot_at + 8192, nlow, nlow + 2048,
                *[a_at + 2048 * i for i in range(7)], hi_at, hi_at + 4096, hi_at + 8192, alln]
        with nc.sbuf_tensor("low", [P, nlow], F32) as low, nc.sbuf_tensor("high", [P, nph], F32) as high:
            pass
        rpiece = {a: ctx.enter_context(nc.sbuf_tensor(f"r{a}", [P, b - a], F32R)) for a, b in zip(cuts, cuts[1:])}

        def rview(at, *shape):
            return Space(rpiece[at][:, :], 0, int(np.prod(shape))).get(*shape)

        root = Space(low[:, :], 0, nlow)
        cst = root.get(NCST)
        C = {}
        o = 0
        for k, n in CST.items():
            C[k] = cst[:, o:o + n]
            o += n
        ident = C["ident"]
        nhalf = C["nhalf"]
        identb = root.get(64).bitcast(BF16)
        cmaskb = root.get(64).bitcast(BF16)
        hT = root.get(NJ, 512)
        gt1_2 = root.get(D)
        gt2_2 = root.get(D)
        colm = root.get(64)
        ccol = root.get(16)
        trig = root.get(9, 2, 32)
        NW = 3
        wslot = [root.get(4096) for _ in range(NW)]
        wring = Ring(NW)
        wline = [line(f"w{i}") for i in range(NW)]
        phase = Space(high[:, :], 0, nph)
        whole = phase.rest()
        assert root.at == nlow
        hTl = rview(hT_at, NJ, 512)
        wlo = [rview(wslot_at + 4096 * i, 4096) for i in range(NW)]
        hTh = rview(hi_at, NJ, 512)
        whi = [rview(hi_at + 4096 * (i + 1), 4096) for i in range(2)]
        banks = [ctx.enter_context(nc.psum_tensor(f"ps{i}", [P, 512], F32)) for i in range(8)]
        ps, po = Ring(6), Ring(2)

        class Bank:
            def __init__(self, ring=ps):
                self.ring = ring
                self.k, self.w = ring.take()
                self.ap = banks[self.k + (0 if ring is ps else 6)][:, :]

            def v(self, n, m, parts=P):
                return self.ap[0:parts, 0:n * m].rearrange("p (a b) -> p a b", a=n)

            def give(self, *toks):
                self.ring.give(self.k, *toks)

        lines = iter([line(f"d{i}") for i in range(40)])
        ldone = []

        def load(out_, in_, *toks, q=SP, ln=None):
            return q.dma(ln or next(lines), out_, in_, *toks)

        def wload(*pairs):
            k, w = wring.take()
            for view, src in pairs:
                t = SP.dma(wline[k], view(wslot[k]), src, *w)
            return k, t

        def wblock(src, n):
            k, t = wload((lambda s: s[:, 0:NJ * n].rearrange("p (j n) -> p j n", j=NJ),
                          src.rearrange("(j p) n -> p j n", p=P)))
            return k, t, wslot[k][:, 0:NJ * n].rearrange("p (j n) -> p j n", j=NJ)

        def dbg(name, ap, *toks):
            if tap is not None:
                dst = tap(name, ap)
                t = load(dst, ap, *toks, ln=line("t_" + name))
                ldone.append(t)
                for q in QS:
                    q.wait(t)

        def barrier():
            toks = [q.t for q in QS]
            for q in QS:
                q.wait(*[t for t in toks if t[0] is not q.sem])
                q.wait(q.t)
            return toks

        def pow_nhalf(ap, n, *toks):
            return G.do(lambda e: e.tensor_tensor(ap, ap, nhalf[:, 0:n], POW), *toks)

        def tt(q, out_, a, b, op, *toks):
            return q.do(lambda e: e.tensor_tensor(out_, a, b, op), *toks)

        def ts(q, out_, a, s1, s2, op0, op1, *toks):
            if op1 is None:
                return q.do(lambda e: e.tensor_scalar(out_, a, s1, None, op0), *toks)
            return q.do(lambda e: e.tensor_scalar(out_, a, s1, s2, op0, op1), *toks)

        def stt(out_, a, s, b, op0, op1, *toks):
            return V.do(lambda e: e.scalar_tensor_tensor(out=out_, in0=a, scalar=s, in1=b, op0=op0, op1=op1), *toks)

        def red(out_, a, op, *toks, negate=None):
            return V.do(lambda e: e.tensor_reduce(out_, a, AXX, op, negate=negate), *toks)

        def act(out_, a, f, *toks, **kw):
            return S.do(lambda e: e.activation(out_, a, f, **kw), *toks)

        def cp(q, out_, a, *toks):
            if q is S:
                return act(out_, a, ACT.Copy, *toks)
            return q.do(lambda e: e.tensor_copy(out_, a), *toks)

        def mm(out_, l, r, start, stop, *toks, inc=False):
            return PE.do(lambda e: e.matmul(out_, l, r, start=start, stop=stop), *toks, inc=inc)

        def tr(out_, in_, *toks, inc=False):
            n = in_.shape[0]
            return PE.do(lambda e: e.transpose(out_, in_, ident[0:n, 0:n]), *toks, inc=inc)

        t_cst = load(cst, A["cst"])
        ct = phase.get(32)
        gcols = phase.get(24 + 8 + 48 + 8 + 8)
        b1c, gp1, b2c, gp2, gp3 = (gcols[:, 0:24], gcols[:, 24:32], gcols[:, 32:80], gcols[:, 80:88], gcols[:, 88:96])
        ln0 = next(lines)
        for dst, src in ((ct[:, 0:8], A["c"]), (ct[:, 8:16], A["c_2"]), (b1c, A["b_ada_c"]), (gp1, A["g_pre"]),
                         (b2c, A["b_ada_2_c"]), (gp2, A["norm_mix_2"]), (gp3, A["norm_ffn_2"])):
            t_cols = load(dst, src, ln=ln0)
        posi = phase.get(16)
        pos = phase.get(16)
        t_pos = load(posi[:, 0:9].bitcast(I32), A["pos"])
        G1 = phase.get(D)
        ln1 = next(lines)
        load(G1, A["b_ada_r"][2 * D:3 * D].partition_broadcast(P), ln=ln1)
        load(gt1_2, A["b_ada_2_r"][2 * D:3 * D].partition_broadcast(P), ln=ln1)
        load(gt2_2, A["b_ada_2_r"][5 * D:6 * D].partition_broadcast(P), ln=ln1)
        t_rows = (ln1[0], ln1[1])

        cp(V, identb, ident, t_cst)
        t_mb = cp(V, cmaskb, C["caus"])
        act(ct[:, 16:32], ct[:, 0:16], ACT.Tanh, t_cols, scale=0.5)
        stt(ccol, ct[:, 16:32], 1.0, ct[:, 0:16], ADD, MUL, S.t)
        t_cc = ts(V, ccol, ccol, 0.5, None, MUL, None, V.t)

        def trig_tables():
            ang = phase_tmp.get(9, 32)
            kk = phase_tmp.get(9, 32)
            r = phase_tmp.get(9, 32)
            nsat = phase_tmp.get(5, 16)
            cp(V, pos[:, 0:9], posi[:, 0:9].bitcast(I32), t_pos)
            inv = C["inv"]
            tt(V, ang[:, 0:4, :], bx(pos[:, 0:4], 2, (P, 4, 32)), bx(inv[:, 0:32], 1, (P, 4, 32)), MUL, V.t)
            tt(V, ang[:, 4, 0:8], pos[:, 4:5].to_broadcast([P, 8]), inv[:, 32:40], MUL)
            tt(V, ang[:, 4, 8:16], pos[:, 4:5].to_broadcast([P, 8]), inv[:, 32:40], MUL)
            tt(V, ang[:, 4, 16:32], pos[:, 4:5].to_broadcast([P, 16]), inv[:, 40:56], MUL)
            tt(V, ang[:, 5:9, 0:16], bx(pos[:, 5:9], 2, (P, 4, 16)), bx(inv[:, 40:56], 1, (P, 4, 16)), MUL)
            tt(V, ang[:, 5:9, 16:24], bx(pos[:, 0:4], 2, (P, 4, 8)), bx(inv[:, 32:40], 1, (P, 4, 8)), MUL)
            tt(V, ang[:, 5:9, 24:32], bx(pos[:, 0:4], 2, (P, 4, 8)), bx(inv[:, 32:40], 1, (P, 4, 8)), MUL)
            pi2 = 2 * np.pi
            m1 = 6.28125
            m2 = float(np.float32(np.round((pi2 - m1) * 2 ** 21) / 2 ** 21))
            m3 = float(np.float32(pi2 - m1 - m2))
            big = 12582912.0
            for w, shift in ((0, 0.25), (1, 0.0)):
                ts(V, kk, ang, float(np.float32(1 / pi2)), shift, MUL, ADD, V.t)
                ts(V, kk, kk, big, None, ADD, None, V.t)
                ts(V, kk, kk, big, None, SUB, None, V.t)
                stt(r, kk, -m1, ang, MUL, ADD, V.t)
                stt(r, kk, -m2, r, MUL, ADD, V.t)
                stt(r, kk, -m3, r, MUL, ADD, V.t)
                if shift:
                    ts(V, r, r, float(np.pi / 2), None, ADD, None, V.t)
                ts(V, r, r, float(np.float32(3.1415925)), -float(np.float32(3.1415925)), MIN, MAX, V.t)
                act(trig[:, :, w, :], r, ACT.Sin, V.t)
                V.wait(S.t)
            return S.t

        phase_tmp = phase.rest()
        xt = phase_tmp.get(NT, D)
        t_x = load(xt, A["x"].rearrange("(t p) d -> p t d", p=P))
        t_trig = trig_tables()
        cosr = lambda k: trig[:, k, 0, :]
        sinr = lambda k: trig[:, k, 1, :]

        side = []
        side_every = [1, 0]

        def fill():
            side_every[1] += 1
            if side and side_every[1] % side_every[0] == 0:
                side.pop(0)()

        def drain_side():
            while side:
                side.pop(0)()

        def mod_cols(src, which, base, cc, halves=(0, 1)):
            for half in halves:
                k, t, w = wblock(src[:, which * D + half * 512:which * D + half * 512 + 512], 512)
                b = Bank()
                PE.wait(t, t_cc, *b.w)
                for n in range(4):
                    for j in range(NJ):
                        mm(b.ap[:, n:n + 1], w[:, j, n * P:(n + 1) * P], ccol[:, cc * 8 + j:cc * 8 + j + 1],
                           j == 0, j == NJ - 1, inc=(n == 3 and j == NJ - 1))
                wring.give(k, PE.t)
                cp(V, colm[:, base + 4 * half:base + 4 * half + 4], b.ap[:, 0:4], PE.t)
                b.give(V.t)
            return V.t

        def mod_row(src, which, dst, cc, mulrow=None, halves=(0, 1)):
            for half in halves:
                k, t, w = wblock(src[:, which * D + half * 512:which * D + half * 512 + 512], 512)
                b = Bank()
                PE.wait(t, t_scb, *b.w)
                for j in range(NJ):
                    mm(b.ap, scb[:, cc, j, :], w[:, j, :], j == 0, j == NJ - 1, inc=(j == NJ - 1))
                wring.give(k, PE.t)
                d_ = dst[:, half * 512:half * 512 + 512]
                tt(V, d_, b.ap, d_, ADD, PE.t, t_rows)
                b.give(V.t)
                if mulrow is not None:
                    tt(V, d_, d_, mulrow[:, half * 512:half * 512 + 512], MUL, V.t)
            return V.t

        def finish_cols(base, bcol, bat, gp):
            sh, sc = colm[:, base:base + 8], colm[:, base + 8:base + 16]
            tt(V, sh, sh, bcol[:, bat:bat + 8], ADD, V.t, t_cols)
            tt(V, sc, sc, bcol[:, bat + 8:bat + 16], ADD, V.t)
            return stt(sc, sc, 1.0, gp, ADD, MUL, V.t)

        mod_cols(A["w_ada"], 0, 0, 0)
        mod_cols(A["w_ada"], 1, 8, 0)
        t_col1 = finish_cols(0, b1c, 0, gp1)

        def make_hT(xt, ready, base, tcol, spare, after=()):
            xh, ss = spare
            S.wait(*ready, *after)
            V.wait(*after)
            for t_ in range(NT):
                act(xh[:, t_, :], xt[:, t_, :], ACT.Square, accum_out=ss[:, t_:t_ + 1])
            ts(V, ss[:, 4:8], ss[:, 0:4], 1.0 / D, 1e-6, MUL, ADD, S.t)
            tp = pow_nhalf(ss[:, 4:8], 4, V.t)
            xd = []
            for t_ in range(NT):
                if t_ % 2:
                    xd.append(ts(V, xh[:, t_, :], xt[:, t_, :], ss[:, 4 + t_:5 + t_], None, MUL, None, tp, S.t, *ready))
                else:
                    xd.append(act(xh[:, t_, :], xt[:, t_, :], ACT.Copy, tp, S.t, scale=ss[:, 4 + t_:5 + t_]))
            for j in range(NJ):
                b = Bank()
                PE.wait(*b.w, *xd)
                for t_ in range(NT):
                    tr(b.ap[:, t_ * P:(t_ + 1) * P], xh[:, t_, j * P:(j + 1) * P], inc=(t_ == NT - 1))
                sc, sh = colm[:, base + 8 + j:base + 9 + j], colm[:, base + j:base + j + 1]
                if j % 2:
                    act(hT[:, j, :], b.ap, ACT.Identity, PE.t, tcol, scale=sc, bias=sh)
                    b.give(S.t)
                else:
                    ts(V, hT[:, j, :], b.ap, sc, sh, MUL, ADD, PE.t, tcol)
                    b.give(V.t)
            return (S.t, V.t)

        xh1 = phase_tmp.get(NT, D)
        ss1 = phase_tmp.get(16)
        hready = make_hT(xt, (t_x,), 0, t_col1, (xh1, ss1))
        t_hT_free = None
        dbg("hT", hT, *hready)
        bt = barrier()

        ph = Space(phase.ap, phase.at, phase.end - phase.at)
        c1 = ph.get(sum(C1.values()))
        t_c1 = load(c1, A["c1"], *bt, q=G)
        K1 = {}
        o = 0
        for k, n in C1.items():
            K1[k] = c1[:, o:o + n]
            o += n
        pe_t = ph.get(2, 16)
        w2s = ph.get(2, 2, 64)
        ln2 = next(lines)
        load(pe_t[:, 0, :], A["cmp_pe_k"], *bt, q=G, ln=ln2)
        load(pe_t[:, 1, :], A["cmp_pe_v"], q=G, ln=ln2)
        load(w2s[:, 0], A["cmp_w2_k"].rearrange("(j p) n -> p j n", p=P), q=G, ln=ln2)
        t_cw = load(w2s[:, 1], A["cmp_w2_v"].rearrange("(j p) n -> p j n", p=P), q=G, ln=ln2)

        mix = ph.get(NT, D)
        nqT = ph.get(4, 512)
        gl = ph.get(NT, 24)
        vs = ph.get(2, NT, 128)
        KT = ph.get(2, 2, 512)
        kc2 = [ph.get(2, 529), ph.get(2, 529)]
        tmp = ph.get(3, 512)
        retsp = ph.rest()
        rqT = ph.get(4, 512)
        rkT = ph.get(4, 512)
        rk = ph.get(NT, 512)
        rv = ph.get(NT, 512)
        t_kz = G.do(lambda e: e.memset(kc2[0], 0.0))
        t_kz = G.do(lambda e: e.memset(kc2[1], 0.0))

        def proj(w, n, t_, b, c0=0):
            for j in range(NJ):
                mm(b.ap[:, 0:n], hT[:, j, t_ * P:(t_ + 1) * P], w[:, j, c0:c0 + n], j == 0, j == NJ - 1,
                   inc=(j == NJ - 1))
            return PE.t

        tring = Ring(3)

        def turn(src_tok, src, dst_of, evac, *w):
            b = Bank()
            PE.wait(src_tok, *b.w)
            for p in range(4):
                tr(b.ap[:, p * P:(p + 1) * P], src[:, p * P:(p + 1) * P], inc=(p == 3))
            cp(evac, dst_of, b.v(4, P), PE.t, *w)
            b.give(evac.t)
            return PE.t, evac.t

        def rope_full(b, dst, t_, tk, w):
            k2, w2 = tring.take()
            u = tmp[:, k2, :].rearrange("p (h d) -> p h d", h=H)
            s = b.v(H, 64)
            c_ = bx(cosr(t_), 1, (P, H, 32))
            s_ = bx(sinr(t_), 1, (P, H, 32))
            V.wait(tk, t_trig, *w, *w2)
            tt(V, dst[:, :, 0:32], s[:, :, 0:32], c_, MUL)
            tt(V, dst[:, :, 32:64], s[:, :, 32:64], c_, MUL)
            tt(V, u[:, :, 0:32], s[:, :, 32:64], s_, MUL)
            r = tt(V, u[:, :, 32:64], s[:, :, 0:32], s_, MUL)
            tt(G, dst[:, :, 0:32], dst[:, :, 0:32], u[:, :, 0:32], SUB, r)
            r2 = tt(G, dst[:, :, 32:64], dst[:, :, 32:64], u[:, :, 32:64], ADD)
            tring.give(k2, r2)
            return r, r2

        def rope_part(x, n, half, cosa, sina, tk, parts=P):
            k2, w2 = tring.take()
            u = tmp[0:parts, k2, 0:n * 4 * half].rearrange("p (a n h) -> p a n h", a=4, n=n)
            c_ = bx(cosa, 1, (parts, n, half))
            s_ = bx(sina, 1, (parts, n, half))
            x1, x2 = x[:, :, 0:half], x[:, :, half:2 * half]
            G.wait(tk, t_trig, *w2)
            tt(G, u[:, 0], x1, c_, MUL)
            tt(G, u[:, 1], x2, s_, MUL)
            tt(G, u[:, 2], x1, s_, MUL)
            a = tt(G, u[:, 3], x2, c_, MUL)
            tt(G, x1, u[:, 0], u[:, 1], SUB, a)
            r = tt(G, x2, u[:, 2], u[:, 3], ADD)
            tring.give(k2, r)
            return r

        rot = ph.get(2, 512)
        rring = Ring(2)

        def after_proj_rot(which):
            k, t, w = wblock(A["w_in"][:, which * 512:which * 512 + 512], 512)
            PE.wait(t, *hready, t_cst)
            pend = []
            tk_ = []
            for t_ in range(NT):
                b = Bank()
                PE.wait(*b.w)
                tk = proj(w, 512, t_, b)
                if t_ == NT - 1:
                    wring.give(k, tk)
                if which == 0:
                    k3, w3 = rring.take()
                    dst = rot[:, k3, :].rearrange("p (h d) -> p h d", h=H)
                    r, r2 = rope_full(b, dst, t_, tk, w3)
                    b.give(r)
                    pend.append((k3, rot[:, k3, :], r2, t_))
                else:
                    dst = rk[:, t_, :].rearrange("p (h d) -> p h d", h=H)
                    r, r2 = rope_full(b, dst, t_, tk, [])
                    b.give(r)
                    pend.append((None, rk[:, t_, :], r2, t_))
                while len(pend) > 1 or (pend and t_ == NT - 1):
                    k3, src, r2, tx = pend.pop(0)
                    a, b_ = turn(r2, src, (rqT if which == 0 else rkT)[:, :, tx * P:(tx + 1) * P], S)
                    if k3 is not None:
                        rring.give(k3, a)
                    tk_.append(b_)
            return tk_

        t_rq = after_proj_rot(0)
        t_rk = after_proj_rot(1)
        k, t, w = wblock(A["w_in"][:, 1024:1536], 512)
        PE.wait(t)
        t_rv = []
        for t_ in range(NT):
            b = Bank()
            PE.wait(*b.w)
            tk = proj(w, 512, t_, b)
            t_rv.append(cp(S, rv[:, t_, :], b.ap, tk))
            b.give(S.t)
        wring.give(k, tk)

        def silu2(w, off, tk_list):
            for t_ in range(NT):
                b = Bank()
                PE.wait(*b.w)
                tk = proj(w, 512, t_, b)
                k2, w2 = tring.take()
                act(tmp[:, k2, :], b.ap, ACT.Tanh, tk, *w2, scale=0.5)
                r = stt(mix[:, t_, off:off + 512], tmp[:, k2, :], 1.0, b.ap, ADD, MUL, S.t)
                b.give(r)
                tring.give(k2, r)
                tk_list.append(r)
            return tk

        k, t, w = wblock(A["w_in"][:, 1536:2048], 512)
        PE.wait(t)
        t_sg1 = []
        wring.give(k, silu2(w, 0, t_sg1))

        PTr = ph.get(2, 512)
        ptr_ring = Ring(2)
        R = ph.get(4, P)
        kz = ph.get(512)
        oo = ph.get(512)
        o2 = ph.get(512)
        st = ph.get(64)
        h3 = lambda ap: ap.rearrange("p (h d) -> p h d", h=H)

        def retention(t_, last):
            sl = slice(t_ * P, (t_ + 1) * P)
            pts = []
            for e in range(2):
                b = Bank()
                PE.wait(*b.w, t_rq[t_], t_rk[t_])
                rows = slice(64 * e, 64 * e + 64)
                for p in range(4):
                    mm(b.ap[:, p * P:(p + 1) * P], rkT[rows, p, sl], rqT[rows, p, sl], True, True, inc=(p == 3))
                k2, w2 = ptr_ring.take()
                dst = PTr[:, k2, :].rearrange("p (h i) -> p h i", h=4)
                dec = K1["dec"].rearrange("p (a e i) -> p e a i", a=4, e=2)[:, e]
                tt(V, dst, b.v(4, P), dec, MUL, PE.t, t_c1, *w2)
                b.give(V.t)
                pts.append((k2, dst, V.t))
            bi = Bank()
            PE.wait(*bi.w, t_rv[t_], *[x[2] for x in pts])
            for h in range(H):
                mm(bi.ap[:, h * 64:h * 64 + 64], pts[h % 2][1][:, h // 2, :], rv[:, t_, h * 64:h * 64 + 64],
                   True, True, inc=(h == 7))
            t_in = PE.t
            for x in pts:
                ptr_ring.give(x[0], PE.t)
            if t_ > 0:
                bc = Bank()
                PE.wait(*bc.w, last["R"])
                for p in range(4):
                    mm(bc.ap[:, p * P:(p + 1) * P], rqT[:, p, sl], R[:, p, :], True, True, inc=(p == 3))
                last["Rread"] = PE.t
                tt(V, h3(o2), bc.v(H, 64), bx(K1["xi"], 2, (P, H, 64)), MUL, PE.t, *last["o2"])
                bc.give(V.t)
                tt(V, h3(oo), bi.v(H, 64), h3(o2), ADD, V.t, t_in, *last["oo"])
            else:
                cp(V, oo, bi.ap, t_in, *last["oo"])
            bi.give(V.t)
            t_oo = V.t
            if t_ < NT - 1:
                tt(G, h3(kz), h3(rk[:, t_, :]), bx(K1["zeta"], 2, (P, H, 64)), MUL, t_rk[t_], t_c1, *last["kz"])
                bk = Bank()
                PE.wait(*bk.w, G.t)
                for p in range(4):
                    mm(bk.ap[:, p * P:(p + 1) * P], kz[:, p * P:(p + 1) * P], rv[:, t_, p * P:(p + 1) * P],
                       True, True, inc=(p == 3))
                last["kz"] = [PE.t]
                bdb = bx(C["bd"], 1, (P, 4, P))
                if t_ == 0:
                    tt(V, R, bk.v(4, P), bdb, MUL, PE.t)
                else:
                    a = tt(G, R, R, K1["cd"].rearrange("p (a b) -> p a b", a=4), MUL, last["Rread"], last["R"])
                    tt(V, o2.rearrange("p (a b) -> p a b", a=4), bk.v(4, P), bdb, MUL, PE.t, t_oo)
                    tt(V, R, R, o2.rearrange("p (a b) -> p a b", a=4), ADD, V.t, a)
                bk.give(V.t)
                last["R"] = V.t
                last["o2"] = [V.t]
            red(st[:, 0:8], h3(oo), ADD, t_oo, *last["st"])
            ts(V, st[:, 0:8], st[:, 0:8], -1.0 / 64, None, MUL, None, V.t)
            a = tt(V, h3(oo), h3(oo), bx(st[:, 0:8], 2, (P, H, 64)), ADD, V.t)
            tt(G, kq, oo, oo, MUL, a, *last["kq"])
            red(st[:, 8:16], h3(kq), ADD, G.t)
            last["kq"] = [V.t]
            ts(V, st[:, 8:16], st[:, 8:16], 4.0 / 64, 4e-5, MUL, ADD, V.t)
            b_ = pow_nhalf(st[:, 8:16], 8, V.t)
            m = mix[:, t_, 0:512]
            tt(G, h3(m), h3(m), bx(st[:, 8:16], 2, (P, H, 64)), MUL, b_, t_sg1[t_])
            tt(V, m, m, oo, MUL, G.t)
            last["oo"] = [V.t]
            last["st"] = [G.t]
            return V.t

        kq = ph.get(512)
        last = {"o2": [], "oo": [], "kz": [], "R": None, "Rread": None, "st": [], "kq": []}

        k, t, w = wblock(A["w_in"][:, 2048:2560], 512)
        PE.wait(t)
        t_nq = []
        t_mix1 = []
        for t_ in range(NT):
            b = Bank()
            PE.wait(*b.w)
            tk = proj(w, 512, t_, b)
            k3, w3 = rring.take()
            a = act(rot[:, k3, :], b.ap, ACT.Copy, tk, *w3, scale=0.125)
            b.give(a)
            r2 = rope_part(rot[:, k3, :].rearrange("p (h d) -> p h d", h=H), H, 8,
                           trig[:, 5 + t_, 0, 16:24], trig[:, 5 + t_, 1, 16:24], a)
            if t_ == NT - 1:
                wring.give(k, tk)
            t_mix1.append(retention(t_, last))
            pt_, e_ = turn(r2, rot[:, k3, :], nqT[:, :, t_ * P:(t_ + 1) * P], S)
            rring.give(k3, pt_)
            t_nq.append(e_)

        if stop == "ret":
            for t_ in range(NT):
                dbg(f"ret{t_}", mix[:, t_, 0:512], *t_mix1)

        ka, ta, wa = wblock(A["w_in"][:, 2560:3072], 512)
        kb, tb, wb = wblock(A["w_in"][:, 3072:3352], 280)
        PE.wait(ta, tb)
        kvd = ph.get(1, 4, 4, 64)
        kvr = Ring(1)
        t_kt = []
        for t_ in range(NT):
            b = Bank()
            b2 = Bank()
            PE.wait(*b.w, *b2.w)
            proj(wa, 512, t_, b)
            tk1 = PE.t
            tk = proj(wb, 280, t_, b2)
            k3, w3 = kvr.take()
            kv = kvd[:, k3]
            S.wait(tk1, *w3)
            for kind, src in ((0, b.ap[:, 0:128]), (1, b.ap[:, 128:256]), (2, b.ap[:, 256:384])):
                cp(S, kv[:, kind].rearrange("p (g u) d -> p g u d", g=2),
                   bx(src.rearrange("p (g d) -> p g d", g=2), 2, (P, 2, 2, 64)))
            cp(S, vs[:, 0, t_, :], b.ap[:, 384:512])
            b.give(S.t)
            S.wait(tk)
            cp(S, kv[:, 3].rearrange("p (g u) d -> p g u d", g=2),
               bx(b2.ap[:, 0:128].rearrange("p (g d) -> p g d", g=2), 2, (P, 2, 2, 64)))
            cp(S, vs[:, 1, t_, :], b2.ap[:, 128:256])
            act(gl[:, t_, :], b2.ap[:, 256:280], ACT.Tanh, scale=0.5)
            b2.give(S.t)
            ca, sa = trig[:, 5 + t_, 0, 16:24], trig[:, 5 + t_, 1, 16:24]
            rope_part(kv[:, 2], 4, 8, ca, sa, S.t)
            r = rope_part(kv[:, 3], 4, 8, ca, sa, S.t)
            if t_ == NT - 1:
                wring.give(ka, tk)
                wring.give(kb, tk)
            for kinds in ((0, 1), (2, 3)):
                bb = Bank()
                PE.wait(*bb.w, r)
                for x, kind in enumerate(kinds):
                    for g in range(2):
                        tr(bb.ap[:, (x * 2 + g) * P:(x * 2 + g + 1) * P],
                           kv[:, kind, 2 * g:2 * g + 2, :].rearrange("p u d -> p (u d)"), inc=(x == 1 and g == 1))
                s4 = bb.ap.rearrange("p (x g t) -> p x g t", x=2, g=2)
                if kinds[0] == 0:
                    V.wait(t_kz)
                    for x in range(2):
                        cp(V, kc2[x][0:64, :, 1 + t_ * P:1 + (t_ + 1) * P], s4[0:64, x], PE.t)
                        cp(V, kc2[x][64:128, :, t_ * P:(t_ + 1) * P], s4[64:128, x])
                    bb.give(V.t)
                else:
                    cp(S, KT[:, :, :, t_ * P:(t_ + 1) * P], s4, PE.t)
                    bb.give(S.t)
            kvr.give(k3, PE.t)
            t_kt.append((V.t, S.t))
        t_gl = ts(G, gl, gl, 1.0, None, ADD, None, S.t)
        k, t, w = wblock(A["w_in"][:, 3352:3864], 512)
        PE.wait(t)
        t_sg2 = []
        wring.give(k, silu2(w, 512, t_sg2))
        t_h1 = PE.t

        bt = barrier()
        a1 = retsp
        fl = a1.get(2048)
        flat = [fl[:, x * 1024:x * 1024 + 1024].rearrange("p (m g n) -> p m g n", m=16, g=2) for x in range(2)]
        hid = a1.get(2, 256)
        hidT = a1.get(2, 2, 64)
        hv4 = a1.get(2, 2, 4, 32)
        kcs = a1.get(2, 64)
        kcT = a1.get(64)
        vcbd = a1.get(2, 4, 64)
        ht = a1.get(256)
        ring3 = [(a1.get(512), a1.get(512)) for _ in range(3)]
        sc8 = a1.get(8, 32)
        pt8 = a1.get(2, P)
        sm = a1.get(2, 64)
        att = a1.get(NT, 512)
        au = a1.get(2, 512)
        for x in range(2):
            for g in range(2):
                for aa in range(2):
                    src = kc2[x][:, g, 1 + 16 * aa:1 + 16 * aa + 512].rearrange(
                        "p (n b two) -> p b n two", n=32, b=8, two=2)[:, :, :, 0]
                    tt(V, flat[x][:, 8 * aa:8 * aa + 8, g, :], src,
                       bx(pe_t[:, x, 8 * aa:8 * aa + 8], 2, (P, 8, 32)), ADD, t_cw)
        t_flat = V.t
        for x, nm in enumerate(("cmp_w1_k", "cmp_w1_v")):
            k, t = wload((lambda s: s.rearrange("p (m n) -> p m n", m=16),
                          A[nm].rearrange("(m p) n -> p m n", p=P)))
            w = wslot[k].rearrange("p (m n) -> p m n", m=16)
            b = Bank()
            PE.wait(t, t_flat, *b.w)
            for m in range(16):
                mm(b.ap[0:64, 0:256], flat[x][:, m].rearrange("p g n -> p (g n)"), w[:, m, :], m == 0, m == 15,
                   inc=(m == 15))
            wring.give(k, PE.t)
            act(ht[0:64, :], b.ap[0:64, 0:256], ACT.Tanh, PE.t, V.t, scale=0.5)
            r = stt(hid[0:64, x, :], ht[0:64, :], 1.0, b.ap[0:64, 0:256], ADD, MUL, S.t)
            b.give(r)
            b = Bank()
            PE.wait(r, *b.w)
            for j in range(2):
                tr(b.ap[:, j * 64:j * 64 + 64], hid[0:64, x, j * P:(j + 1) * P], inc=(j == 1))
            if x == 0:
                cp(V, hidT[:, 0], b.v(2, 64), PE.t)
            else:
                for j in range(2):
                    for g in range(2):
                        s_ = b.ap[:, j * 64 + g * 32:j * 64 + g * 32 + 32]
                        cp(V, hv4[:, j, g], bx(s_, 1, (P, 4, 32)), PE.t)
            b.give(V.t)
            b = Bank()
            PE.wait(V.t, *b.w)
            if x == 0:
                for j in range(2):
                    mm(b.ap[0:64, 0:64], hidT[:, 0, j], w2s[:, 0, j], j == 0, j == 1, inc=(j == 1))
                act(kcs[0:64], bx(b.ap[0:64, 0:64], 1, (64, 2, 64)), ACT.Copy, PE.t, scale=0.5)
                b.give(S.t)
                r = rope_part(kcs[0:64], 2, 8, trig[0:64, 4, 0, 0:8], trig[0:64, 4, 1, 0:8], S.t, 64)
                b = Bank()
                PE.wait(r, *b.w)
                tr(b.ap[:, 0:64], kcs[0:64].rearrange("p u d -> p (u d)"), inc=True)
                t_kct = cp(V, kcT, b.ap[:, 0:64], PE.t)
                b.give(V.t)
            else:
                for g in range(2):
                    for j in range(2):
                        mm(b.ap[:, g * 64:g * 64 + 64], hv4[:, j, g].rearrange("p a n -> p (a n)"), w2s[:, 1, j],
                           j == 0, j == 1, inc=(j == 1 and g == 1))
                for g in range(2):
                    t_vc = tt(V, vcbd[:, g], bx(b.ap[:, g * 64:g * 64 + 64], 1, (P, 4, 64)),
                              bx(K1["hsel"], 2, (P, 4, 64)), MUL, PE.t)
                b.give(V.t)

        def attention(t_, heads, qf, kf, vf, ob, sums, nmx, scale, ring, bufs, ready, vready):
            n = (t_ + 1) * P
            stg = [None] * len(heads)

            def scores(i):
                h = heads[i]
                b = Bank()
                PE.wait(*b.w, *ready)
                mm(b.ap[:, 0:n], qf(h), kf(h, n), True, False)
                mm(b.ap[:, t_ * P:n], identb, cmaskb, False, True, inc=True)
                kx, wx = ring.take()
                Pb, Tb = bufs[kx]
                red(nmx[:, i:i + 1], b.ap[:, 0:n], MAX, PE.t, negate=True)
                if scale != 1.0:
                    ts(V, nmx[:, i:i + 1], nmx[:, i:i + 1], scale, None, MUL, None, V.t)
                act(Pb[:, 0:n], b.ap[:, 0:n], ACT.Exp, V.t, *wx, bias=nmx[:, i:i + 1], scale=scale,
                    accum_out=sums[:, i:i + 1])
                b.give(S.t)
                stg[i] = [kx, Pb, Tb, S.t]

            def turns(i):
                kx, Pb, Tb, te = stg[i]
                b = Bank()
                PE.wait(*b.w, te)
                for kb in range(t_ + 1):
                    tr(b.ap[:, kb * P:(kb + 1) * P], Pb[:, kb * P:(kb + 1) * P], inc=(kb == t_))
                q = V if i % 2 else S
                cp(q, Tb[:, 0:n], b.ap[:, 0:n], PE.t)
                b.give(q.t)
                stg[i].append(q.t)

            def pv(i):
                kx, Pb, Tb, te, tc = stg[i]
                PE.wait(tc, *vready)
                for kb in range(t_ + 1):
                    mm(ob.ap[:, heads[i] * 64:heads[i] * 64 + 64], Tb[:, kb * P:(kb + 1) * P], vf(heads[i], kb),
                       kb == 0, kb == t_, inc=(kb == t_))
                ring.give(kx, PE.t)

            for i in range(len(heads) + 2):
                fill()
                if i < len(heads):
                    scores(i)
                if 1 <= i <= len(heads):
                    turns(i - 1)
                if i >= 2:
                    pv(i - 2)
            return PE.t

        G1b = a1.get(D)
        scb = fl.rearrange("p (a j n) -> p a j n", a=2, j=NJ)
        xt = a1.get(NT, D)
        t_rows = load(G1b, A["g_post"].partition_broadcast(P), *bt, q=G)
        t_x = load(xt, A["x"].rearrange("(t p) d -> p t d", p=P), q=G)
        t_scb = cp(V, scb, bx(ccol.rearrange("p (a j) -> p a j", a=2), 3, (P, 2, NJ, P)), V.t)
        for half in ((0,), (1,)):
            side.append(lambda half=half: mod_row(A["w_ada"], 2, G1, 0, G1b, half))
        for which, base in ((0, 16), (1, 24), (3, 32), (4, 40)):
            for half in ((0,), (1,)):
                side.append(lambda which=which, base=base, half=half: mod_cols(A["w_ada_2"], which, base, 1, half))
        for which, dst in ((2, gt1_2), (5, gt2_2)):
            for half in ((0,), (1,)):
                side.append(lambda which=which, dst=dst, half=half: mod_row(A["w_ada_2"], which, dst, 1, None, half))
        side_every[0] = 5
        aring = Ring(3)
        smr = Ring(2)
        aur = Ring(2)
        t_att = []
        sc_free = []
        for t_ in range(NT):
            sl = slice(t_ * P, (t_ + 1) * P)
            kS, wS = smr.take()
            sv = sm[:, kS, :]
            for e in range(2):
                b = Bank()
                PE.wait(*b.w, t_nq[t_], t_kct)
                rows = slice(64 * e, 64 * e + 64)
                for p in range(4):
                    g = (2 * p + e) // 4
                    mm(b.ap[:, p * 32:p * 32 + 32], nqT[rows, p, sl], kcT[rows, g * 32:g * 32 + 32], True, True,
                       inc=(p == 3))
                tt(V, sc8.rearrange("p (a e) n -> p e a n", e=2)[:, e], b.v(4, 32),
                   bx(K1["cneg"][:, t_ * 32:t_ * 32 + 32], 1, (P, 4, 32)), ADD, PE.t, *sc_free)
                b.give(V.t)
            red(sv[:, 0:8], sc8, MAX, V.t, *wS)
            tt(V, sc8, sc8, bx(sv[:, 0:8], 2, (P, 8, 32)), SUB, V.t)
            act(sc8, sc8, ACT.Exp, V.t)
            red(sv[:, 8:16], sc8, ADD, S.t)
            tt(V, sc8, sc8, bx(K1["cmul"][:, t_ * 32:t_ * 32 + 32], 1, (P, 8, 32)), MUL, V.t)
            b = Bank()
            PE.wait(*b.w, V.t)
            for g in range(2):
                tr(b.ap[:, g * P:(g + 1) * P], sc8[:, 4 * g:4 * g + 4, :].rearrange("p h n -> p (h n)"), inc=(g == 1))
            sc_free = [PE.t]
            cp(V, pt8, b.v(2, P), PE.t)
            b.give(V.t)
            ob = Bank(po)
            PE.wait(V.t, t_vc, *ob.w)
            for g in range(2):
                mm(ob.ap[:, g * 256:g * 256 + 256], pt8[:, g], vcbd[:, g].rearrange("p a d -> p (a d)"), True, True,
                   inc=(g == 1))
            V.do(lambda e, sv=sv: e.reciprocal(sv[:, 8:16], sv[:, 8:16]))
            gv = gl[:, t_, :].rearrange("p (h c) -> p h c", c=3)
            stt(sv[:, 8:16], sv[:, 8:16], 0.25, gv[:, :, 0], MUL, MUL, V.t, t_gl)
            tt(V, h3(att[:, t_, :]), ob.v(H, 64), bx(sv[:, 8:16], 2, (P, H, 64)), MUL, V.t, PE.t)
            ob.give(V.t)
            tlast = V.t
            for kind in range(2):
                ob = Bank(po)
                PE.wait(*ob.w)
                o_ = 16 + 24 * kind
                attention(
                    t_, list(range(H)),
                    lambda h: nqT[64 * (h % 2):64 * (h % 2) + 64, h // 2, sl],
                    lambda h, n: KT[64 * (h % 2):64 * (h % 2) + 64, kind, h // 4, 0:n],
                    lambda h, kb: vs[:, kind, kb, (h // 4) * 64:(h // 4) * 64 + 64],
                    ob, sv[:, o_:o_ + 8], sv[:, o_ + 8:o_ + 16], 1.0, aring, ring3,
                    [t_nq[t_], *t_kt[t_]], [])
                V.do(lambda e, sv=sv, o_=o_: e.reciprocal(sv[:, o_ + 16:o_ + 24], sv[:, o_:o_ + 8]), S.t)
                stt(sv[:, o_ + 16:o_ + 24], sv[:, o_ + 16:o_ + 24], 0.25, gv[:, :, 1 + kind], MUL, MUL, V.t)
                ka_, wa_ = aur.take()
                tt(V, h3(au[:, ka_, :]), ob.v(H, 64), bx(sv[:, o_ + 16:o_ + 24], 2, (P, H, 64)), MUL, V.t, PE.t, *wa_)
                ob.give(V.t)
                tt(G, att[:, t_, :], att[:, t_, :], au[:, ka_, :], ADD, V.t, tlast)
                tlast = G.t
                aur.give(ka_, G.t)
            smr.give(kS, V.t)
            tt(G, mix[:, t_, 512:1024], mix[:, t_, 512:1024], att[:, t_, :], MUL, G.t, t_sg2[t_])
            t_att.append(G.t)
        if tap is not None:
            dbg("mix", mix, *t_att, *t_mix1)

        drain_side()
        t_G1 = V.t
        t_col2 = finish_cols(16, b2c, 0, gp2)
        t_col3 = finish_cols(32, b2c, 24, gp3)

        def transpose_into_hT(src, n, toks):
            for j in range(n):
                b = Bank()
                PE.wait(*b.w, *toks)
                for t_ in range(NT):
                    tr(b.ap[:, t_ * P:(t_ + 1) * P], src[:, t_, j * P:(j + 1) * P], inc=(t_ == NT - 1))
                q = V if j % 2 else S
                cp(q, hT[:, j, :], b.ap, PE.t, t_h1)
                b.give(q.t)
            return (S.t, V.t)

        mtok = transpose_into_hT(mix, NJ, (*t_att, *t_mix1))
        ws = [wblock(A["w_out"][:, n * 512:n * 512 + 512], 512) for n in range(2)]
        ysp = a1.get(NT, D) if False else att
        y2 = mix
        ss2 = sm
        for t_ in range(NT):
            for n in range(2):
                k, t, w = ws[n]
                b = Bank()
                PE.wait(*b.w, t, *mtok)
                proj(w, 512, t_, b)
                act(au[:, 0, :], b.ap, ACT.Square, PE.t, V.t, G.t, accum_out=ss2[:, 0, 8 + 2 * t_ + n:9 + 2 * t_ + n])
                tt(V, y2[:, t_, n * 512:n * 512 + 512], b.ap, G1[:, n * 512:n * 512 + 512], MUL, S.t, t_G1)
                b.give(V.t)
        for n in range(2):
            wring.give(ws[n][0], PE.t)
        t_h2 = PE.t
        red(ss2[:, 0, 0:4], ss2[:, 0, 8:16].rearrange("p (t n) -> p t n", n=2), ADD, S.t, V.t)
        ts(V, ss2[:, 0, 0:4], ss2[:, 0, 0:4], 1.0 / D, 1e-6, MUL, ADD, V.t)
        tp = pow_nhalf(ss2[:, 0, 0:4], 4, V.t)
        for t_ in range(NT):
            t_x1 = stt(xt[:, t_, :], y2[:, t_, :], ss2[:, 0, t_:t_ + 1], xt[:, t_, :], MUL, ADD, tp, V.t, t_x)
        dbg("x1", xt, t_x1)
        t_xsp = load(A["xs"].rearrange("(t p) d -> p t d", p=P), xt, t_x1, q=S)

        hready = make_hT(xt, (t_x1,), 16, t_col2, (mix, sm[:, 0, :]), (V.t, t_h2))
        dbg("h2T", hT, *hready)
        bt = barrier()
        for q in QS:
            q.wait(t_xsp)
        if stop in ("b1", "ret"):
            return finish(nc, ctx, (PE, V, S, G, SP), ldone)

        ph = whole.rest()
        omla = ph.get(NT, 512)
        m2 = ph.rest()
        nrm = m2.get(2, 96)
        qan = m2.get(4)
        ln3 = next(lines)
        load(nrm[:, 0, :], A["q_norm_2"].partition_broadcast(P), *bt, t_xsp, q=G, ln=ln3)
        load(nrm[:, 1, :], A["k_norm_2"].partition_broadcast(P), q=G, ln=ln3)
        load(qan[:, 0:2], A["q_a_norm_2"], q=G, ln=ln3)
        t_nrm = load(qan[:, 2:3], A["kv_a_norm_2"], q=G, ln=ln3)
        mqT = m2.get(H, 512)
        mkT = m2.get(H, 512)
        mv = m2.get(NT, 512)
        lat = m2.get(NT, 416)
        lT = m2.get(3, 512)
        qk = m2.get(2, 2, H, 96)
        sq = m2.get(2, H, 96)
        mst = m2.get(NT, 64)
        ring3 = [(m2.get(512), m2.get(512)) for _ in range(3)]
        tmp = m2.get(3, 512)
        pst = m2.get(2, 512)
        tring = Ring(3)
        psr = Ring(2)
        k, t, w = wblock(A["w_in_2"][:, 0:416], 416)
        PE.wait(t, *hready)
        for t_ in range(NT):
            b = Bank()
            PE.wait(*b.w)
            proj(w, 416, t_, b)
            cp(S, lat[:, t_, :], b.ap[:, 0:416], PE.t)
            b.give(S.t)
        wring.give(k, PE.t)
        t_l = S.t
        for t_ in range(NT):
            act(sq.rearrange("p a h d -> p (a h d)")[:, 0:256], lat[:, t_, 0:256], ACT.Square, t_l, S.t,
                accum_out=mst[:, t_, 0:1])
            act(sq.rearrange("p a h d -> p (a h d)")[:, 256:384], lat[:, t_, 256:384], ACT.Square, S.t,
                accum_out=mst[:, t_, 1:2])
            act(sq.rearrange("p a h d -> p (a h d)")[:, 384:416], lat[:, t_, 384:416], ACT.Square, S.t,
                accum_out=mst[:, t_, 2:3])
        ts(V, mst[:, :, 0:1], mst[:, :, 0:1], 1.0 / 256, 1e-6, MUL, ADD, S.t)
        ts(V, mst[:, :, 1:2], mst[:, :, 1:2], 1.0 / 128, 1e-6, MUL, ADD)
        ts(V, mst[:, :, 2:3], mst[:, :, 2:3], 1.0 / 32, 1e-6, MUL, ADD)
        tp = G.do(lambda e: e.tensor_tensor(mst[:, :, 0:3], mst[:, :, 0:3],
                                            nhalf[:, 0:12].rearrange("p (a b) -> p a b", a=4), POW), V.t)
        for t_ in range(NT):
            ts(V, lat[:, t_, 0:256], lat[:, t_, 0:256], mst[:, t_, 0:1], None, MUL, None, tp)
            ts(V, lat[:, t_, 256:384], lat[:, t_, 256:384], mst[:, t_, 1:2], None, MUL, None)
            stt(lat[:, t_, 384:416], lat[:, t_, 384:416], mst[:, t_, 2:3], nrm[:, 1, 64:96], MUL, MUL, t_nrm)
        t_lv = V.t
        for t_ in range(NT):
            t_kr = rope_part(lat[:, t_, 384:416].unsqueeze(1), 1, 16, trig[:, 5 + t_, 0, 0:16],
                             trig[:, 5 + t_, 1, 0:16], t_lv)
        for j in range(3):
            b = Bank()
            PE.wait(*b.w, t_lv)
            for t_ in range(NT):
                tr(b.ap[:, t_ * P:(t_ + 1) * P], lat[:, t_, j * P:(j + 1) * P], inc=(t_ == NT - 1))
            ts(V, lT[:, j, :], b.ap, qan[:, j:j + 1], None, MUL, None, PE.t)
            b.give(V.t)
        t_lT = V.t
        k, t = wload((lambda s: s[:, 0:1536].rearrange("p (j n) -> p j n", j=2),
                      A["w_uq_2"].rearrange("(j p) n -> p j n", p=P)),
                     (lambda s: s[:, 1536:2560], A["w_ukv_2"]))
        wuq = wslot[k][:, 0:1536].rearrange("p (j n) -> p j n", j=2)
        wkv = wslot[k][:, 1536:2560]
        qkr = Ring(2)
        sqf = []
        t_mq = []
        for t_ in range(NT):
            sl = slice(t_ * P, (t_ + 1) * P)
            kx, wx = qkr.take()
            q_, k_ = qk[:, kx, 0], qk[:, kx, 1]
            S.wait(*wx)
            G.wait(*wx)
            V.wait(*wx)
            for n in range(2):
                b = Bank()
                PE.wait(*b.w, t_lT, t)
                for j in range(2):
                    mm(b.ap[:, 0:384], lT[:, j, sl], wuq[:, j, n * 384:(n + 1) * 384], j == 0, j == 1, inc=(j == 1))
                cp(S, q_[:, 4 * n:4 * n + 4, :], b.v(4, 96), PE.t)
                b.give(S.t)
                b = Bank()
                PE.wait(*b.w)
                mm(b.ap, lT[:, 2, sl], wkv[:, n * 512:(n + 1) * 512], True, True, inc=True)
                cp(V, k_[:, 4 * n:4 * n + 4, 0:64], b.v(4, P)[:, :, 0:64], PE.t)
                cp(V, mv[:, t_, n * 256:n * 256 + 256].rearrange("p (h d) -> p h d", h=4), b.v(4, P)[:, :, 64:128])
                b.give(V.t)
            ms = mst[:, t_, 8:32]
            tt(G, sq[:, 0], q_, q_, MUL, S.t, *sqf)
            tt(G, sq[:, 1, :, 0:64], k_[:, :, 0:64], k_[:, :, 0:64], MUL, V.t)
            red(ms[:, 0:8], sq[:, 0, :, 0:64], ADD, G.t)
            red(ms[:, 8:16], sq[:, 1, :, 0:64], ADD)
            red(ms[:, 16:24], sq[:, 0, :, 64:96], ADD)
            sqf = [V.t]
            ts(V, ms[:, 0:16], ms[:, 0:16], 1.0 / 64, 1e-6, MUL, ADD, V.t)
            ts(V, ms[:, 16:24], ms[:, 16:24], 1.0 / 32, 1e-6, MUL, ADD)
            pow_nhalf(ms, 24, V.t)
            tt(V, q_[:, :, 0:64], q_[:, :, 0:64], bx(ms[:, 0:8], 2, (P, H, 64)), MUL, G.t)
            tt(V, q_[:, :, 64:96], q_[:, :, 64:96], bx(ms[:, 16:24], 2, (P, H, 32)), MUL)
            tt(V, k_[:, :, 0:64], k_[:, :, 0:64], bx(ms[:, 8:16], 2, (P, H, 64)), MUL)
            tt(V, q_, q_, bx(nrm[:, 0, :], 1, (P, H, 96)), MUL, V.t, t_nrm)
            tq = V.t
            tt(V, k_[:, :, 0:64], k_[:, :, 0:64], bx(nrm[:, 1, 0:64], 1, (P, H, 64)), MUL)
            tk_ = V.t
            cp(G, k_[:, :, 64:96], bx(lat[:, t_, 384:416], 1, (P, H, 32)), t_kr)
            r = rope_part(q_[:, :, 64:96], H, 16, trig[:, 5 + t_, 0, 0:16], trig[:, 5 + t_, 1, 0:16], tq)
            for which, src, dst in ((0, q_, mqT), (1, k_, mkT)):
                for n in range(2):
                    b = Bank()
                    PE.wait(*b.w, r, tk_)
                    for hh in range(4):
                        tr(b.ap[0:96, hh * P:(hh + 1) * P], src[:, 4 * n + hh, :], inc=(hh == 3))
                    cp(S, dst[0:96, 4 * n:4 * n + 4, sl], b.v(4, P, 96), PE.t)
                    b.give(S.t)
            qkr.give(kx, PE.t)
            t_mq.append((S.t, V.t))
        wring.give(k, PE.t)

        psd = A["ps"]
        zrow = m2.get(RW // 16)
        G.do(lambda e: e.memset(zrow, 0.0))
        ln4 = [next(lines) for _ in range(3)]
        t_ps = [(x[0], 0) for x in ln4]
        t_ps[2] = load(psd[0:1, :].rearrange("a (p n) -> (a p) n", p=16), zrow[0:16, :], G.t, q=S, ln=ln4[2])
        pjobs = []
        for blk, (c0, n) in enumerate(((416, 512), (928, 512), (1440, 512), (1952, 256))):
            k, t, w = wblock(A["w_in_2"][:, c0:c0 + n], n)

            def job(t_, k=k, t=t, w=w, c0=c0, n=n):
                b = Bank()
                PE.wait(t, *b.w)
                proj(w, n, t_, b)
                if t_ == NT - 1:
                    wring.give(k, PE.t)
                kx, wx = psr.take()
                cp(S, pst[:, kx, 0:n], b.ap[:, 0:n], PE.t, *wx)
                b.give(S.t)
                t2 = S.dma(ln4[kx], psd[1 + t_ * P:1 + (t_ + 1) * P, c0 - 416:c0 - 416 + n], pst[:, kx, 0:n], S.t)
                psr.give(kx, t2)
                t_ps[kx] = t2
            for t_ in range(NT):
                job(t_)

        aring = Ring(3)
        SC = float(np.float32(96 ** -0.5))
        for t_ in range(NT):
            sl = slice(t_ * P, (t_ + 1) * P)
            ob = Bank(po)
            PE.wait(*ob.w)
            attention(t_, list(range(H)), lambda h: mqT[0:96, h, sl], lambda h, n: mkT[0:96, h, 0:n],
                      lambda h, kb: mv[:, kb, h * 64:h * 64 + 64], ob, mst[:, t_, 32:40], mst[:, t_, 40:48], SC,
                      aring, ring3, t_mq[t_], [])
            V.do(lambda e, t_=t_: e.reciprocal(mst[:, t_, 48:56], mst[:, t_, 32:40]), S.t)
            tt(V, h3(omla[:, t_, :]), ob.v(H, 64), bx(mst[:, t_, 48:56], 2, (P, H, 64)), MUL, V.t, PE.t)
            ob.give(V.t)
        dbg("omla", omla, V.t)
        bt = barrier()
        if stop == "mla":
            return finish(nc, ctx, (PE, V, S, G, SP), ldone)

        r2 = Space(high[:, :], NT * 512, nph - NT * 512)
        K2 = {}
        c2 = r2.get(sum(C2.values()))
        o = 0
        for kx, n in C2.items():
            K2[kx] = c2[:, o:o + n]
            o += n
        rows = r2.get(RW + 7 * 512)
        ln5 = next(lines)
        load(c2, A["c2"], *bt, *t_ps, q=G, ln=ln5)
        o = 0
        RWS = []
        for nm, n in (("mu_shift_2", RW), ("decay_base_2", 512), ("aaa_base_2", 512), ("k_k_2", 512), ("k_a_2", 512),
                      ("r_k_2", 512), ("ln_x_w_2", 512), ("ln_x_b_2", 512)):
            t_row = load(rows[:, o:o + n], A[nm].partition_broadcast(P), q=G, ln=ln5)
            RWS.append(rows[:, o:o + n])
            o += n
        mu, dbase, abase, kkw, kaw, rkw, lnw, lnb = RWS
        pp = r2.get(RW)
        pr = r2.get(RW)
        tl = [r2.get(512) for _ in range(9)]
        X1 = r2.get(4, 2, P)
        BK = r2.get(4, 2, P)
        MM = r2.get(2, 4, 4, P)
        Xb = [r2.get(4, P) for _ in range(2)]
        XTb = [r2.get(4, P) for _ in range(2)]
        T1b = [r2.get(4, P) for _ in range(2)]
        AMb = [r2.get(4, P) for _ in range(2)]
        T_ = [r2.get(4, P) for _ in range(3)]
        PCm = r2.get(2, 4, P)
        pcc = r2.get(4, 2)
        rst = r2.get(64)
        orw = [r2.get(512) for _ in range(1)]
        k, t_up = wload((lambda s: s[0:64, 0:512], A["w_decay_up_2"]), (lambda s: s[64:128, 0:512], A["w_aaa_up_2"]),
                        (lambda s: s[:, 512:1024], A["w_gate_up_2"]))
        kup = k
        wup = wslot[k]
        ln6 = next(lines)
        v4 = lambda ap: ap.rearrange("p (a b) -> p a b", a=4)
        G.do(lambda e: e.memset(T_[0], 0.0))
        t_T = G.t
        cur = 0
        c_ = 0
        orT = r2.get(4, 512) if False else None
        olist = []
        oro = A["orw"]
        for t_ in range(NT):
            bt = [q.t for q in QS]
            load(pp, psd[1 + t_ * P:1 + (t_ + 1) * P, :], *bt, *t_ps, q=S, ln=ln6)
            t_in = load(pr, psd[t_ * P:(t_ + 1) * P, :], q=S, ln=ln6)
            tt(G, pr, pr, pp, SUB, t_in)
            tt(V, pr, pr, mu, MUL, G.t, t_row)
            tt(G, pr, pr, pp, ADD, V.t)
            t_p = G.t
            r_, k_, v_ = pr[:, 0:512], pr[:, 512:1024], pr[:, 1024:1536]
            wd, gd = pr[:, 1536:1600], pr[:, 1664:1792]
            act(wd, wd, ACT.Tanh, t_p)
            act(gd, gd, ACT.Tanh, scale=0.5)
            ts(V, gd, gd, 0.5, 0.5, MUL, ADD, S.t)
            b = Bank()
            PE.wait(*b.w, V.t, t_p)
            for j in range(2):
                tr(b.ap[:, j * P:(j + 1) * P], pr[:, 1536 + j * P:1536 + (j + 1) * P], inc=(j == 1))
            loT = pp[:, 0:256].rearrange("p (a b) -> p a b", a=2)
            cp(V, loT, b.v(2, P), PE.t)
            b.give(V.t)
            b0, b1, b2 = Bank(), Bank(), Bank()
            PE.wait(*b0.w, *b1.w, *b2.w, V.t, t_up)
            mm(b0.ap, loT[0:64, 0], wup[0:64, 0:512], True, True, inc=True)
            mm(b1.ap, loT[64:128, 0], wup[64:128, 0:512], True, True, inc=True)
            mm(b2.ap, loT[:, 1], wup[:, 512:1024], True, True, inc=True)
            if t_ == NT - 1:
                wring.give(kup, PE.t)
            L, a_, g_, kk, kh, e1, e2, bt_, y_ = tl
            tt(V, L, b0.ap, dbase, ADD, PE.t, t_row)
            b0.give(V.t)
            tt(V, a_, b1.ap, abase, ADD)
            b1.give(V.t)
            cp(S, g_, b2.ap, PE.t)
            b2.give(S.t)
            act(L, L, ACT.Tanh, V.t, scale=0.5)
            act(a_, a_, ACT.Tanh, scale=0.5)
            ts(V, L, L, -0.5 * EM05, -0.5 * EM05, MUL, ADD, S.t)
            t_L = V.t
            bc = Bank()
            PE.wait(*bc.w, t_L)
            mm(bc.ap, K2["tri"], L, True, True, inc=True)
            t_cum = PE.t
            bp = Bank()
            PE.wait(*bp.w)
            for p in range(4):
                mm(bp.ap[:, 2 * p:2 * p + 2], L[:, p * P:(p + 1) * P], K2["sel"], True, True, inc=(p == 3))
            t_pc = PE.t
            ts(V, a_, a_, 0.5, 0.5, MUL, ADD)
            tt(V, kk, k_, kkw, MUL, t_row, t_p)
            tt(G, e1, kk, kk, MUL, V.t)
            red(rst[:, 0:8], h3(e1), ADD, G.t)
            ts(V, rst[:, 0:8], rst[:, 0:8], 1e-24, None, MAX, None, V.t)
            pow_nhalf(rst[:, 0:8], 8, V.t)
            tt(V, h3(kk), h3(kk), bx(rst[:, 0:8], 2, (P, H, 64)), MUL, G.t)
            t_kk = V.t
            stt(bt_, kk, -1.0, a_, MUL, MUL, V.t)
            stt(kh, a_, -1.0, kaw, ADD, MUL, V.t)
            stt(kh, kh, 1.0, k_, ADD, MUL, V.t)
            t_kh = V.t
            tt(V, e2, r_, kh, MUL, V.t)
            tt(V, e2, e2, rkw, MUL, V.t)
            red(rst[:, 8:16], h3(e2), ADD, V.t)
            t_e2 = V.t
            act(e1, bc.ap, ACT.Exp, t_cum, V.t)
            tt(V, r_, r_, e1, MUL, S.t)
            t_Rp = V.t
            act(e1, bc.ap, ACT.Exp, V.t, scale=-1.0)
            tt(V, L, bc.ap, L, SUB, S.t, t_pc)
            bc.give(V.t)
            act(e2, L, ACT.Exp, V.t)
            act(pcc, bp.v(4, 2), ACT.Exp, t_pc)
            bp.give(S.t)
            tt(V, kk, kk, e2, MUL, S.t)
            tt(V, kh, kh, e1, MUL)
            tt(V, bt_, bt_, e1, MUL)
            t_all = V.t
            for c in range(2):
                tt(G, PCm[:, c], bx(C["bd"], 1, (P, 4, P)), bx(pcc[:, :, c], 2, (P, 4, P)), MUL, S.t)
            t_PC = G.t
            for n, (src, dst) in enumerate(((kk, X1[:, :, 0]), (r_, X1[:, :, 1]), (bt_, BK[:, :, 0]), (kh, BK[:, :, 1]))):
                turn(t_all, src, dst, V if n % 2 else S)
            t_X = (V.t, S.t)
            mk = bx(K2["mm"], 1, (P, 2, 256))
            for e in range(2):
                rw = slice(64 * e, 64 * e + 64)
                for p in range(4):
                    b = Bank()
                    PE.wait(*b.w, *t_X)
                    x1 = X1[rw, p].rearrange("p a b -> p (a b)")
                    mm(b.ap[:, 0:256], BK[rw, p, 0, :], x1, True, True)
                    mm(b.ap[:, 256:512], BK[rw, p, 1, :], x1, True, True, inc=True)
                    tt(V, MM[:, e, p].rearrange("p (a b) c -> p a (b c)", a=2), b.v(2, 256), mk, MUL, PE.t)
                    b.give(V.t)
            t_MM = V.t
            for e in range(2):
                rw = slice(64 * e, 64 * e + 64)
                b = Bank()
                PE.wait(*b.w)
                for p in range(4):
                    mm(b.ap[:, p * P:(p + 1) * P], X1[rw, p, 0, :], BK[rw, p, 0, :], True, True, inc=(p == 3))
                tt(V, Xb[e], b.v(4, P), bx(K2["m1"], 1, (P, 4, P)), MUL, PE.t)
                b.give(V.t)
                tt(V, Xb[e], Xb[e], bx(ident, 1, (P, 4, P)), ADD, V.t)
                tt(G, XTb[e], MM[:, e, :, 0, :], bx(K2["mt"][:, 0:P], 1, (P, 4, P)), MUL, t_MM)
                tt(G, XTb[e], XTb[e], bx(ident, 1, (P, 4, P)), ADD, G.t)
            xt_t = [[V.t, G.t], [V.t, G.t]]
            am_w = [[], []]
            for l in range(1, 6):
                am = []
                for e in range(2):
                    am.append(tt(G, AMb[e], MM[:, e, :, 0, :], bx(K2["mt"][:, l * P:(l + 1) * P], 1, (P, 4, P)), MUL,
                                 *am_w[e]))
                t1 = []
                for e in range(2):
                    b = Bank()
                    PE.wait(*b.w, am[e], *xt_t[e])
                    for p in range(4):
                        mm(b.ap[:, p * P:(p + 1) * P], AMb[e][:, p], Xb[e][:, p], True, True, inc=(p == 3))
                    am_w[e] = [PE.t]
                    cp(S, T1b[e], b.v(4, P), PE.t)
                    b.give(S.t)
                    t1.append(S.t)
                for e in range(2):
                    ba = Bank() if l < 5 else None
                    bb = Bank()
                    PE.wait(*bb.w, t1[e])
                    if ba:
                        PE.wait(*ba.w)
                        for p in range(4):
                            mm(ba.ap[:, p * P:(p + 1) * P], XTb[e][:, p], T1b[e][:, p], True, True, inc=(p == 3))
                    for p in range(4):
                        mm(bb.ap[:, p * P:(p + 1) * P], T1b[e][:, p], XTb[e][:, p], True, True, inc=(p == 3))
                    if ba:
                        tt(V, Xb[e], Xb[e], ba.v(4, P), ADD, PE.t)
                        ba.give(V.t)
                    tt(V, XTb[e], XTb[e], bb.v(4, P), ADD, PE.t)
                    bb.give(V.t)
                    xt_t[e] = [V.t]
            BV, U, WT, SA = T1b[0].rearrange("p a b -> p (a b)"), T1b[1].rearrange("p a b -> p (a b)"), \
                AMb[0], AMb[1].rearrange("p a b -> p (a b)")
            hs = lambda h: slice(h * 64, h * 64 + 64)
            b = Bank()
            PE.wait(*b.w, V.t, t_p)
            for h in range(H):
                mm(b.ap[:, hs(h)], MM[:, h % 2, h // 2, 2, :], v_[:, hs(h)], True, True, inc=(h == 7))
            cp(S, BV, b.ap, PE.t)
            b.give(S.t)
            b = Bank()
            PE.wait(*b.w, S.t)
            for h in range(H):
                mm(b.ap[:, hs(h)], XTb[h % 2][:, h // 2], BV[:, hs(h)], True, True, inc=(h == 7))
            cp(S, U, b.ap, PE.t)
            b.give(S.t)
            t_U = S.t
            b = Bank()
            PE.wait(*b.w)
            for e in range(2):
                for p in range(4):
                    h = 2 * p + e
                    mm(b.ap[64 * e:64 * e + 64, p * P:(p + 1) * P], kk[:, hs(h)], XTb[e][:, p], True, True,
                       inc=(e == 1 and p == 3))
            cp(S, WT, b.v(4, P), PE.t)
            b.give(S.t)
            t_WT = S.t
            by = Bank(po)
            for c in range(2):
                rw = slice(64 * c, 64 * c + 64)
                Tc, Tn = T_[cur], T_[(cur + 1) % 3]
                b = Bank()
                PE.wait(*b.w, t_WT, t_T)
                for p in range(4):
                    mm(b.ap[rw, p * P:(p + 1) * P], WT[:, p, rw], Tc[:, p], True, True, inc=(p == 3))
                tt(V, SA[rw, :], b.ap[rw, :], U[rw, :], ADD, PE.t, t_U)
                b.give(V.t)
                t_sa = V.t
                b = Bank()
                PE.wait(*b.w, *by.w, t_sa)
                for p in range(4):
                    mm(by.ap[rw, p * P:(p + 1) * P], X1[:, p, 1, rw], Tc[:, p], True, True, inc=(p == 3))
                t_by = PE.t
                for p in range(4):
                    cs = slice(p * P, (p + 1) * P)
                    mm(b.ap[:, cs], kh[rw, cs], v_[rw, cs], True, False)
                    mm(b.ap[:, cs], bt_[rw, cs], SA[rw, cs], False, True, inc=(p == 3))
                tt(V, Tn, Tc, b.v(4, P), ADD, PE.t)
                b.give(V.t)
                tt(V, Tn, Tn, PCm[:, c], MUL, V.t, t_PC)
                t_T = V.t
                cur = (cur + 1) % 3
            b = Bank()
            PE.wait(*b.w, t_sa)
            for h in range(H):
                mm(b.ap[:, hs(h)], MM[:, h % 2, h // 2, 1, :], SA[:, hs(h)], True, False)
                mm(b.ap[:, hs(h)], MM[:, h % 2, h // 2, 3, :], v_[:, hs(h)], False, True, inc=(h == 7))
            cp(S, y_, by.ap, t_by)
            by.give(S.t)
            tt(V, y_, y_, b.ap, ADD, PE.t, S.t)
            b.give(V.t)
            red(rst[:, 16:24], h3(y_), ADD, V.t)
            ts(V, rst[:, 16:24], rst[:, 16:24], -1.0 / 64, None, MUL, None, V.t)
            tt(V, h3(y_), h3(y_), bx(rst[:, 16:24], 2, (P, H, 64)), ADD, V.t)
            tt(G, e1, y_, y_, MUL, V.t)
            red(rst[:, 24:32], h3(e1), ADD, G.t)
            ts(V, rst[:, 24:32], rst[:, 24:32], 1.0 / 64, 64e-5, MUL, ADD, V.t)
            pow_nhalf(rst[:, 24:32], 8, V.t)
            tt(V, h3(y_), h3(y_), bx(rst[:, 24:32], 2, (P, H, 64)), MUL, G.t)
            tt(V, y_, y_, lnw, MUL, V.t)
            tt(V, y_, y_, lnb, ADD, V.t)
            tt(G, h3(v_), h3(v_), bx(rst[:, 8:16], 2, (P, H, 64)), MUL, PE.t, V.t)
            tt(V, y_, y_, v_, ADD, G.t)
            tt(V, y_, y_, g_, MUL, V.t)
            if tap is not None:
                dbg(f"y{t_}", y_, V.t)
            t_o = load(oro[t_ * P:(t_ + 1) * P, :], y_, V.t, q=S, ln=ln6)
            for q in QS:
                q.wait(t_o)
        bt = barrier()
        if stop == "rwkv":
            return finish(nc, ctx, (PE, V, S, G, SP), ldone)

        def split_ops(raw, hi, lo, toks, hi_toks, q):
            a = act(hi, raw, ACT.Copy, *toks, *hi_toks)
            return tt(q, lo, raw, hi.bitcast(F32), SUB, a)

        hring = Ring(2)
        loq = [V]

        class Stream:
            def __init__(self, srcs):
                self.srcs, self.loaded, self.split, self.at = srcs, [], [], 0

            def load_to(self, n):
                while len(self.loaded) < min(n, len(self.srcs)):
                    src = self.srcs[len(self.loaded)]
                    if len(src.shape) == 3:
                        self.loaded.append(wload((lambda s: s.rearrange("p (j n) -> p j n", j=src.shape[1]), src)))
                    else:
                        self.loaded.append(wload((lambda s: s, src)))

            def split_to(self, n):
                while len(self.split) < min(n, len(self.srcs)):
                    k, t = self.loaded[len(self.split)]
                    kh, wh = hring.take()
                    r = []
                    for o in range(0, 4096, 1024):
                        c = slice(o, o + 1024)
                        r.append(split_ops(wslot[k][:, c], whi[kh][:, c], wlo[k][:, c], [t], wh, loq[0]))
                    self.split.append((k, kh, r))

            def enter(self):
                self.load_to(self.at + 2)
                self.split_to(self.at + 1)
                self.load_to(self.at + 3)
                self.split_to(self.at + 2)
                k, kh, r = self.split[self.at]
                self.at += 1
                self.cur = (k, kh)
                return whi[kh], wlo[k], r

            def leave(self, *cur):
                k, kh = cur
                wring.give(k, PE.t)
                hring.give(kh, PE.t)

        def mm3(out_, lh, ll, rh, rl, start, stop, inc=False):
            mm(out_, lh, rh, start, False)
            mm(out_, lh, rl, False, False)
            mm(out_, ll, rh, False, stop, inc=inc)

        srcs = [A[n].rearrange("(j p) n -> p j n", p=P) for n in ("w_o_mla_2", "w_o_rwkv_2")]
        srcs += [A["w_in_2"][:, 2208 + n * 512:2720 + n * 512].rearrange("(j p) n -> p j n", p=P) for n in range(4)]
        srcs += [A["w_out_2"][:, n * 512:n * 512 + 512].rearrange("(j p) n -> p j n", p=P) for n in range(2)]
        srcs += [A["w_query_2"][:, n * 512:n * 512 + 512].rearrange("(j p) n -> p j n", p=P) for n in range(4)]
        srcs += [A["down"][u] for u in range(NE_)]
        for i in range(NU - NE_):
            srcs += [A["down"][NE_ + i]]
            srcs += [A["up"][i]]
            srcs += [A["up"][NE_ + i]]
        ws_ = Stream(srcs)

        def jn(ap):
            return ap.rearrange("p (j n) -> p j n", j=NJ)

        def up_chunk(wh, wl, m, ht=()):
            b = Bank()
            PE.wait(*b.w)
            for j in range(NJ):
                if ht:
                    PE.wait(ht[j])
                c = slice(m * P, (m + 1) * P)
                mm3(b.ap, wh[:, j, c], wl[:, j, c], hTh[:, j, :], hTl[:, j, :], j == 0, j == NJ - 1,
                    inc=(j == NJ - 1))
            return b

        def jn(ap):
            return ap.rearrange("p (j n) -> p j n", j=NJ)

        def jproj(wh, wl, t_, lh, ll, n, ht=()):
            b = Bank()
            PE.wait(*b.w)
            c = slice(t_ * P, (t_ + 1) * P)
            for j in range(n):
                if ht:
                    PE.wait(ht[j])
                mm3(b.ap, lh[:, j, c], ll[:, j, c], wh[:, j, :], wl[:, j, :], j == 0, j == n - 1, inc=(j == n - 1))
            return b

        ph = Space(high[:, :], NT * 512, hi_at - nlow - NT * 512)
        xt = ph.get(NT, D)
        mix = ph.get(NT, D)
        orr = ph.get(NT, 512)
        assert ph.at == a_at - nlow + 4096
        oT = [ph.get(4, 512) for _ in range(2)]
        oTl = [rview(a_at + 4096 + 2048 * i, 4, 512) for i in range(2)]
        oTh = [rview(nlow, 4, 512), rview(a_at + 2048, 4, 512)]
        tg = ph.get(2, 512)
        ss3 = ph.get(16)
        t_or = load(orr, oro.rearrange("(t p) d -> p t d", p=P), *bt, q=G, ln=next(lines))
        ws_.load_to(3)
        ot = [[], []]
        for which, src, w_ in ((0, omla, ()), (1, orr, (t_or,))):
            tk = []
            for j in range(4):
                b = Bank()
                PE.wait(*b.w, *w_)
                for t_ in range(NT):
                    tr(b.ap[:, t_ * P:(t_ + 1) * P], src[:, t_, j * P:(j + 1) * P], inc=(t_ == NT - 1))
                q = V if j % 2 else S
                tk.append(cp(q, oT[which][:, j, :], b.ap, PE.t))
                b.give(q.t)
            for j in range(4):
                ot[which].append(split_ops(oT[which][:, j, :], oTh[which][:, j, :], oTl[which][:, j, :],
                                           [tk[j], PE.t], (), V))
            if which == 0:
                ws_.split_to(1)
        ht = [split_ops(hT[:, j, :], hTh[:, j, :], hTl[:, j, :], (), (), V) for j in range(NJ)]
        for which in range(2):
            wh, wl, r = ws_.enter()
            cur = ws_.cur
            PE.wait(*r, *ot[which])
            wh, wl = [x.rearrange("p (j n) -> p j n", j=4) for x in (wh, wl)]
            for n in range(2):
                nc_ = slice(n * 512, n * 512 + 512)
                for t_ in range(NT):
                    b = jproj(wh[:, :, nc_], wl[:, :, nc_], t_, oTh[which], oTl[which], 4)
                    q = S if t_ % 2 else V
                    cp(q, (mix, xt)[which][:, t_, nc_], b.ap, PE.t)
                    b.give(q.t)
            ws_.leave(*cur)
        t_z = (S.t, V.t)
        gring = Ring(2)
        for which in range(2):
            for n in range(2):
                wh, wl, r = ws_.enter()
                cur = ws_.cur
                PE.wait(*r, *ht)
                nc_ = slice(n * 512, n * 512 + 512)
                for t_ in range(NT):
                    b = jproj(jn(wh), jn(wl), t_, hTh, hTl, NJ)
                    kx, wx = gring.take()
                    act(tg[:, kx, :], b.ap, ACT.Tanh, PE.t, *wx, scale=0.5)
                    b.give(S.t)
                    dst = mix[:, t_, nc_]
                    if which == 0:
                        stt(dst, tg[:, kx, :], 1.0, dst, ADD, MUL, S.t, *t_z)
                        gring.give(kx, V.t)
                    else:
                        stt(tg[:, kx, :], tg[:, kx, :], 1.0, xt[:, t_, nc_], ADD, MUL, S.t)
                        tt(G, dst, dst, tg[:, kx, :], ADD, V.t)
                        gring.give(kx, G.t)
                ws_.leave(*cur)
        t_x2 = load(xt, A["xs"].rearrange("(t p) d -> p t d", p=P), V.t, G.t, q=G, ln=next(lines))
        t_h1 = PE.t
        mtok = transpose_into_hT(mix, NJ, (G.t, V.t))
        ht = [split_ops(hT[:, j, :], hTh[:, j, :], hTl[:, j, :], mtok, (t_h1,), V) for j in range(NJ)]
        x3t = []
        for n in range(2):
            wh, wl, r = ws_.enter()
            cur = ws_.cur
            PE.wait(*r)
            nc_ = slice(n * 512, n * 512 + 512)
            for t_ in range(NT):
                b = jproj(jn(wh), jn(wl), t_, hTh, hTl, NJ, ht if n == t_ == 0 else ())
                stt(mix[:, t_, nc_], b.ap, 0.5, gt1_2[:, nc_], MUL, MUL, PE.t)
                b.give(V.t)
                tt(G, xt[:, t_, nc_], xt[:, t_, nc_], mix[:, t_, nc_], ADD, V.t, t_x2)
            ws_.leave(*cur)
        t_x3 = G.t
        dbg("x2", xt, t_x3)
        hready = make_hT(xt, (t_x3,), 32, t_col3, (mix, ss3), (G.t, PE.t))
        dbg("h3T", hT, *hready)
        bt = barrier()
        t_xsp = load(A["xs"].rearrange("(t p) d -> p t d", p=P), xt, *bt, q=S, ln=next(lines))
        for q in QS:
            q.wait(t_xsp)

        ph = Space(high[:, :], 0, hi_at - nlow)
        loq[0] = G
        hkT = ph.get(3, 512)
        ust = [ph.get(512) for _ in range(2)]
        early0 = ph.at
        early = ph.rest()

        ht = [split_ops(hT[:, j, :], hTh[:, j, :], hTl[:, j, :], hready, (), V) for j in range(NJ)]
        sk = early.get(2, P)
        qT = early.get(16, 512)
        ln8 = next(lines)
        load(sk[:, 0, :], A["sub_keys1_2"], *bt, t_xsp, q=G, ln=ln8)
        t_sk = load(sk[:, 1, :], A["sub_keys2_2"], q=G, ln=ln8)

        for n in range(4):
            wh, wl, r = ws_.enter()
            cur = ws_.cur
            PE.wait(*r)
            for m in range(4):
                b = up_chunk(jn(wh), jn(wl), m, ht if n == m == 0 else ())
                cp(S, qT[:, 4 * n + m, :], b.ap, PE.t)
                b.give(S.t)
            ws_.leave(*cur)
        t_qT = S.t

        usr = Ring(2)
        lnu = [line(f"u{i}") for i in range(2)]
        st_ = {}

        def early_piece(u, m):
            if m == 0:
                wh, wl, r = ws_.enter()
                PE.wait(*r)
                st_["w"] = (jn(wh), jn(wl), ws_.cur)
            wh, wl, cur = st_["w"]
            b = up_chunk(wh, wl, m)
            if m == 3:
                ws_.leave(*cur)
            kx, wx = usr.take()
            act(ust[kx], b.ap, ACT.Gelu_apprx_tanh, PE.t, *wx)
            b.give(S.t)
            t = load(A["au"][u][:, m * 512:m * 512 + 512], ust[kx], S.t, ln=lnu[kx])
            usr.give(kx, t)

        for u in range(NE_):
            for m in range(4):
                side.append(lambda u=u, m=m: early_piece(u, m))
        side_every[0] = 1
        sb_ = early.get(2, 16, P)
        sbr = Ring(2)
        v16 = early.get(16, 16)
        i16 = early.get(16, 16).bitcast(U32)
        if16 = early.get(16, 16)
        cand = early.get(H, 256)
        cv = early.get(H, 16)
        ci = early.get(H, 16).bitcast(U32)
        cif = early.get(4, H, 16)
        eq = cand.rearrange("p h (a b) -> p h a b", a=16)
        e3 = early.get(3, P)
        NEGF = -3.0e38
        s_free = []

        def top16(n, src, vals, idx):
            def mx(m, o):
                s_, v_ = src(m), vals(m)[:, o:o + 8]
                return V.do(lambda e: e.max(v_, s_), tk[m])

            def ix(m, o):
                s_, v_, i_ = src(m), vals(m)[:, o:o + 8], idx(m)[:, o:o + 8]
                return V.do(lambda e: e.max_index(i_, v_, s_), tk[m])

            def rp(m, o):
                s_, v_ = src(m), vals(m)[:, 0:8]
                return V.do(lambda e: e.match_replace(s_, v_, s_, NEGF), tk[m])

            tk = [V.t] * n
            for f, o in ((mx, 0), (ix, 0), (rp, 0), (mx, 8), (ix, 8)):
                tk = [f(m, o) for m in range(n)]
                fill()

        def scores(t_):
            kx, wx = sbr.take()
            sc = sb_[:, kx]
            for n in range(4):
                b = Bank()
                PE.wait(*b.w, t_qT, t_sk)
                for m in range(4):
                    mm(b.ap[:, m * P:(m + 1) * P], qT[:, 4 * n + m, t_ * P:(t_ + 1) * P], sk[:, m % 2, :], True, True,
                       inc=(m == 3))
                cp(S, sc[:, 4 * n:4 * n + 4, :], b.v(4, P), PE.t, *wx)
                b.give(S.t)
            return kx, S.t

        nxt_sc = scores(0)
        for t_ in range(NT):
            kx, t_sc = nxt_sc
            sc = sb_[:, kx]
            if t_ + 1 < NT:
                nxt_sc = scores(t_ + 1)
            fill()
            V.wait(t_sc)
            top16(16, lambda m: sc[:, m, :], lambda m: v16[:, m, :], lambda m: i16[:, m, :])
            sbr.give(kx, V.t)
            cp(V, if16, i16, V.t)
            vv = v16.rearrange("p (h w) k -> p h w k", w=2)
            ii = if16.rearrange("p (h w) k -> p h w k", w=2)
            tcd = V.t
            for h in range(H):
                cd = cand[:, h, :].rearrange("p (a b) -> p a b", a=16)
                tt(V, cd, bx(vv[:, h, 0], 2, (P, 16, 16)), bx(vv[:, h, 1], 1, (P, 16, 16)), ADD, tcd)
            top16(8, lambda h: cand[:, h, :], lambda h: cv[:, h, :], lambda h: ci[:, h, :])
            cu = cif[:, 3].bitcast(U32)
            V.do(lambda e: e.tensor_scalar(cu, ci, 4, None, ALU.logical_shift_right), V.t)
            cp(V, cif[:, 0], cu, V.t)
            V.do(lambda e: e.tensor_scalar(cu, ci, 15, None, ALU.bitwise_and), V.t)
            cp(V, cif[:, 1], cu, V.t)
            io = C["iota"][:, 0:16]
            for w_ in range(2):
                te0 = V.t
                te = [tt(V, eq[:, h], bx(cif[:, w_, h], 2, (P, 16, 16)), bx(io, 1, (P, 16, 16)), EQ, te0)
                      for h in range(H)]
                for h in range(H):
                    tt(V, eq[:, h], eq[:, h], bx(ii[:, h, w_], 1, (P, 16, 16)), MUL, te[h])
                red(e3[:, w_, :].rearrange("p (h k) -> p h k", h=H), eq, ADD, V.t, *s_free)
                fill()
            cpm = cif[:, 2, :, 0]
            cp(V, cpm, cv[:, :, 0], V.t)
            tt(V, cv, cv, bx(cpm, 2, (P, H, 16)), SUB, V.t)
            act(cv, cv, ACT.Exp, V.t)
            red(cpm, cv, ADD, S.t)
            V.do(lambda e: e.reciprocal(cpm, cpm), V.t)
            tt(V, e3[:, 2, :].rearrange("p (h k) -> p h k", h=H), cv, bx(cpm, 2, (P, H, 16)), MUL, V.t)
            b = Bank()
            PE.wait(*b.w, V.t)
            for w_ in range(3):
                tr(b.ap[:, w_ * P:(w_ + 1) * P], e3[:, w_, :], inc=(w_ == 2))
            s_free = [PE.t]
            cp(S, hkT[:, :, t_ * P:(t_ + 1) * P], b.ap[:, 0:384].rearrange("p (a b) -> p a b", a=3), PE.t)
            b.give(S.t)

        bt = barrier()
        TB = 64
        ls = Space(high[:, :], early0, hi_at - nlow - early0)
        stg = [ls.get(P, TB) for _ in range(2)]
        oh = [ls.get(2, 4, P) for _ in range(2)]
        ohr = Ring(2)
        stgr = Ring(2)
        loq[0] = V
        gd_ = A["gd"]
        lng = [line("g2"), line("g3")]
        iota = C["iota"]
        qi = 0
        for tb in range(512 // TB):
            ks, wst = stgr.take()
            for q4 in range(TB // 4):
                qi += 1
                if qi % 8 == 3 and side:
                    side.pop(0)()
                b = Bank()
                PE.wait(*b.w)
                tok = tb * TB + q4 * 4
                kx, wx = ohr.take()
                o1, o2_ = oh[kx][:, 0], oh[kx][:, 1]
                a = tt(V, oh[kx], bx(bx(iota, 1, (P, 4, P)), 1, (P, 2, 4, P)),
                       bx(hkT[:, 0:2, tok:tok + 4], 3, (P, 2, 4, P)), EQ, *wx)
                c = tt(G, o1, o1, bx(hkT[:, 2, tok:tok + 4], 2, (P, 4, P)), MUL, a)
                PE.wait(c)
                for u in range(4):
                    mm(b.ap[:, u * P:(u + 1) * P], o2_[:, u], o1[:, u], True, True, inc=(u == 3))
                ohr.give(kx, PE.t)
                src = b.v(4, P).rearrange("p u a -> p a u")
                cp(S, stg[ks][:, :, q4 * 4:q4 * 4 + 4], src, PE.t, *wst)
                b.give(S.t)
            t_g = S.dma(lng[tb % 2], gd_[tb].rearrange("b a t -> b (a t)"), stg[ks].rearrange("p a t -> p (a t)"), S.t)
            stgr.give(ks, t_g)
        drain_side()
        t_gd = [(l[0], l[1]) for l in (*lng, *lnu)]
        for q in (V, G, S, SP):
            q.wait(*t_gd)
        bt = [q.t for q in QS]
        SP.wait(*bt)
        V.wait(*bt)
        G.wait(*bt)
        S.wait(*bt)

        ls = Space(high[:, :], 0, hi_at - nlow)
        Y = ls.get(NT, D)
        Gb = [ls.get(8, 4, TB) for _ in range(2)]
        NA = 4
        assert ls.at == a_at - nlow
        Ab = [ls.get(4, 512) for _ in range(NA)]
        Al = [rview(a_at + 2048 * i, 4, 512) for i in range(NA)]
        assert ls.at == m_at - nlow
        Ah = [rview(m_at + 2048 * i, 4, 512) for i in range(2)]
        Aring, mring, gring = Ring(NA), Ring(2), Ring(2)
        gline = [line("g0"), line("g1")]
        aline = [line(f"a{i}") for i in range(NA)]
        where, mtok_, gload, ytok = {}, {}, {}, {}

        def fetch(u):
            kg, wg = gring.take()
            gload[u] = (kg, G.dma(gline[kg], Gb[kg].rearrange("p b a t -> p b (a t)"),
                                  gd_[:, :, 4 * u:4 * u + 4, :].rearrange("b p a t -> p b (a t)"), *wg))
            if u < NE_:
                ka_, wa = Aring.take()
                where[u] = (ka_, [G.dma(aline[ka_], Ab[ka_].rearrange("p m t -> p (m t)"), A["au"][u], *wa)] * 4)

        def compute(u):
            wh, wl, r = ws_.enter()
            cur = ws_.cur
            ka_, wa = Aring.take()
            toks = []
            PE.wait(*r)
            for m in range(4):
                b = up_chunk(jn(wh), jn(wl), m)
                toks.append(act(Ab[ka_][:, m, :], b.ap, ACT.Gelu_apprx_tanh, PE.t, *wa))
                b.give(S.t)
            ws_.leave(*cur)
            where[u] = (ka_, toks)

        def gates(u):
            kg, t = gload[u]
            ka_, toks = where[u]
            km, wm = mring.take()
            r = []
            for m in range(4):
                a = Ab[ka_][:, m, :].rearrange("p (b t) -> p b t", b=8)
                x = tt(V, a, a, Gb[kg][:, :, m, :], MUL, t, toks[m])
                r.append(split_ops(Ab[ka_][:, m, :], Ah[km][:, m, :], Al[ka_][:, m, :], [x], wm, V))
            gring.give(kg, V.t)
            mtok_[u] = (ka_, km, r)

        def down_sum(u):
            ka_, km, ta = mtok_[u]
            wh, wl, r = ws_.enter()
            cur = ws_.cur
            wh, wl = [x.rearrange("p (m n) -> p m n", m=4) for x in (wh, wl)]
            for t_ in range(NT):
                for n in range(2):
                    b = Bank()
                    PE.wait(*b.w, *ta, *r)
                    tc, nc_ = slice(t_ * P, (t_ + 1) * P), slice(n * 512, n * 512 + 512)
                    for m in range(4):
                        mm3(b.ap, Ah[km][:, m, tc], Al[ka_][:, m, tc], wh[:, m, nc_], wl[:, m, nc_],
                            m == 0, m == 3, inc=(m == 3))
                    y = Y[:, t_, nc_]
                    if (t_, n) in ytok:
                        ytok[t_, n] = tt(V, y, y, b.ap, ADD, PE.t, ytok[t_, n])
                    else:
                        ytok[t_, n] = cp(V, y, b.ap, PE.t)
                    b.give(V.t)
            ws_.leave(*cur)
            Aring.give(ka_, PE.t)
            mring.give(km, PE.t)

        for i in range(NU - NE_):
            if i == 0:
                fetch(0)
            fetch(NE_ + i)
            gates(i)
            compute(NE_ + i)
            gates(NE_ + i)
            if i + 1 < NU - NE_:
                fetch(i + 1)
            down_sum(i)
            down_sum(NE_ + i)
        xo = Space(high[:, :], a_at - nlow, 4096).get(NT, D)
        lno = next(lines)
        t_xl = load(xo, A["xs"].rearrange("(t p) d -> p t d", p=P), PE.t, V.t, G.t, q=S, ln=next(lines))
        for t_ in range(NT):
            tt(V, Y[:, t_, :], Y[:, t_, :], gt2_2, MUL, V.t)
            tt(V, Y[:, t_, :], Y[:, t_, :], xo[:, t_, :], ADD, V.t, t_xl)
            to = SP.dma(lno, out[t_ * P:(t_ + 1) * P, :], Y[:, t_, :], V.t)
        ldone.append(to)
        return finish(nc, ctx, (PE, V, S, G, SP), ldone)


def finish(nc, ctx, queues, ldone):
    PE, V, S, G, SP = queues
    SP.wait(*ldone)
    block = ctx.enter_context(nc.Block())

    @block.sync
    def _(e):
        SP.emit(e)

    @block.gpsimd
    def _(e):
        G.emit(e)

    @block.scalar
    def _(e):
        S.emit(e)

    @block.vector
    def _(e):
        V.emit(e)

    @block.tensor
    def _(e):
        PE.emit(e)


def layout(inputs):
    f = lambda n: np.asarray(inputs[n])
    col = lambda a, n: np.ascontiguousarray(a.reshape(n, 128).T)
    m = {}
    m["cst"], m["c1"], m["c2"] = constants()
    m["x"] = f("x")[0]
    m["c"] = col(f("c")[0], 8)
    m["c_2"] = col(f("c_2")[0], 8)
    p1, p2 = f("positions")[0], f("positions_2")[0]
    ce = p1[31::16]
    ce = np.concatenate([ce, ce[-1:]])
    ce = np.concatenate([ce, ce, ce, ce])
    m["pos"] = np.ascontiguousarray(np.concatenate([p1.reshape(4, 128), ce[None], p2.reshape(4, 128)]).T)
    m["w_ada"], m["w_ada_2"] = f("w_ada")[0], f("w_ada_2")[0]
    m["b_ada_c"], m["b_ada_2_c"] = col(f("b_ada")[0], 24), col(f("b_ada_2")[0], 48)
    m["b_ada_r"], m["b_ada_2_r"] = f("b_ada")[0], f("b_ada_2")[0]
    for n in ("g_pre", "norm_mix_2", "norm_ffn_2"):
        m[n] = col(f(n)[0], 8)
    m["g_post"] = f("g_post")[0]
    for n in ("w_in", "w_out", "cmp_w1_k", "cmp_w1_v", "cmp_w2_k", "cmp_w2_v", "w_in_2", "w_uq_2", "w_ukv_2",
              "w_o_mla_2", "w_decay_up_2", "w_aaa_up_2", "w_gate_up_2", "w_o_rwkv_2", "w_out_2", "w_query_2",
              "mu_shift_2", "decay_base_2", "aaa_base_2", "k_k_2", "k_a_2", "ln_x_w_2", "ln_x_b_2",
              "q_norm_2", "k_norm_2"):
        m[n] = f(n)[0]
    m["r_k_2"] = f("r_k_2")[0].reshape(512)
    for n in ("cmp_pe_k", "cmp_pe_v"):
        m[n] = col(f(n)[0].reshape(-1), 16)
    m["q_a_norm_2"] = col(f("q_a_norm_2")[0], 2)
    m["kv_a_norm_2"] = col(f("kv_a_norm_2")[0], 1)
    for n in ("sub_keys1_2", "sub_keys2_2"):
        m[n] = f(n)[0].T
    m["down"] = f("expert_down_2")[0].reshape(32, 512, 8, 128).transpose(0, 3, 2, 1).reshape(32, 128, 4096)
    m["up"] = f("expert_up_2")[0].reshape(32, 4, 128, 1024).transpose(0, 2, 1, 3).reshape(32, 128, 4096)
    return {k: np.ascontiguousarray(v) for k, v in m.items()}


def program(nc, shapes, tap=None, stop=None):
    A = {}
    for name, (shape, dt) in shapes.items():
        A[name] = nc.dram_tensor("in_" + name, shape, dt, kind="ExternalInput").ap()
    for name, shape in (("xs", (512, D)), ("ps", (513, RW)), ("orw", (512, 512)), ("gd", (8, P, P, 64)), ("au", (NE_, P, 2048))):
        A[name] = nc.dram_tensor("scratch_" + name, shape, F32, kind="Internal").ap()
    out = nc.dram_tensor("out_0", (512, D), F32, kind="ExternalOutput").ap()
    build(nc, A, out, tap, stop)


def kernel(**inputs):
    import concourse.bacc as bacc
    from concourse.bass_utils import run_bass_kernel_spmd

    arrays = layout(inputs)
    nc = bacc.Bacc("TRN2", target_bir_lowering=False, num_devices=1)
    program(nc, {k: (v.shape, mybir.dt.from_np(v.dtype)) for k, v in arrays.items()})
    r = run_bass_kernel_spmd(nc, [{"in_" + k: v for k, v in arrays.items()}], core_ids=[0])
    return r.results[0]["out_0"].reshape(1, 512, 1024)
```

```python
from contextlib import ExitStack

import numpy as np

import concourse.bass as bass
from concourse import mybir

F32 = mybir.dt.float32
F32R = mybir.dt.float32r
BF16 = mybir.dt.bfloat16
I32 = mybir.dt.int32
U32 = mybir.dt.uint32
ALU = mybir.AluOpType
ACT = mybir.ActivationFunctionType
AXX = mybir.AxisListType.X
ADD, SUB, MUL, MAX, MIN, EQ, POW = (ALU.add, ALU.subtract, ALU.mult, ALU.max, ALU.min, ALU.is_equal, ALU.pow)

P = 128
NT = 4
D = 1024
NJ = 8
H = 8
PW1 = 3864
PW2 = 4256
RW = 1792
NE = 16384
NU = NE // 512
NE_ = 16
EM05 = float(np.exp(-0.5))


def constants():
    f = np.float32
    i = np.arange(128)
    c = {}
    c["ident"] = np.eye(128, dtype=f)
    c["caus"] = np.where(i[None, :] <= i[:, None], 0.0, -1e30).astype(f)
    c["iota"] = np.broadcast_to(i.astype(f), (128, 128))
    c["bd"] = (i[:, None] // 64 == i[None, :] // 64).astype(f)
    inv = [np.power(f(b), -np.arange(n, dtype=f) / f(n)).astype(f)
           for b, n in ((10000.0, 32), (500000.0, 8), (10000.0, 16))]
    c["inv"] = np.broadcast_to(np.concatenate(inv), (128, 56))
    c["nhalf"] = np.full((128, 32), -0.5, f)
    cst = np.ascontiguousarray(np.concatenate([c[k] for k in CST], axis=1), f)

    d = {}
    lg = np.log1p(-np.power(2.0, -5.0 - np.arange(H))).astype(f)
    diff = (i[None, :] - i[:, None]).astype(f)
    dec = np.where(diff[:, None, :] >= 0, np.exp(np.maximum(diff, 0)[:, None, :] * lg[None, :, None]), 0) * 0.125
    d["dec"] = dec.astype(f).reshape(128, 1024)
    d["zeta"] = np.exp((127 - i).astype(f)[:, None] * lg[None, :])
    d["xi"] = np.exp((i + 1).astype(f)[:, None] * lg[None, :]) * f(0.125)
    cd = np.exp(f(128) * lg)
    d["cd"] = np.concatenate([np.where(c["bd"] > 0, np.repeat(cd[2 * p:2 * p + 2], 64)[:, None], 0) for p in range(4)], 1)
    t = np.arange(512).reshape(4, 128)
    n = np.arange(32)
    ok = (n[None, None, :] * 16 + 31 <= t[:, :, None]) & (n < 31)
    ok = ok.transpose(1, 0, 2).reshape(128, 128)
    d["cneg"] = np.where(ok, 0.0, -1e30)
    d["cmul"] = ok.astype(f)
    d["hsel"] = 0.5 * (i[:, None] // 32 == np.arange(4)[None, :])
    c1 = np.ascontiguousarray(np.concatenate([d[k].astype(f) for k in C1], axis=1), f)

    e = {}
    same = i[:, None] // 64 == i[None, :] // 64
    e["tri"] = ((i[:, None] <= i[None, :]) & same).astype(f)
    e["mm"] = np.concatenate([((i[:, None] < i[None, :]) & same), ((i[:, None] <= i[None, :]) & same)], 1)

    def lev(l):
        b = 1 << (l - 1)
        t, s = i[:, None], i[None, :]
        return ((t // (2 * b) == s // (2 * b)) & (t // b % 2 == 1) & (s // b % 2 == 0)).astype(f)

    e["m1"] = lev(1)
    e["mt"] = np.concatenate([lev(l).T for l in range(1, 7)], 1)
    e["sel"] = (i[:, None] // 64 == np.arange(2)[None, :])
    c2 = np.ascontiguousarray(np.concatenate([e[k].astype(f) for k in C2], axis=1), f)
    return cst, c1, c2


CST = {"ident": 128, "caus": 128, "iota": 128, "bd": 128, "inv": 56, "nhalf": 32}
C1 = {"dec": 1024, "zeta": 8, "xi": 8, "cd": 512, "cneg": 128, "cmul": 128, "hsel": 4}
C2 = {"tri": 128, "mm": 256, "m1": 128, "mt": 768, "sel": 2}


class Queue:

    def __init__(self, sem):
        self.sem, self.n, self.items, self.seen = sem, 0, [], {}

    @property
    def t(self):
        return (self.sem, self.n)

    def wait(self, *toks):
        for sem, n in toks:
            if self.seen.get(id(sem), 0) < n:
                self.seen[id(sem)] = n
                self.items.append(lambda e, sem=sem, n=n: e.wait_ge(sem, n))

    def do(self, fn, *toks, inc=True):
        self.wait(*toks)
        if inc:
            self.n += 1
            self.items.append(lambda e: fn(e).then_inc(self.sem, 1))
        else:
            self.items.append(fn)
        return (self.sem, self.n)

    def dma(self, line, out, in_, *toks, **kw):
        self.wait(*toks)
        line[1] += 16
        self.items.append(lambda e: e.dma_start(out, in_, **kw).then_inc(line[0], 16))
        return (line[0], line[1])

    def emit(self, e):
        for f in self.items:
            f(e)


class Ring:

    def __init__(self, n, toks=()):
        self.free = [(k, list(toks)) for k in range(n)]

    def take(self):
        assert self.free, "no buffer has been given back"
        return self.free.pop(0)

    def give(self, k, *toks):
        self.free.append((k, list(toks)))


class Space:
    def __init__(self, ap, base, size):
        self.ap, self.at, self.end = ap, base, base + size

    def get(self, *shape):
        n = int(np.prod(shape))
        assert self.at + n <= self.end, (self.at, n, self.end)
        v = self.ap[:, self.at:self.at + n]
        self.at += n
        if len(shape) == 1:
            return v
        names = "abcd"[:len(shape)]
        return v.rearrange(f"p ({' '.join(names)}) -> p {' '.join(names)}",
                           **{names[k]: shape[k] for k in range(len(shape))})

    def fork(self, n):
        assert self.at + n <= self.end
        s = Space(self.ap, self.at, n)
        self.at += n
        return s

    def rest(self):
        return Space(self.ap, self.at, self.end - self.at)


def bx(ap, axis, shape):
    return ap.unsqueeze(axis).to_broadcast(list(shape))


def build(nc, A, out, tap=None, stop=None):
    ctx = ExitStack()
    with ctx:
        def sem(name):
            return ctx.enter_context(nc.semaphore(name))

        def line(name):
            return [sem(name), 0]

        PE, V, S, G, SP = [Queue(sem(n)) for n in ("pe", "dve", "act", "pool", "sp")]
        QS = (PE, V, S, G)
        alln = 53208
        NCST = sum(CST.values())
        nlow = 19816
        nph = alln - nlow
        hT_at, wslot_at, hi_at = 728, 7528, alln - 3 * 4096
        a_at, m_at = nlow + 8192, nlow + 16384
        cuts = [0, hT_at, hT_at + 4096, wslot_at, wslot_at + 4096, wslot_at + 8192, nlow, nlow + 2048,
                *[a_at + 2048 * i for i in range(7)], hi_at, hi_at + 4096, hi_at + 8192, alln]
        with nc.sbuf_tensor("low", [P, nlow], F32) as low, nc.sbuf_tensor("high", [P, nph], F32) as high:
            pass
        rpiece = {a: ctx.enter_context(nc.sbuf_tensor(f"r{a}", [P, b - a], F32R)) for a, b in zip(cuts, cuts[1:])}

        def rview(at, *shape):
            return Space(rpiece[at][:, :], 0, int(np.prod(shape))).get(*shape)

        root = Space(low[:, :], 0, nlow)
        cst = root.get(NCST)
        C = {}
        o = 0
        for k, n in CST.items():
            C[k] = cst[:, o:o + n]
            o += n
        ident = C["ident"]
        nhalf = C["nhalf"]
        identb = root.get(64).bitcast(BF16)
        cmaskb = root.get(64).bitcast(BF16)
        hT = root.get(NJ, 512)
        gt1_2 = root.get(D)
        gt2_2 = root.get(D)
        colm = root.get(64)
        ccol = root.get(16)
        trig = root.get(9, 2, 32)
        NW = 3
        wslot = [root.get(4096) for _ in range(NW)]
        wring = Ring(NW)
        wline = [line(f"w{i}") for i in range(NW)]
        phase = Space(high[:, :], 0, nph)
        whole = phase.rest()
        assert root.at == nlow
        hTl = rview(hT_at, NJ, 512)
        wlo = [rview(wslot_at + 4096 * i, 4096) for i in range(NW)]
        hTh = rview(hi_at, NJ, 512)
        whi = [rview(hi_at + 4096 * (i + 1), 4096) for i in range(2)]
        banks = [ctx.enter_context(nc.psum_tensor(f"ps{i}", [P, 512], F32)) for i in range(8)]
        ps, po = Ring(6), Ring(2)

        class Bank:
            def __init__(self, ring=ps):
                self.ring = ring
                self.k, self.w = ring.take()
                self.ap = banks[self.k + (0 if ring is ps else 6)][:, :]

            def v(self, n, m, parts=P):
                return self.ap[0:parts, 0:n * m].rearrange("p (a b) -> p a b", a=n)

            def give(self, *toks):
                self.ring.give(self.k, *toks)

        lines = iter([line(f"d{i}") for i in range(40)])
        ldone = []

        def load(out_, in_, *toks, q=SP, ln=None):
            return q.dma(ln or next(lines), out_, in_, *toks)

        def wload(*pairs):
            k, w = wring.take()
            for view, src in pairs:
                t = SP.dma(wline[k], view(wslot[k]), src, *w)
            return k, t

        def wblock(src, n):
            k, t = wload((lambda s: s[:, 0:NJ * n].rearrange("p (j n) -> p j n", j=NJ),
                          src.rearrange("(j p) n -> p j n", p=P)))
            return k, t, wslot[k][:, 0:NJ * n].rearrange("p (j n) -> p j n", j=NJ)

        def dbg(name, ap, *toks):
            if tap is not None:
                dst = tap(name, ap)
                t = load(dst, ap, *toks, ln=line("t_" + name))
                ldone.append(t)
                for q in QS:
                    q.wait(t)

        def barrier():
            toks = [q.t for q in QS]
            for q in QS:
                q.wait(*[t for t in toks if t[0] is not q.sem])
                q.wait(q.t)
            return toks

        def pow_nhalf(ap, n, *toks):
            return G.do(lambda e: e.tensor_tensor(ap, ap, nhalf[:, 0:n], POW), *toks)

        def tt(q, out_, a, b, op, *toks):
            return q.do(lambda e: e.tensor_tensor(out_, a, b, op), *toks)

        def ts(q, out_, a, s1, s2, op0, op1, *toks):
            if op1 is None:
                return q.do(lambda e: e.tensor_scalar(out_, a, s1, None, op0), *toks)
            return q.do(lambda e: e.tensor_scalar(out_, a, s1, s2, op0, op1), *toks)

        def stt(out_, a, s, b, op0, op1, *toks):
            return V.do(lambda e: e.scalar_tensor_tensor(out=out_, in0=a, scalar=s, in1=b, op0=op0, op1=op1), *toks)

        def red(out_, a, op, *toks, negate=None):
            return V.do(lambda e: e.tensor_reduce(out_, a, AXX, op, negate=negate), *toks)

        def act(out_, a, f, *toks, **kw):
            return S.do(lambda e: e.activation(out_, a, f, **kw), *toks)

        def cp(q, out_, a, *toks):
            if q is S:
                return act(out_, a, ACT.Copy, *toks)
            return q.do(lambda e: e.tensor_copy(out_, a), *toks)

        def mm(out_, l, r, start, stop, *toks, inc=False):
            return PE.do(lambda e: e.matmul(out_, l, r, start=start, stop=stop), *toks, inc=inc)

        def tr(out_, in_, *toks, inc=False):
            n = in_.shape[0]
            return PE.do(lambda e: e.transpose(out_, in_, ident[0:n, 0:n]), *toks, inc=inc)

        t_cst = load(cst, A["cst"])
        ct = phase.get(32)
        gcols = phase.get(24 + 8 + 48 + 8 + 8)
        b1c, gp1, b2c, gp2, gp3 = (gcols[:, 0:24], gcols[:, 24:32], gcols[:, 32:80], gcols[:, 80:88], gcols[:, 88:96])
        ln0 = next(lines)
        for dst, src in ((ct[:, 0:8], A["c"]), (ct[:, 8:16], A["c_2"]), (b1c, A["b_ada_c"]), (gp1, A["g_pre"]),
                         (b2c, A["b_ada_2_c"]), (gp2, A["norm_mix_2"]), (gp3, A["norm_ffn_2"])):
            t_cols = load(dst, src, ln=ln0)
        posi = phase.get(16)
        pos = phase.get(16)
        t_pos = load(posi[:, 0:9].bitcast(I32), A["pos"])
        G1 = phase.get(D)
        ln1 = next(lines)

        cp(V, identb, ident, t_cst)
        t_mb = cp(V, cmaskb, C["caus"])
        act(ct[:, 16:32], ct[:, 0:16], ACT.Tanh, t_cols, scale=0.5)
        stt(ccol, ct[:, 16:32], 1.0, ct[:, 0:16], ADD, MUL, S.t)
        t_cc = ts(V, ccol, ccol, 0.5, None, MUL, None, V.t)

        def trig_tables():
            ang = phase_tmp.get(9, 32)
            kk = phase_tmp.get(9, 32)
            r = phase_tmp.get(9, 32)
            nsat = phase_tmp.get(5, 16)
            cp(V, pos[:, 0:9], posi[:, 0:9].bitcast(I32), t_pos)
            inv = C["inv"]
            tt(V, ang[:, 0:4, :], bx(pos[:, 0:4], 2, (P, 4, 32)), bx(inv[:, 0:32], 1, (P, 4, 32)), MUL, V.t)
            tt(V, ang[:, 4, 0:8], pos[:, 4:5].to_broadcast([P, 8]), inv[:, 32:40], MUL)
            tt(V, ang[:, 4, 8:16], pos[:, 4:5].to_broadcast([P, 8]), inv[:, 32:40], MUL)
            tt(V, ang[:, 4, 16:32], pos[:, 4:5].to_broadcast([P, 16]), inv[:, 40:56], MUL)
            tt(V, ang[:, 5:9, 0:16], bx(pos[:, 5:9], 2, (P, 4, 16)), bx(inv[:, 40:56], 1, (P, 4, 16)), MUL)
            tt(V, ang[:, 5:9, 16:24], bx(pos[:, 0:4], 2, (P, 4, 8)), bx(inv[:, 32:40], 1, (P, 4, 8)), MUL)
            tt(V, ang[:, 5:9, 24:32], bx(pos[:, 0:4], 2, (P, 4, 8)), bx(inv[:, 32:40], 1, (P, 4, 8)), MUL)
            pi2 = 2 * np.pi
            m1 = 6.28125
            m2 = float(np.float32(np.round((pi2 - m1) * 2 ** 21) / 2 ** 21))
            m3 = float(np.float32(pi2 - m1 - m2))
            big = 12582912.0
            for w, shift in ((0, 0.25), (1, 0.0)):
                ts(V, kk, ang, float(np.float32(1 / pi2)), shift, MUL, ADD, V.t)
                ts(V, kk, kk, big, None, ADD, None, V.t)
                ts(V, kk, kk, big, None, SUB, None, V.t)
                stt(r, kk, -m1, ang, MUL, ADD, V.t)
                stt(r, kk, -m2, r, MUL, ADD, V.t)
                stt(r, kk, -m3, r, MUL, ADD, V.t)
                if shift:
                    ts(V, r, r, float(np.pi / 2), None, ADD, None, V.t)
                ts(V, r, r, float(np.float32(3.1415925)), -float(np.float32(3.1415925)), MIN, MAX, V.t)
                act(trig[:, :, w, :], r, ACT.Sin, V.t)
                V.wait(S.t)
            return S.t

        phase_tmp = phase.rest()
        xt = phase_tmp.get(NT, D)
        t_x = load(xt, A["x"].rearrange("(t p) d -> p t d", p=P))
        t_trig = trig_tables()
        cosr = lambda k: trig[:, k, 0, :]
        sinr = lambda k: trig[:, k, 1, :]

        side = []
        side_every = [1, 0]

        def fill():
            side_every[1] += 1
            if side and side_every[1] % side_every[0] == 0:
                side.pop(0)()

        def drain_side():
            while side:
                side.pop(0)()

        accr = Ring(2)

        def mod_pieces(src, which, cc, half, accs, finish, accr):
            st_ = {}

            def sums(js):
                if 0 in js:
                    st_["w"] = wblock(src[:, which * D + half * 512:which * D + half * 512 + 512], 512)
                    st_["a"] = accr.take()
                k, t, w = st_["w"]
                ka, wa = st_["a"]
                acc = accs[ka]
                for j in js:
                    c = ccol[:, cc * 8 + j:cc * 8 + j + 1]
                    if j == 0:
                        ts(V, acc, w[:, j, :], c, None, MUL, None, t, t_cc, *wa)
                    else:
                        stt(acc, w[:, j, :], c, acc, MUL, ADD, V.t)
                if NJ - 1 in js:
                    wring.give(k, V.t)
                    st_["t"] = V.t

            def close():
                ka, _ = st_["a"]
                b = Bank()
                PE.wait(st_["t"], *b.w)
                finish(b, accs[ka])
                accr.give(ka, PE.t)

            return [lambda: sums((0, 1, 2, 3)), lambda: sums((4, 5, 6, 7)), close]

        def mod_cols(src, which, base, cc, half, accs):
            def finish(b, acc):
                for n in range(4):
                    mm(b.ap[:, n:n + 1], acc[:, n * P:(n + 1) * P], nhalf[:, 0:1], True, True, inc=(n == 3))
                ts(V, colm[:, base + 4 * half:base + 4 * half + 4], b.ap[:, 0:4], -2.0, None, MUL, None, PE.t)
                b.give(V.t)
            return mod_pieces(src, which, cc, half, accs, finish, accr)

        def mod_row(src, which, dst, cc, half, accs, mulrow=None):
            def finish(b, acc):
                mm(b.ap, ones, acc, True, True, t_ones, inc=True)
                d_ = dst[:, half * 512:half * 512 + 512]
                tt(V, d_, b.ap, d_, ADD, PE.t, t_rows)
                b.give(V.t)
                if mulrow is not None:
                    tt(V, d_, d_, mulrow[:, half * 512:half * 512 + 512], MUL, V.t)
            return mod_pieces(src, which, cc, half, accs, finish, accr)

        def finish_cols(base, bcol, bat, gp):
            sh, sc = colm[:, base:base + 8], colm[:, base + 8:base + 16]
            tt(V, sh, sh, bcol[:, bat:bat + 8], ADD, V.t, t_cols)
            tt(V, sc, sc, bcol[:, bat + 8:bat + 16], ADD, V.t)
            return stt(sc, sc, 1.0, gp, ADD, MUL, V.t)

        def normalise_tile(xt, t_, spare, *toks):
            xh, ss = spare
            act(xh[:, t_, :], xt[:, t_, :], ACT.Square, *toks, accum_out=ss[:, t_:t_ + 1])
            r = ss[:, 4 + t_:5 + t_]
            ts(V, r, ss[:, t_:t_ + 1], 1.0 / D, 1e-6, MUL, ADD, S.t)
            tp = pow_nhalf(r, 1, V.t)
            if t_ % 2:
                return ts(V, xh[:, t_, :], xt[:, t_, :], r, None, MUL, None, tp, *toks)
            return act(xh[:, t_, :], xt[:, t_, :], ACT.Copy, tp, scale=r)

        def normalised(xt, ready, spare, after=()):
            S.wait(*ready, *after)
            V.wait(*after)
            return [t for t_ in range(NT) for t in [normalise_tile(xt, t_, spare, *ready)]]

        def make_hT(xt, ready, base, tcol, spare, after=(), xd=None):
            xh = spare[0]
            xd = xd or normalised(xt, ready, spare, after)
            for j in range(NJ):
                b = Bank()
                PE.wait(*b.w, *xd)
                for t_ in range(NT):
                    tr(b.ap[:, t_ * P:(t_ + 1) * P], xh[:, t_, j * P:(j + 1) * P], inc=(t_ == NT - 1))
                sc, sh = colm[:, base + 8 + j:base + 9 + j], colm[:, base + j:base + j + 1]
                if j % 2:
                    act(hT[:, j, :], b.ap, ACT.Identity, PE.t, tcol, scale=sc, bias=sh)
                    b.give(S.t)
                else:
                    ts(V, hT[:, j, :], b.ap, sc, sh, MUL, ADD, PE.t, tcol)
                    b.give(V.t)
            return (S.t, V.t)

        xh1 = phase_tmp.get(NT, D)
        ss1 = phase_tmp.get(16)
        accs = [phase_tmp.get(512) for _ in range(2)]
        xd1 = normalised(xt, (t_x,), (xh1, ss1))
        halves = [mod_cols(A["w_ada"], which, 8 * which, 0, half, accs) for which in range(2) for half in range(2)]
        for p_ in halves:
            for piece in p_:
                piece()
        t_col1 = finish_cols(0, b1c, 0, gp1)
        load(G1, A["b_ada_r"][2 * D:3 * D].partition_broadcast(P), ln=ln1)
        load(gt1_2, A["b_ada_2_r"][2 * D:3 * D].partition_broadcast(P), ln=ln1)
        load(gt2_2, A["b_ada_2_r"][5 * D:6 * D].partition_broadcast(P), ln=ln1)
        t_rows = (ln1[0], ln1[1])
        hready = make_hT(xt, (t_x,), 0, t_col1, (xh1, ss1), (), xd1)
        dbg("hT", hT, *hready)
        bt = barrier()

        ph = Space(phase.ap, phase.at, phase.end - phase.at)
        c1 = ph.get(sum(C1.values()))
        t_c1 = load(c1, A["c1"], *bt, q=G)
        K1 = {}
        o = 0
        for k, n in C1.items():
            K1[k] = c1[:, o:o + n]
            o += n
        pe_t = ph.get(2, 16)
        w2s = ph.get(2, 2, 64)
        ln2 = next(lines)
        load(pe_t[:, 0, :], A["cmp_pe_k"], *bt, q=G, ln=ln2)
        load(pe_t[:, 1, :], A["cmp_pe_v"], q=G, ln=ln2)
        load(w2s[:, 0], A["cmp_w2_k"].rearrange("(j p) n -> p j n", p=P), q=G, ln=ln2)
        t_cw = load(w2s[:, 1], A["cmp_w2_v"].rearrange("(j p) n -> p j n", p=P), q=G, ln=ln2)

        end = Space(high[:, :], nph - 1152, 1152)
        ones, accs = end.get(P), [end.get(512) for _ in range(2)]
        ph.end -= 1152
        t_ones = G.do(lambda e: e.memset(ones, 1.0), *bt)
        accr = Ring(2, bt)
        for half in range(2):
            side += mod_row(A["w_ada"], 2, G1, 0, half, accs)
        for which, base in ((0, 16), (1, 24), (3, 32), (4, 40)):
            for half in range(2):
                side += mod_cols(A["w_ada_2"], which, base, 1, half, accs)
        for which, dst in ((2, gt1_2), (5, gt2_2)):
            for half in range(2):
                side += mod_row(A["w_ada_2"], which, dst, 1, half, accs)
        for i in range(2, len(side) - 1, 3):
            side[i], side[i + 1] = side[i + 1], side[i]
        side_every[0] = 1
        mix = ph.get(NT, D)
        nqT = ph.get(4, 512)
        gl = ph.get(NT, 24)
        vs = ph.get(2, NT, 128)
        KT = ph.get(2, 2, 512)
        kc2 = [ph.get(2, 529), ph.get(2, 529)]
        tmp = ph.get(3, 512)
        retsp = ph.rest()
        rqT = ph.get(4, 512)
        rkT = ph.get(4, 512)
        rk = ph.get(NT, 512)
        rv = ph.get(NT, 512)
        t_kz = G.do(lambda e: e.memset(kc2[0], 0.0))
        t_kz = G.do(lambda e: e.memset(kc2[1], 0.0))

        early_side = [True]

        def proj(w, n, t_, b, c0=0):
            for j in range(NJ):
                mm(b.ap[:, 0:n], hT[:, j, t_ * P:(t_ + 1) * P], w[:, j, c0:c0 + n], j == 0, j == NJ - 1,
                   inc=(j == NJ - 1))
            t = PE.t
            if early_side[0]:
                fill()
            return t

        tring = Ring(3)

        def turn(src_tok, src, dst_of, evac, *w):
            b = Bank()
            PE.wait(src_tok, *b.w)
            for p in range(4):
                tr(b.ap[:, p * P:(p + 1) * P], src[:, p * P:(p + 1) * P], inc=(p == 3))
            cp(evac, dst_of, b.v(4, P), PE.t, *w)
            b.give(evac.t)
            return PE.t, evac.t

        def rope_full(b, dst, t_, tk, w):
            k2, w2 = tring.take()
            u = tmp[:, k2, :].rearrange("p (h d) -> p h d", h=H)
            s = b.v(H, 64)
            c_ = bx(cosr(t_), 1, (P, H, 32))
            s_ = bx(sinr(t_), 1, (P, H, 32))
            V.wait(tk, t_trig, *w, *w2)
            tt(V, dst[:, :, 0:32], s[:, :, 0:32], c_, MUL)
            tt(V, dst[:, :, 32:64], s[:, :, 32:64], c_, MUL)
            tt(V, u[:, :, 0:32], s[:, :, 32:64], s_, MUL)
            r = tt(V, u[:, :, 32:64], s[:, :, 0:32], s_, MUL)
            tt(G, dst[:, :, 0:32], dst[:, :, 0:32], u[:, :, 0:32], SUB, r)
            r2 = tt(G, dst[:, :, 32:64], dst[:, :, 32:64], u[:, :, 32:64], ADD)
            tring.give(k2, r2)
            return r, r2

        def rope_part(x, n, half, cosa, sina, tk, parts=P):
            k2, w2 = tring.take()
            u = tmp[0:parts, k2, 0:n * 4 * half].rearrange("p (a n h) -> p a n h", a=4, n=n)
            c_ = bx(cosa, 1, (parts, n, half))
            s_ = bx(sina, 1, (parts, n, half))
            x1, x2 = x[:, :, 0:half], x[:, :, half:2 * half]
            G.wait(tk, t_trig, *w2)
            tt(G, u[:, 0], x1, c_, MUL)
            tt(G, u[:, 1], x2, s_, MUL)
            tt(G, u[:, 2], x1, s_, MUL)
            a = tt(G, u[:, 3], x2, c_, MUL)
            tt(G, x1, u[:, 0], u[:, 1], SUB, a)
            r = tt(G, x2, u[:, 2], u[:, 3], ADD)
            tring.give(k2, r)
            return r

        rot = ph.get(2, 512)
        rring = Ring(2)

        def after_proj_rot(which):
            k, t, w = wblock(A["w_in"][:, which * 512:which * 512 + 512], 512)
            PE.wait(t, *hready, t_cst)
            pend = []
            tk_ = []
            for t_ in range(NT):
                b = Bank()
                PE.wait(*b.w)
                tk = proj(w, 512, t_, b)
                if t_ == NT - 1:
                    wring.give(k, tk)
                if which == 0:
                    k3, w3 = rring.take()
                    dst = rot[:, k3, :].rearrange("p (h d) -> p h d", h=H)
                    r, r2 = rope_full(b, dst, t_, tk, w3)
                    b.give(r)
                    pend.append((k3, rot[:, k3, :], r2, t_))
                else:
                    dst = rk[:, t_, :].rearrange("p (h d) -> p h d", h=H)
                    r, r2 = rope_full(b, dst, t_, tk, [])
                    b.give(r)
                    pend.append((None, rk[:, t_, :], r2, t_))
                while len(pend) > 1 or (pend and t_ == NT - 1):
                    k3, src, r2, tx = pend.pop(0)
                    a, b_ = turn(r2, src, (rqT if which == 0 else rkT)[:, :, tx * P:(tx + 1) * P], S)
                    if k3 is not None:
                        rring.give(k3, a)
                    tk_.append(b_)
            return tk_

        t_rq = after_proj_rot(0)
        t_rk = after_proj_rot(1)
        k, t, w = wblock(A["w_in"][:, 1024:1536], 512)
        PE.wait(t)
        t_rv = []
        for t_ in range(NT):
            b = Bank()
            PE.wait(*b.w)
            tk = proj(w, 512, t_, b)
            t_rv.append(cp(S, rv[:, t_, :], b.ap, tk))
            b.give(S.t)
        wring.give(k, tk)

        def silu2(w, off, tk_list):
            for t_ in range(NT):
                b = Bank()
                PE.wait(*b.w)
                tk = proj(w, 512, t_, b)
                k2, w2 = tring.take()
                act(tmp[:, k2, :], b.ap, ACT.Tanh, tk, *w2, scale=0.5)
                r = stt(mix[:, t_, off:off + 512], tmp[:, k2, :], 1.0, b.ap, ADD, MUL, S.t)
                b.give(r)
                tring.give(k2, r)
                tk_list.append(r)
            return tk

        k, t, w = wblock(A["w_in"][:, 1536:2048], 512)
        PE.wait(t)
        t_sg1 = []
        wring.give(k, silu2(w, 0, t_sg1))

        PTr = ph.get(2, 512)
        ptr_ring = Ring(2)
        R = ph.get(4, P)
        kz = ph.get(512)
        oo = ph.get(512)
        o2 = ph.get(512)
        st = ph.get(64)
        h3 = lambda ap: ap.rearrange("p (h d) -> p h d", h=H)

        def retention(t_, last):
            sl = slice(t_ * P, (t_ + 1) * P)
            pts = []
            for e in range(2):
                b = Bank()
                PE.wait(*b.w, t_rq[t_], t_rk[t_])
                rows = slice(64 * e, 64 * e + 64)
                for p in range(4):
                    mm(b.ap[:, p * P:(p + 1) * P], rkT[rows, p, sl], rqT[rows, p, sl], True, True, inc=(p == 3))
                k2, w2 = ptr_ring.take()
                dst = PTr[:, k2, :].rearrange("p (h i) -> p h i", h=4)
                dec = K1["dec"].rearrange("p (a e i) -> p e a i", a=4, e=2)[:, e]
                tt(V, dst, b.v(4, P), dec, MUL, PE.t, t_c1, *w2)
                b.give(V.t)
                pts.append((k2, dst, V.t))
            bi = Bank()
            PE.wait(*bi.w, t_rv[t_], *[x[2] for x in pts])
            for h in range(H):
                mm(bi.ap[:, h * 64:h * 64 + 64], pts[h % 2][1][:, h // 2, :], rv[:, t_, h * 64:h * 64 + 64],
                   True, True, inc=(h == 7))
            t_in = PE.t
            for x in pts:
                ptr_ring.give(x[0], PE.t)
            if t_ > 0:
                bc = Bank()
                PE.wait(*bc.w, last["R"])
                for p in range(4):
                    mm(bc.ap[:, p * P:(p + 1) * P], rqT[:, p, sl], R[:, p, :], True, True, inc=(p == 3))
                last["Rread"] = PE.t
                tt(V, h3(o2), bc.v(H, 64), bx(K1["xi"], 2, (P, H, 64)), MUL, PE.t, *last["o2"])
                bc.give(V.t)
                tt(V, h3(oo), bi.v(H, 64), h3(o2), ADD, V.t, t_in, *last["oo"])
            else:
                cp(V, oo, bi.ap, t_in, *last["oo"])
            bi.give(V.t)
            t_oo = V.t
            if t_ < NT - 1:
                tt(G, h3(kz), h3(rk[:, t_, :]), bx(K1["zeta"], 2, (P, H, 64)), MUL, t_rk[t_], t_c1, *last["kz"])
                bk = Bank()
                PE.wait(*bk.w, G.t)
                for p in range(4):
                    mm(bk.ap[:, p * P:(p + 1) * P], kz[:, p * P:(p + 1) * P], rv[:, t_, p * P:(p + 1) * P],
                       True, True, inc=(p == 3))
                last["kz"] = [PE.t]
                bdb = bx(C["bd"], 1, (P, 4, P))
                if t_ == 0:
                    tt(V, R, bk.v(4, P), bdb, MUL, PE.t)
                else:
                    a = tt(G, R, R, K1["cd"].rearrange("p (a b) -> p a b", a=4), MUL, last["Rread"], last["R"])
                    tt(V, o2.rearrange("p (a b) -> p a b", a=4), bk.v(4, P), bdb, MUL, PE.t, t_oo)
                    tt(V, R, R, o2.rearrange("p (a b) -> p a b", a=4), ADD, V.t, a)
                bk.give(V.t)
                last["R"] = V.t
                last["o2"] = [V.t]
            red(st[:, 0:8], h3(oo), ADD, t_oo, *last["st"])
            ts(V, st[:, 0:8], st[:, 0:8], -1.0 / 64, None, MUL, None, V.t)
            a = tt(V, h3(oo), h3(oo), bx(st[:, 0:8], 2, (P, H, 64)), ADD, V.t)
            tt(G, kq, oo, oo, MUL, a, *last["kq"])
            red(st[:, 8:16], h3(kq), ADD, G.t)
            last["kq"] = [V.t]
            ts(V, st[:, 8:16], st[:, 8:16], 4.0 / 64, 4e-5, MUL, ADD, V.t)
            b_ = pow_nhalf(st[:, 8:16], 8, V.t)
            m = mix[:, t_, 0:512]
            tt(G, h3(m), h3(m), bx(st[:, 8:16], 2, (P, H, 64)), MUL, b_, t_sg1[t_])
            tt(V, m, m, oo, MUL, G.t)
            last["oo"] = [V.t]
            last["st"] = [G.t]
            return V.t

        kq = ph.get(512)
        last = {"o2": [], "oo": [], "kz": [], "R": None, "Rread": None, "st": [], "kq": []}

        k, t, w = wblock(A["w_in"][:, 2048:2560], 512)
        PE.wait(t)
        t_nq = []
        t_mix1 = []
        for t_ in range(NT):
            b = Bank()
            PE.wait(*b.w)
            tk = proj(w, 512, t_, b)
            k3, w3 = rring.take()
            a = act(rot[:, k3, :], b.ap, ACT.Copy, tk, *w3, scale=0.125)
            b.give(a)
            r2 = rope_part(rot[:, k3, :].rearrange("p (h d) -> p h d", h=H), H, 8,
                           trig[:, 5 + t_, 0, 16:24], trig[:, 5 + t_, 1, 16:24], a)
            if t_ == NT - 1:
                wring.give(k, tk)
            t_mix1.append(retention(t_, last))
            pt_, e_ = turn(r2, rot[:, k3, :], nqT[:, :, t_ * P:(t_ + 1) * P], S)
            rring.give(k3, pt_)
            t_nq.append(e_)

        if stop == "ret":
            for t_ in range(NT):
                dbg(f"ret{t_}", mix[:, t_, 0:512], *t_mix1)

        ka, ta, wa = wblock(A["w_in"][:, 2560:3072], 512)
        kb, tb, wb = wblock(A["w_in"][:, 3072:3352], 280)
        PE.wait(ta, tb)
        kvd = ph.get(1, 4, 4, 64)
        kvr = Ring(1)
        t_kt = []
        for t_ in range(NT):
            b = Bank()
            b2 = Bank()
            PE.wait(*b.w, *b2.w)
            proj(wa, 512, t_, b)
            tk1 = PE.t
            tk = proj(wb, 280, t_, b2)
            k3, w3 = kvr.take()
            kv = kvd[:, k3]
            S.wait(tk1, *w3)
            for kind, src in ((0, b.ap[:, 0:128]), (1, b.ap[:, 128:256]), (2, b.ap[:, 256:384])):
                cp(S, kv[:, kind].rearrange("p (g u) d -> p g u d", g=2),
                   bx(src.rearrange("p (g d) -> p g d", g=2), 2, (P, 2, 2, 64)))
            cp(S, vs[:, 0, t_, :], b.ap[:, 384:512])
            b.give(S.t)
            S.wait(tk)
            cp(S, kv[:, 3].rearrange("p (g u) d -> p g u d", g=2),
               bx(b2.ap[:, 0:128].rearrange("p (g d) -> p g d", g=2), 2, (P, 2, 2, 64)))
            cp(S, vs[:, 1, t_, :], b2.ap[:, 128:256])
            act(gl[:, t_, :], b2.ap[:, 256:280], ACT.Tanh, scale=0.5)
            b2.give(S.t)
            ca, sa = trig[:, 5 + t_, 0, 16:24], trig[:, 5 + t_, 1, 16:24]
            rope_part(kv[:, 2], 4, 8, ca, sa, S.t)
            r = rope_part(kv[:, 3], 4, 8, ca, sa, S.t)
            if t_ == NT - 1:
                wring.give(ka, tk)
                wring.give(kb, tk)
            for kinds in ((0, 1), (2, 3)):
                bb = Bank()
                PE.wait(*bb.w, r)
                for x, kind in enumerate(kinds):
                    for g in range(2):
                        tr(bb.ap[:, (x * 2 + g) * P:(x * 2 + g + 1) * P],
                           kv[:, kind, 2 * g:2 * g + 2, :].rearrange("p u d -> p (u d)"), inc=(x == 1 and g == 1))
                s4 = bb.ap.rearrange("p (x g t) -> p x g t", x=2, g=2)
                if kinds[0] == 0:
                    V.wait(t_kz)
                    for x in range(2):
                        cp(V, kc2[x][0:64, :, 1 + t_ * P:1 + (t_ + 1) * P], s4[0:64, x], PE.t)
                        cp(V, kc2[x][64:128, :, t_ * P:(t_ + 1) * P], s4[64:128, x])
                    bb.give(V.t)
                else:
                    cp(S, KT[:, :, :, t_ * P:(t_ + 1) * P], s4, PE.t)
                    bb.give(S.t)
            kvr.give(k3, PE.t)
            t_kt.append((V.t, S.t))
        t_gl = ts(G, gl, gl, 1.0, None, ADD, None, S.t)
        k, t, w = wblock(A["w_in"][:, 3352:3864], 512)
        PE.wait(t)
        t_sg2 = []
        wring.give(k, silu2(w, 512, t_sg2))
        t_h1 = PE.t

        bt = barrier()
        a1 = retsp
        fl = a1.get(2048)
        flat = [fl[:, x * 1024:x * 1024 + 1024].rearrange("p (m g n) -> p m g n", m=16, g=2) for x in range(2)]
        hid = a1.get(2, 256)
        hidT = a1.get(2, 2, 64)
        hv4 = a1.get(2, 2, 4, 32)
        kcs = a1.get(2, 64)
        kcT = a1.get(64)
        vcbd = a1.get(2, 4, 64)
        ht = a1.get(256)
        ring3 = [(a1.get(512), a1.get(512)) for _ in range(3)]
        sc8 = a1.get(8, 32)
        pt8 = a1.get(2, P)
        sm = a1.get(2, 64)
        att = a1.get(NT, 512)
        au = a1.get(2, 512)
        for x in range(2):
            for g in range(2):
                for aa in range(2):
                    src = kc2[x][:, g, 1 + 16 * aa:1 + 16 * aa + 512].rearrange(
                        "p (n b two) -> p b n two", n=32, b=8, two=2)[:, :, :, 0]
                    tt(V, flat[x][:, 8 * aa:8 * aa + 8, g, :], src,
                       bx(pe_t[:, x, 8 * aa:8 * aa + 8], 2, (P, 8, 32)), ADD, t_cw)
        t_flat = V.t
        for x, nm in enumerate(("cmp_w1_k", "cmp_w1_v")):
            k, t = wload((lambda s: s.rearrange("p (m n) -> p m n", m=16),
                          A[nm].rearrange("(m p) n -> p m n", p=P)))
            w = wslot[k].rearrange("p (m n) -> p m n", m=16)
            b = Bank()
            PE.wait(t, t_flat, *b.w)
            for m in range(16):
                mm(b.ap[0:64, 0:256], flat[x][:, m].rearrange("p g n -> p (g n)"), w[:, m, :], m == 0, m == 15,
                   inc=(m == 15))
            wring.give(k, PE.t)
            act(ht[0:64, :], b.ap[0:64, 0:256], ACT.Tanh, PE.t, V.t, scale=0.5)
            r = stt(hid[0:64, x, :], ht[0:64, :], 1.0, b.ap[0:64, 0:256], ADD, MUL, S.t)
            b.give(r)
            b = Bank()
            PE.wait(r, *b.w)
            for j in range(2):
                tr(b.ap[:, j * 64:j * 64 + 64], hid[0:64, x, j * P:(j + 1) * P], inc=(j == 1))
            if x == 0:
                cp(V, hidT[:, 0], b.v(2, 64), PE.t)
            else:
                for j in range(2):
                    for g in range(2):
                        s_ = b.ap[:, j * 64 + g * 32:j * 64 + g * 32 + 32]
                        cp(V, hv4[:, j, g], bx(s_, 1, (P, 4, 32)), PE.t)
            b.give(V.t)
            b = Bank()
            PE.wait(V.t, *b.w)
            if x == 0:
                for j in range(2):
                    mm(b.ap[0:64, 0:64], hidT[:, 0, j], w2s[:, 0, j], j == 0, j == 1, inc=(j == 1))
                act(kcs[0:64], bx(b.ap[0:64, 0:64], 1, (64, 2, 64)), ACT.Copy, PE.t, scale=0.5)
                b.give(S.t)
                r = rope_part(kcs[0:64], 2, 8, trig[0:64, 4, 0, 0:8], trig[0:64, 4, 1, 0:8], S.t, 64)
                b = Bank()
                PE.wait(r, *b.w)
                tr(b.ap[:, 0:64], kcs[0:64].rearrange("p u d -> p (u d)"), inc=True)
                t_kct = cp(V, kcT, b.ap[:, 0:64], PE.t)
                b.give(V.t)
            else:
                for g in range(2):
                    for j in range(2):
                        mm(b.ap[:, g * 64:g * 64 + 64], hv4[:, j, g].rearrange("p a n -> p (a n)"), w2s[:, 1, j],
                           j == 0, j == 1, inc=(j == 1 and g == 1))
                for g in range(2):
                    t_vc = tt(V, vcbd[:, g], bx(b.ap[:, g * 64:g * 64 + 64], 1, (P, 4, 64)),
                              bx(K1["hsel"], 2, (P, 4, 64)), MUL, PE.t)
                b.give(V.t)

        class Attention:

            def __init__(self, bufs):
                self.bufs, self.pr, self.tr_, self.a, self.b, self.i = bufs, Ring(3), Ring(3), [], [], 0

            def feed(self, t_, q, k, v, out_, sum_, nmx, scale=1.0, ready=(), done=None):
                n = (t_ + 1) * P
                b = Bank()
                PE.wait(*b.w, *ready)
                mm(b.ap[:, 0:n], q, k, True, False)
                mm(b.ap[:, t_ * P:n], identb, cmaskb, False, True, inc=True)
                kx, wx = self.pr.take()
                Pb = self.bufs[kx][0]
                red(nmx, b.ap[:, 0:n], MAX, PE.t, negate=True)
                if scale != 1.0:
                    ts(V, nmx, nmx, scale, None, MUL, None, V.t)
                act(Pb[:, 0:n], b.ap[:, 0:n], ACT.Exp, V.t, *wx, bias=nmx, scale=scale, accum_out=sum_)
                b.give(S.t)
                self.a.append((t_, kx, S.t, v, out_, done))
                self.step(2, 1)

            def step(self, na, nb):
                fill()
                if len(self.a) > na:
                    self.turn()
                if len(self.b) > nb:
                    self.product()

            def flush(self):
                while self.a or self.b:
                    self.step(0, 1 if self.a else 0)

            def turn(self):
                t_, kx, te, v, out_, done = self.a.pop(0)
                n = (t_ + 1) * P
                b = Bank()
                PE.wait(*b.w, te)
                for kb in range(t_ + 1):
                    tr(b.ap[:, kb * P:(kb + 1) * P], self.bufs[kx][0][:, kb * P:(kb + 1) * P], inc=(kb == t_))
                self.pr.give(kx, PE.t)
                ky, wy = self.tr_.take()
                self.i += 1
                q = V if self.i % 2 else S
                cp(q, self.bufs[ky][1][:, 0:n], b.ap[:, 0:n], PE.t, *wy)
                b.give(q.t)
                self.b.append((t_, ky, q.t, v, out_, done))

            def product(self):
                t_, ky, tc, v, out_, done = self.b.pop(0)
                PE.wait(tc)
                for kb in range(t_ + 1):
                    mm(out_, self.bufs[ky][1][:, kb * P:(kb + 1) * P], v(kb), kb == 0, kb == t_, inc=(kb == t_))
                self.tr_.give(ky, PE.t)
                if done:
                    done()

        G1b = kc2[0].rearrange("p a b -> p (a b)")[:, 0:D]
        xt = a1.get(NT, D)
        t_G1b = load(G1b, A["g_post"].partition_broadcast(P), PE.t, V.t, G.t, S.t, q=G)
        t_x = load(xt, A["x"].rearrange("(t p) d -> p t d", p=P), q=G)
        pipe = Attention(ring3)
        smr = Ring(2)
        aur = Ring(2)
        t_att = []
        sc_free = []
        early_side[0] = False
        cst_, attd = {}, {}

        def compressed(t_, stage):
            sl = slice(t_ * P, (t_ + 1) * P)
            if stage == 0:
                kS, wS = smr.take()
                sv = sm[:, kS, :]
                cst_[t_] = (kS, sv)
                for e in range(2):
                    b = Bank()
                    PE.wait(*b.w, t_nq[t_], t_kct)
                    rows = slice(64 * e, 64 * e + 64)
                    for p in range(4):
                        g = (2 * p + e) // 4
                        mm(b.ap[:, p * 32:p * 32 + 32], nqT[rows, p, sl], kcT[rows, g * 32:g * 32 + 32], True, True,
                           inc=(p == 3))
                    tt(V, sc8.rearrange("p (a e) n -> p e a n", e=2)[:, e], b.v(4, 32),
                       bx(K1["cneg"][:, t_ * 32:t_ * 32 + 32], 1, (P, 4, 32)), ADD, PE.t, *sc_free)
                    b.give(V.t)
                red(sv[:, 0:8], sc8, MAX, V.t, *wS)
                tt(V, sc8, sc8, bx(sv[:, 0:8], 2, (P, 8, 32)), SUB, V.t)
                act(sc8, sc8, ACT.Exp, V.t)
                cst_["exp"] = S.t
                return
            kS, sv = cst_[t_]
            if stage == 1:
                red(sv[:, 8:16], sc8, ADD, cst_["exp"])
                tt(V, sc8, sc8, bx(K1["cmul"][:, t_ * 32:t_ * 32 + 32], 1, (P, 8, 32)), MUL, V.t)
                cst_["p"] = V.t
                V.do(lambda e, sv=sv: e.reciprocal(sv[:, 8:16], sv[:, 8:16]), V.t)
                gv = gl[:, t_, :].rearrange("p (h c) -> p h c", c=3)
                stt(sv[:, 8:16], sv[:, 8:16], 0.25, gv[:, :, 0], MUL, MUL, V.t, t_gl)
                cst_["g"] = V.t
            if stage == 2:
                b = Bank()
                PE.wait(*b.w, cst_["p"])
                for g in range(2):
                    tr(b.ap[:, g * P:(g + 1) * P], sc8[:, 4 * g:4 * g + 4, :].rearrange("p h n -> p (h n)"),
                       inc=(g == 1))
                sc_free[:] = [PE.t]
                cst_["t"] = cp(V, pt8, b.v(2, P), PE.t)
                b.give(V.t)
            if stage == 3:
                ob = Bank()
                PE.wait(cst_["t"], t_vc, *ob.w)
                for g in range(2):
                    mm(ob.ap[:, g * 256:g * 256 + 256], pt8[:, g], vcbd[:, g].rearrange("p a d -> p (a d)"), True,
                       True, inc=(g == 1))
                attd[t_] = tt(V, h3(att[:, t_, :]), ob.v(H, 64), bx(sv[:, 8:16], 2, (P, H, 64)), MUL, cst_["g"], PE.t)
                ob.give(V.t)

        def weigh(t_, kind, ob):
            kS, sv = cst_[t_]
            o_ = 16 + 24 * kind
            gv = gl[:, t_, :].rearrange("p (h c) -> p h c", c=3)
            V.do(lambda e: e.reciprocal(sv[:, o_ + 16:o_ + 24], sv[:, o_:o_ + 8]), S.t)
            stt(sv[:, o_ + 16:o_ + 24], sv[:, o_ + 16:o_ + 24], 0.25, gv[:, :, 1 + kind], MUL, MUL, V.t)
            ka_, wa_ = aur.take()
            tt(V, h3(au[:, ka_, :]), ob.v(H, 64), bx(sv[:, o_ + 16:o_ + 24], 2, (P, H, 64)), MUL, V.t, PE.t, *wa_)
            ob.give(V.t)
            attd[t_] = tt(G, att[:, t_, :], att[:, t_, :], au[:, ka_, :], ADD, V.t, attd[t_])
            aur.give(ka_, G.t)
            if kind == 1:
                smr.give(kS, V.t)
                tt(G, mix[:, t_, 512:1024], mix[:, t_, 512:1024], att[:, t_, :], MUL, G.t, t_sg2[t_])
                t_att.append(G.t)

        for stage in range(4):
            compressed(0, stage)
        it = 0
        for t_ in range(NT):
            sl = slice(t_ * P, (t_ + 1) * P)
            n = (t_ + 1) * P
            for kind in range(2):
                ob = Bank(po)
                PE.wait(*ob.w)
                o_ = 16 + 24 * kind
                sv = cst_[t_][1]
                for h in range(H):
                    rows = slice(64 * (h % 2), 64 * (h % 2) + 64)
                    g = h // 4
                    pipe.feed(t_, nqT[rows, h // 2, sl], KT[rows, kind, g, 0:n],
                              lambda kb, kind=kind, g=g: vs[:, kind, kb, g * 64:g * 64 + 64],
                              ob.ap[:, h * 64:h * 64 + 64], sv[:, o_ + h:o_ + h + 1], sv[:, o_ + 8 + h:o_ + 9 + h],
                              ready=[t_nq[t_], *t_kt[t_]],
                              done=(lambda t_=t_, kind=kind, ob=ob: weigh(t_, kind, ob)) if h == 7 else None)
                    if t_ + 1 < NT and kind * 8 + h in (5, 7, 9, 11):
                        compressed(t_ + 1, (kind * 8 + h - 5) // 2)
        pipe.flush()
        if tap is not None:
            dbg("mix", mix, *t_att, *t_mix1)

        drain_side()
        t_G1 = tt(V, G1, G1, G1b, MUL, V.t, t_G1b)
        t_col2 = finish_cols(16, b2c, 0, gp2)
        t_col3 = finish_cols(32, b2c, 24, gp3)

        def transpose_into_hT(src, n, toks):
            for j in range(n):
                b = Bank()
                PE.wait(*b.w, *toks)
                for t_ in range(NT):
                    tr(b.ap[:, t_ * P:(t_ + 1) * P], src[:, t_, j * P:(j + 1) * P], inc=(t_ == NT - 1))
                q = V if j % 2 else S
                cp(q, hT[:, j, :], b.ap, PE.t, t_h1)
                b.give(q.t)
            return (S.t, V.t)

        mtok = transpose_into_hT(mix, NJ, (*t_att, *t_mix1))
        ws = [wblock(A["w_out"][:, n * 512:n * 512 + 512], 512) for n in range(2)]
        y2 = mix
        ss2 = sm
        xd2 = []
        for t_ in range(NT):
            for n in range(2):
                k, t, w = ws[n]
                b = Bank()
                PE.wait(*b.w, t, *mtok)
                proj(w, 512, t_, b)
                act(au[:, 0, :], b.ap, ACT.Square, PE.t, V.t, G.t, accum_out=ss2[:, 0, 8 + 2 * t_ + n:9 + 2 * t_ + n])
                tt(V, y2[:, t_, n * 512:n * 512 + 512], b.ap, G1[:, n * 512:n * 512 + 512], MUL, S.t, t_G1)
                b.give(V.t)
            m = ss2[:, 0, t_:t_ + 1]
            tt(V, m, ss2[:, 0, 8 + 2 * t_:9 + 2 * t_], ss2[:, 0, 9 + 2 * t_:10 + 2 * t_], ADD, S.t)
            ts(V, m, m, 1.0 / D, 1e-6, MUL, ADD, V.t)
            tp = pow_nhalf(m, 1, V.t)
            t_x1 = stt(xt[:, t_, :], y2[:, t_, :], m, xt[:, t_, :], MUL, ADD, tp, V.t, t_x)
            xd2.append(normalise_tile(xt, t_, (mix, sm[:, 1, :]), t_x1))
        for n in range(2):
            wring.give(ws[n][0], PE.t)
        dbg("x1", xt, t_x1)
        t_xsp = load(A["xs"].rearrange("(t p) d -> p t d", p=P), xt, t_x1, q=S)

        hready = make_hT(xt, (t_x1,), 16, t_col2, (mix, sm[:, 1, :]), (), xd2)
        dbg("h2T", hT, *hready)
        bt = barrier()
        for q in QS:
            q.wait(t_xsp)
        if stop in ("b1", "ret"):
            return finish(nc, ctx, (PE, V, S, G, SP), ldone)

        ph = whole.rest()
        omla = ph.get(NT, 512)
        m2 = ph.rest()
        nrm = m2.get(2, 96)
        qan = m2.get(4)
        ln3 = next(lines)
        load(nrm[:, 0, :], A["q_norm_2"].partition_broadcast(P), *bt, t_xsp, q=G, ln=ln3)
        load(nrm[:, 1, :], A["k_norm_2"].partition_broadcast(P), q=G, ln=ln3)
        load(qan[:, 0:2], A["q_a_norm_2"], q=G, ln=ln3)
        t_nrm = load(qan[:, 2:3], A["kv_a_norm_2"], q=G, ln=ln3)
        mqT = m2.get(H, 512)
        mkT = m2.get(H, 512)
        mv = m2.get(NT, 512)
        mst = m2.get(NT, 64)
        ring3 = [(m2.get(512), m2.get(512)) for _ in range(3)]
        mla_end = m2.at
        lat = m2.get(NT, 416)
        lT = m2.get(3, 512)
        qk = m2.get(2, 2, H, 96)
        sq = m2.get(2, H, 96)
        tmp = m2.get(3, 512)
        pst = m2.get(2, 512)
        tring = Ring(3)
        psr = Ring(2)
        k, t, w = wblock(A["w_in_2"][:, 0:416], 416)
        PE.wait(t, *hready)
        for t_ in range(NT):
            b = Bank()
            PE.wait(*b.w)
            proj(w, 416, t_, b)
            cp(S, lat[:, t_, :], b.ap[:, 0:416], PE.t)
            b.give(S.t)
        wring.give(k, PE.t)
        psd = A["ps"]
        zrow = m2.get(RW // 16)
        G.do(lambda e: e.memset(zrow, 0.0))
        ln4 = [next(lines) for _ in range(3)]
        t_ps = [(x[0], 0) for x in ln4]
        t_ps[2] = load(psd[0:1, :].rearrange("a (p n) -> (a p) n", p=16), zrow[0:16, :], G.t, q=S, ln=ln4[2])
        pw = [None]
        side_every[0] = 1
        for blk, (c0, n) in enumerate(((416, 512), (928, 512), (1440, 512), (1952, 256))):
            def job(t_, c0=c0, n=n):
                if t_ == 0:
                    pw[0] = wblock(A["w_in_2"][:, c0:c0 + n], n)
                k, t, w = pw[0]
                b = Bank()
                PE.wait(t, *b.w)
                proj(w, n, t_, b)
                if t_ == NT - 1:
                    wring.give(k, PE.t)
                kx, wx = psr.take()
                cp(S, pst[:, kx, 0:n], b.ap[:, 0:n], PE.t, *wx)
                b.give(S.t)
                t2 = S.dma(ln4[kx], psd[1 + t_ * P:1 + (t_ + 1) * P, c0 - 416:c0 - 416 + n], pst[:, kx, 0:n], S.t)
                psr.give(kx, t2)
                t_ps[kx] = t2
            for t_ in range(NT):
                side.append(lambda t_=t_, job=job: job(t_))

        t_l = S.t
        for t_ in range(NT):
            act(sq.rearrange("p a h d -> p (a h d)")[:, 0:256], lat[:, t_, 0:256], ACT.Square, t_l, S.t,
                accum_out=mst[:, t_, 0:1])
            act(sq.rearrange("p a h d -> p (a h d)")[:, 256:384], lat[:, t_, 256:384], ACT.Square, S.t,
                accum_out=mst[:, t_, 1:2])
            act(sq.rearrange("p a h d -> p (a h d)")[:, 384:416], lat[:, t_, 384:416], ACT.Square, S.t,
                accum_out=mst[:, t_, 2:3])
        ts(V, mst[:, :, 0:1], mst[:, :, 0:1], 1.0 / 256, 1e-6, MUL, ADD, S.t)
        ts(V, mst[:, :, 1:2], mst[:, :, 1:2], 1.0 / 128, 1e-6, MUL, ADD)
        ts(V, mst[:, :, 2:3], mst[:, :, 2:3], 1.0 / 32, 1e-6, MUL, ADD)
        tp = G.do(lambda e: e.tensor_tensor(mst[:, :, 0:3], mst[:, :, 0:3],
                                            nhalf[:, 0:12].rearrange("p (a b) -> p a b", a=4), POW), V.t)
        for t_ in range(NT):
            ts(V, lat[:, t_, 0:256], lat[:, t_, 0:256], mst[:, t_, 0:1], None, MUL, None, tp)
            ts(V, lat[:, t_, 256:384], lat[:, t_, 256:384], mst[:, t_, 1:2], None, MUL, None)
            stt(lat[:, t_, 384:416], lat[:, t_, 384:416], mst[:, t_, 2:3], nrm[:, 1, 64:96], MUL, MUL, t_nrm)
        t_lv = V.t
        for _ in range(4):
            fill()
        for t_ in range(NT):
            t_kr = rope_part(lat[:, t_, 384:416].unsqueeze(1), 1, 16, trig[:, 5 + t_, 0, 0:16],
                             trig[:, 5 + t_, 1, 0:16], t_lv)
        for j in range(3):
            b = Bank()
            PE.wait(*b.w, t_lv)
            for t_ in range(NT):
                tr(b.ap[:, t_ * P:(t_ + 1) * P], lat[:, t_, j * P:(j + 1) * P], inc=(t_ == NT - 1))
            ts(V, lT[:, j, :], b.ap, qan[:, j:j + 1], None, MUL, None, PE.t)
            b.give(V.t)
        t_lT = V.t
        fill()
        k, t = wload((lambda s: s[:, 0:1536].rearrange("p (j n) -> p j n", j=2),
                      A["w_uq_2"].rearrange("(j p) n -> p j n", p=P)),
                     (lambda s: s[:, 1536:2560], A["w_ukv_2"]))
        wuq = wslot[k][:, 0:1536].rearrange("p (j n) -> p j n", j=2)
        wkv = wslot[k][:, 1536:2560]
        qkr = Ring(2)
        sqf = []
        t_mq = []
        SC = float(np.float32(96 ** -0.5))
        pipe = Attention(ring3)

        def normalise(t_, ob):
            V.do(lambda e: e.reciprocal(mst[:, t_, 48:56], mst[:, t_, 32:40]), S.t)
            tt(V, h3(omla[:, t_, :]), ob.v(H, 64), bx(mst[:, t_, 48:56], 2, (P, H, 64)), MUL, V.t, PE.t)
            ob.give(V.t)

        def mla_attend(t_):
            sl = slice(t_ * P, (t_ + 1) * P)
            ob = Bank(po)
            PE.wait(*ob.w)
            for h in range(H):
                pipe.feed(t_, mqT[0:96, h, sl], mkT[0:96, h, 0:(t_ + 1) * P],
                          lambda kb, h=h: mv[:, kb, h * 64:h * 64 + 64], ob.ap[:, h * 64:h * 64 + 64],
                          mst[:, t_, 32 + h:33 + h], mst[:, t_, 40 + h:41 + h], SC, t_mq[t_],
                          (lambda t_=t_, ob=ob: normalise(t_, ob)) if h == 7 else None)

        for t_ in range(NT):
            sl = slice(t_ * P, (t_ + 1) * P)
            kx, wx = qkr.take()
            q_, k_ = qk[:, kx, 0], qk[:, kx, 1]
            S.wait(*wx)
            G.wait(*wx)
            V.wait(*wx)
            for n in range(2):
                b = Bank()
                PE.wait(*b.w, t_lT, t)
                for j in range(2):
                    mm(b.ap[:, 0:384], lT[:, j, sl], wuq[:, j, n * 384:(n + 1) * 384], j == 0, j == 1, inc=(j == 1))
                cp(S, q_[:, 4 * n:4 * n + 4, :], b.v(4, 96), PE.t)
                b.give(S.t)
                b = Bank()
                PE.wait(*b.w)
                mm(b.ap, lT[:, 2, sl], wkv[:, n * 512:(n + 1) * 512], True, True, inc=True)
                cp(V, k_[:, 4 * n:4 * n + 4, 0:64], b.v(4, P)[:, :, 0:64], PE.t)
                cp(V, mv[:, t_, n * 256:n * 256 + 256].rearrange("p (h d) -> p h d", h=4), b.v(4, P)[:, :, 64:128])
                b.give(V.t)
                fill()
            ms = mst[:, t_, 8:32]
            tt(G, sq[:, 0], q_, q_, MUL, S.t, *sqf)
            tt(G, sq[:, 1, :, 0:64], k_[:, :, 0:64], k_[:, :, 0:64], MUL, V.t)
            red(ms[:, 0:8], sq[:, 0, :, 0:64], ADD, G.t)
            red(ms[:, 8:16], sq[:, 1, :, 0:64], ADD)
            red(ms[:, 16:24], sq[:, 0, :, 64:96], ADD)
            sqf = [V.t]
            ts(V, ms[:, 0:16], ms[:, 0:16], 1.0 / 64, 1e-6, MUL, ADD, V.t)
            ts(V, ms[:, 16:24], ms[:, 16:24], 1.0 / 32, 1e-6, MUL, ADD)
            pow_nhalf(ms, 24, V.t)
            tt(V, q_[:, :, 0:64], q_[:, :, 0:64], bx(ms[:, 0:8], 2, (P, H, 64)), MUL, G.t)
            tt(V, q_[:, :, 64:96], q_[:, :, 64:96], bx(ms[:, 16:24], 2, (P, H, 32)), MUL)
            tt(V, k_[:, :, 0:64], k_[:, :, 0:64], bx(ms[:, 8:16], 2, (P, H, 64)), MUL)
            tt(V, q_, q_, bx(nrm[:, 0, :], 1, (P, H, 96)), MUL, V.t, t_nrm)
            tq = V.t
            tt(V, k_[:, :, 0:64], k_[:, :, 0:64], bx(nrm[:, 1, 0:64], 1, (P, H, 64)), MUL)
            tk_ = V.t
            cp(G, k_[:, :, 64:96], bx(lat[:, t_, 384:416], 1, (P, H, 32)), t_kr)
            r = rope_part(q_[:, :, 64:96], H, 16, trig[:, 5 + t_, 0, 0:16], trig[:, 5 + t_, 1, 0:16], tq)
            side_every[0] = 2
            if t_:
                mla_attend(t_ - 1)
            side_every[0] = 1
            if t_ < 2:
                fill()
                fill()
            for which, src, dst in ((0, q_, mqT), (1, k_, mkT)):
                for n in range(2):
                    b = Bank()
                    PE.wait(*b.w, r, tk_)
                    for hh in range(4):
                        tr(b.ap[0:96, hh * P:(hh + 1) * P], src[:, 4 * n + hh, :], inc=(hh == 3))
                    cp(S, dst[0:96, 4 * n:4 * n + 4, sl], b.v(4, P, 96), PE.t)
                    b.give(S.t)
            qkr.give(kx, PE.t)
            t_mq.append((S.t, V.t))
        wring.give(k, PE.t)

        drain_side()
        top = Space(high[:, :], mla_end, nph - mla_end)
        r2 = Space(high[:, :], NT * 512, mla_end - NT * 512)
        bt = [q.t for q in QS]
        K2 = {}
        c2 = top.get(sum(C2.values()))
        o = 0
        for kx, n in C2.items():
            K2[kx] = c2[:, o:o + n]
            o += n
        rows = top.get(RW + 7 * 512)
        ln5 = next(lines)
        load(c2, A["c2"], *bt, ln=ln5)
        o = 0
        RWS = []
        for nm, n in (("mu_shift_2", RW), ("decay_base_2", 512), ("aaa_base_2", 512), ("k_k_2", 512), ("k_a_2", 512),
                      ("r_k_2", 512), ("ln_x_w_2", 512), ("ln_x_b_2", 512)):
            t_row = load(rows[:, o:o + n], A[nm].partition_broadcast(P), ln=ln5)
            RWS.append(rows[:, o:o + n])
            o += n
        mu, dbase, abase, kkw, kaw, rkw, lnw, lnb = RWS
        pp = top.get(RW)
        prs = [top.get(RW) for _ in range(2)]
        loT = top.get(2, P)
        rst = top.get(64)
        L, a_, e1, e2, bt_, kh = [top.get(512) for _ in range(6)]
        e3 = trig.rearrange("p a b c -> p (a b c)")[:, 0:512]
        gs = [top.get(512) for _ in range(2)]
        kks = [top.get(512) for _ in range(2)]
        y_ = r2.get(512)
        X1 = r2.get(4, 2, P)
        BK = r2.get(4, 2, P)
        MM = r2.get(2, 4, 4, P)
        Xb = [r2.get(4, P) for _ in range(2)]
        XTb = [r2.get(4, P) for _ in range(2)]
        T1b = [r2.get(4, P) for _ in range(2)]
        AMb = [r2.get(4, P) for _ in range(2)]
        T_ = [r2.get(4, P) for _ in range(3)]
        PCm = r2.get(2, 4, P)
        pcc = r2.get(4, 2)
        k, t_up = wload((lambda s: s[0:64, 0:512], A["w_decay_up_2"]), (lambda s: s[64:128, 0:512], A["w_aaa_up_2"]),
                        (lambda s: s[:, 512:1024], A["w_gate_up_2"]))
        kup = k
        wup = wslot[k]
        ln6 = next(lines)
        v4 = lambda ap: ap.rearrange("p (a b) -> p a b", a=4)
        oro = A["orw"]
        lnm = [line(f"m{i}") for i in range(2)]
        prep = {}

        def mix_pieces(t_):
            pr, g_, kk = prs[t_ % 2], gs[t_ % 2], kks[t_ % 2]
            rs = rst[:, 32 * (t_ % 2):32 * (t_ % 2) + 8]
            s = prep[t_] = {}
            r_, k_, v_ = pr[:, 0:512], pr[:, 512:1024], pr[:, 1024:1536]
            wd, gd = pr[:, 1536:1600], pr[:, 1664:1792]

            def loads():
                bt = [q.t for q in QS]
                load(pp, psd[1 + t_ * P:1 + (t_ + 1) * P, :], *bt, *t_ps, ln=lnm[t_ % 2])
                s["in"] = load(pr, psd[t_ * P:(t_ + 1) * P, :], ln=lnm[t_ % 2])

            def shift1():
                s["x"] = tt(V, pr, pr, pp, SUB, s["in"])

            def shift2():
                s["x"] = tt(V, pr, pr, mu, MUL, s["x"], t_row)

            def shift3():
                tt(V, pr, pr, pp, ADD, s["x"])
                s["p"] = V.t

            def low():
                act(wd, wd, ACT.Tanh, s["p"])
                act(gd, gd, ACT.Tanh, scale=0.5)
                ts(V, gd, gd, 0.5, 0.5, MUL, ADD, S.t)
                s["low"] = V.t

            def turned():
                b = Bank()
                PE.wait(*b.w, s["low"])
                for j in range(2):
                    tr(b.ap[:, j * P:(j + 1) * P], pr[:, 1536 + j * P:1536 + (j + 1) * P], inc=(j == 1))
                cp(V, loT, b.v(2, P), PE.t)
                b.give(V.t)
                s["loT"] = V.t

            def up():
                b0, b1, b2 = Bank(), Bank(), Bank()
                PE.wait(*b0.w, *b1.w, *b2.w, s["loT"], t_up)
                mm(b0.ap, loT[0:64, 0], wup[0:64, 0:512], True, True, inc=True)
                mm(b1.ap, loT[64:128, 0], wup[64:128, 0:512], True, True, inc=True)
                mm(b2.ap, loT[:, 1], wup[:, 512:1024], True, True, inc=True)
                tt(V, L, b0.ap, dbase, ADD, PE.t, t_row)
                b0.give(V.t)
                tt(V, a_, b1.ap, abase, ADD)
                b1.give(V.t)
                cp(S, g_, b2.ap, PE.t)
                b2.give(S.t)
                act(L, L, ACT.Tanh, V.t, scale=0.5)
                act(a_, a_, ACT.Tanh, scale=0.5)
                s["L"] = S.t

            def key():
                ts(V, L, L, -0.5 * EM05, -0.5 * EM05, MUL, ADD, s["L"])
                s["L"] = V.t
                ts(V, a_, a_, 0.5, 0.5, MUL, ADD)
                tt(V, kk, k_, kkw, MUL, t_row, s["p"])
                tt(G, e3, kk, kk, MUL, V.t)
                red(rs, h3(e3), ADD, G.t)
                ts(V, rs, rs, 1e-24, None, MAX, None, V.t)
                pow_nhalf(rs, 8, V.t)
                tt(V, h3(kk), h3(kk), bx(rs, 2, (P, H, 64)), MUL, G.t)
                s["kk"] = V.t

            return [loads, shift1, shift2, shift3, low, turned, up, key]

        def tail_pieces(t_):
            rs = rst[:, 32 * (t_ % 2):32 * (t_ % 2) + 32]
            v_, g_ = prs[t_ % 2][:, 1024:1536], gs[t_ % 2]

            def mean():
                red(rs[:, 16:24], h3(y_), ADD, V.t)
                ts(V, rs[:, 16:24], rs[:, 16:24], -1.0 / 64, None, MUL, None, V.t)
                tt(V, h3(y_), h3(y_), bx(rs[:, 16:24], 2, (P, H, 64)), ADD, V.t)
                tt(G, e3, y_, y_, MUL, V.t)
                tt(G, h3(v_), h3(v_), bx(rs[:, 8:16], 2, (P, H, 64)), MUL)

            def var():
                red(rs[:, 24:32], h3(e3), ADD, G.t)
                ts(V, rs[:, 24:32], rs[:, 24:32], 1.0 / 64, 64e-5, MUL, ADD, V.t)
                pow_nhalf(rs[:, 24:32], 8, V.t)
                tt(V, h3(y_), h3(y_), bx(rs[:, 24:32], 2, (P, H, 64)), MUL, G.t)
                tt(V, y_, y_, lnw, MUL, V.t)

            def end():
                tt(V, y_, y_, lnb, ADD, V.t)
                tt(V, y_, y_, v_, ADD, V.t)
                tt(V, y_, y_, g_, MUL, V.t)
                if tap is not None:
                    dbg(f"y{t_}", y_, V.t)
                t_y[0] = load(oro[t_ * P:(t_ + 1) * P, :], y_, V.t, ln=ln6)

            return [mean, var, end]

        t_y = [(ln6[0], 0)]
        gst = [wup[:, 1024:1536], wup[:, 1536:2048]]
        gstr = Ring(2)
        lngt = [line(f"gt{i}") for i in range(2)]

        def gate_stream():
            for n in range(4):
                k, t, w = wblock(A["w_in_2"][:, 2208 + n * 512:2720 + n * 512], 512)
                for tile in range(NT):
                    b = Bank(po)
                    for j in range(NJ):
                        if j == 0:
                            PE.wait(t, *b.w)
                        mm(b.ap, hT[:, j, tile * P:(tile + 1) * P], w[:, j, :], j == 0, j == NJ - 1,
                           inc=(j == NJ - 1))
                        if j < NJ - 1:
                            yield
                    if tile == NT - 1:
                        wring.give(k, PE.t)
                    kx, wx = gstr.take()
                    act(gst[kx], b.ap, ACT.Tanh, PE.t, *wx, scale=0.5)
                    b.give(S.t)
                    gstr.give(kx, load(A["gt"][n // 2, :, tile, (n % 2) * 512:(n % 2) * 512 + 512], gst[kx], S.t,
                                       ln=lngt[kx]))
                    yield

        gates_left = gate_stream()

        def trickle(n=1):
            for _ in range(n):
                next(gates_left, None)

        side += mix_pieces(0)
        side[1:1] = [lambda: None] * 3
        side_every[0] = 1
        mla_attend(NT - 1)
        pipe.flush()
        dbg("omla", omla, V.t)
        drain_side()
        bt = barrier()
        G.do(lambda e: e.memset(T_[0], 0.0))
        t_T = G.t
        cur = 0
        for t_ in range(NT):
            s_ = prep[t_]
            pr, g_, kk = prs[t_ % 2], gs[t_ % 2], kks[t_ % 2]
            r_, k_, v_ = pr[:, 0:512], pr[:, 512:1024], pr[:, 1024:1536]
            sb8 = rst[:, 32 * (t_ % 2) + 8:32 * (t_ % 2) + 16]
            t_p = s_["p"]
            barrier()
            bc = Bank()
            PE.wait(*bc.w, s_["L"])
            mm(bc.ap, K2["tri"], L, True, True, inc=True)
            t_cum = PE.t
            bp = Bank()
            PE.wait(*bp.w)
            for p in range(4):
                mm(bp.ap[:, 2 * p:2 * p + 2], L[:, p * P:(p + 1) * P], K2["sel"], True, True, inc=(p == 3))
            t_pc = PE.t
            mean, var, end = tail_pieces(t_ - 1) if t_ else [lambda: None] * 3
            loads, sh1, sh2, sh3, low, turned, up, key = mix_pieces(t_ + 1) if t_ + 1 < NT else [lambda: None] * 8
            work = iter([(mean,), (var,), (end, loads), (), (sh1,), (sh2,), (sh3,), (low,), (turned, up), (key,)])

            def between():
                for piece in next(work):
                    piece()

            stt(bt_, kk, -1.0, a_, MUL, MUL, V.t)
            stt(kh, a_, -1.0, kaw, ADD, MUL, V.t)
            stt(kh, kh, 1.0, k_, ADD, MUL, V.t)
            t_kh = V.t
            tt(V, e2, r_, kh, MUL, V.t)
            tt(V, e2, e2, rkw, MUL, V.t)
            red(sb8, h3(e2), ADD, V.t)
            t_e2 = V.t
            act(e1, bc.ap, ACT.Exp, t_cum, V.t)
            tt(V, r_, r_, e1, MUL, S.t)
            t_Rp = V.t
            act(e1, bc.ap, ACT.Exp, V.t, scale=-1.0)
            tt(V, L, bc.ap, L, SUB, S.t, t_pc)
            bc.give(V.t)
            act(e2, L, ACT.Exp, V.t)
            act(pcc, bp.v(4, 2), ACT.Exp, t_pc)
            bp.give(S.t)
            tt(V, kk, kk, e2, MUL, S.t)
            tt(V, kh, kh, e1, MUL)
            tt(V, bt_, bt_, e1, MUL)
            t_all = V.t
            for c in range(2):
                tt(G, PCm[:, c], bx(C["bd"], 1, (P, 4, P)), bx(pcc[:, :, c], 2, (P, 4, P)), MUL, S.t)
            t_PC = G.t
            trickle(6)
            for n, (src, dst) in enumerate(((kk, X1[:, :, 0]), (r_, X1[:, :, 1]), (bt_, BK[:, :, 0]), (kh, BK[:, :, 1]))):
                turn(t_all, src, dst, V if n % 2 else S)
            t_X = (V.t, S.t)
            mk = bx(K2["mm"], 1, (P, 2, 256))
            for e in range(2):
                rw = slice(64 * e, 64 * e + 64)
                for p in range(4):
                    b = Bank()
                    PE.wait(*b.w, *t_X)
                    x1 = X1[rw, p].rearrange("p a b -> p (a b)")
                    mm(b.ap[:, 0:256], BK[rw, p, 0, :], x1, True, True)
                    mm(b.ap[:, 256:512], BK[rw, p, 1, :], x1, True, True, inc=True)
                    tt(V, MM[:, e, p].rearrange("p (a b) c -> p a (b c)", a=2), b.v(2, 256), mk, MUL, PE.t)
                    b.give(V.t)
            t_MM = V.t
            for e in range(2):
                rw = slice(64 * e, 64 * e + 64)
                b = Bank()
                PE.wait(*b.w)
                for p in range(4):
                    mm(b.ap[:, p * P:(p + 1) * P], X1[rw, p, 0, :], BK[rw, p, 0, :], True, True, inc=(p == 3))
                tt(V, Xb[e], b.v(4, P), bx(K2["m1"], 1, (P, 4, P)), MUL, PE.t)
                b.give(V.t)
                tt(V, Xb[e], Xb[e], bx(ident, 1, (P, 4, P)), ADD, V.t)
                tt(G, XTb[e], MM[:, e, :, 0, :], bx(K2["mt"][:, 0:P], 1, (P, 4, P)), MUL, t_MM)
                tt(G, XTb[e], XTb[e], bx(ident, 1, (P, 4, P)), ADD, G.t)
            xt_t = [[V.t, G.t], [V.t, G.t]]
            am_w = [[], []]

            def masked(l, e):
                return tt(G, AMb[e], MM[:, e, :, 0, :], bx(K2["mt"][:, l * P:(l + 1) * P], 1, (P, 4, P)), MUL,
                          *am_w[e])

            am = [masked(1, e) for e in range(2)]
            trickle(4)
            for l in range(1, 6):
                t1 = []
                for e in range(2):
                    trickle(1)
                    b = Bank()
                    PE.wait(*b.w, am[e], *xt_t[e])
                    for p in range(4):
                        mm(b.ap[:, p * P:(p + 1) * P], AMb[e][:, p], Xb[e][:, p], True, True, inc=(p == 3))
                    am_w[e] = [PE.t]
                    if l < 5:
                        am[e] = masked(l + 1, e)
                    cp(S, T1b[e], b.v(4, P), PE.t)
                    b.give(S.t)
                    t1.append(S.t)
                for e in range(2):
                    ba = Bank() if l < 5 else None
                    trickle(1 - e)
                    bb = Bank()
                    PE.wait(*bb.w, t1[e])
                    if ba:
                        PE.wait(*ba.w)
                        for p in range(4):
                            mm(ba.ap[:, p * P:(p + 1) * P], XTb[e][:, p], T1b[e][:, p], True, True, inc=(p == 3))
                    for p in range(4):
                        mm(bb.ap[:, p * P:(p + 1) * P], T1b[e][:, p], XTb[e][:, p], True, True, inc=(p == 3))
                    if ba:
                        tt(V, Xb[e], Xb[e], ba.v(4, P), ADD, PE.t)
                        ba.give(V.t)
                    tt(V, XTb[e], XTb[e], bb.v(4, P), ADD, PE.t)
                    bb.give(V.t)
                    xt_t[e] = [V.t]
                between()
            trickle(2)
            BV, U, WT, SA = T1b[0].rearrange("p a b -> p (a b)"), T1b[1].rearrange("p a b -> p (a b)"), \
                AMb[0], AMb[1].rearrange("p a b -> p (a b)")
            hs = lambda h: slice(h * 64, h * 64 + 64)
            b = Bank()
            PE.wait(*b.w, V.t, t_p)
            for h in range(H):
                mm(b.ap[:, hs(h)], MM[:, h % 2, h // 2, 2, :], v_[:, hs(h)], True, True, inc=(h == 7))
            cp(S, BV, b.ap, PE.t)
            b.give(S.t)
            t_BV = S.t
            between()
            trickle(1)
            b = Bank()
            PE.wait(*b.w, t_BV)
            for h in range(H):
                mm(b.ap[:, hs(h)], XTb[h % 2][:, h // 2], BV[:, hs(h)], True, True, inc=(h == 7))
            cp(S, U, b.ap, PE.t)
            b.give(S.t)
            t_U = S.t
            between()
            b = Bank()
            PE.wait(*b.w)
            for e in range(2):
                for p in range(4):
                    h = 2 * p + e
                    mm(b.ap[64 * e:64 * e + 64, p * P:(p + 1) * P], kk[:, hs(h)], XTb[e][:, p], True, True,
                       inc=(e == 1 and p == 3))
            cp(S, WT, b.v(4, P), PE.t)
            b.give(S.t)
            t_WT = S.t
            between()
            by = Bank(po)
            for c in range(2):
                rw = slice(64 * c, 64 * c + 64)
                Tc, Tn = T_[cur], T_[(cur + 1) % 3]
                trickle(1)
                b = Bank()
                PE.wait(*b.w, t_WT, t_T)
                for p in range(4):
                    mm(b.ap[rw, p * P:(p + 1) * P], WT[:, p, rw], Tc[:, p], True, True, inc=(p == 3))
                tt(V, SA[rw, :], b.ap[rw, :], U[rw, :], ADD, PE.t, t_U)
                b.give(V.t)
                t_sa = V.t
                trickle(1)
                b = Bank()
                PE.wait(*b.w, *by.w, t_sa)
                for p in range(4):
                    mm(by.ap[rw, p * P:(p + 1) * P], X1[:, p, 1, rw], Tc[:, p], True, True, inc=(p == 3))
                t_by = PE.t
                for p in range(4):
                    cs = slice(p * P, (p + 1) * P)
                    mm(b.ap[:, cs], kh[rw, cs], v_[rw, cs], True, False)
                    mm(b.ap[:, cs], bt_[rw, cs], SA[rw, cs], False, True, inc=(p == 3))
                tt(V, Tn, Tc, b.v(4, P), ADD, PE.t)
                b.give(V.t)
                tt(V, Tn, Tn, PCm[:, c], MUL, V.t, t_PC)
                t_T = V.t
                cur = (cur + 1) % 3
                between()
            b = Bank()
            PE.wait(*b.w, t_sa)
            for h in range(H):
                mm(b.ap[:, hs(h)], MM[:, h % 2, h // 2, 1, :], SA[:, hs(h)], True, False)
                mm(b.ap[:, hs(h)], MM[:, h % 2, h // 2, 3, :], v_[:, hs(h)], False, True, inc=(h == 7))
            cp(S, y_, by.ap, t_by, t_y[0])
            by.give(S.t)
            tt(V, y_, y_, b.ap, ADD, PE.t, S.t)
            b.give(V.t)
        def split_ops(raw, hi, lo, toks, hi_toks, q):
            a = act(hi, raw, ACT.Copy, *toks, *hi_toks)
            return tt(q, lo, raw, hi.bitcast(F32), SUB, a)

        hring = Ring(2)
        loq = [V]

        class Stream:
            def __init__(self, srcs):
                self.srcs, self.loaded, self.split, self.at = srcs, [], [], 0

            def load_to(self, n):
                while len(self.loaded) < min(n, len(self.srcs)):
                    src = self.srcs[len(self.loaded)]
                    if len(src.shape) == 3:
                        self.loaded.append(wload((lambda s: s.rearrange("p (j n) -> p j n", j=src.shape[1]), src)))
                    else:
                        self.loaded.append(wload((lambda s: s, src)))

            def split_to(self, n):
                while len(self.split) < min(n, len(self.srcs)):
                    k, t = self.loaded[len(self.split)]
                    kh, wh = hring.take()
                    r = []
                    for o in range(0, 4096, 1024):
                        c = slice(o, o + 1024)
                        r.append(split_ops(wslot[k][:, c], whi[kh][:, c], wlo[k][:, c], [t], wh, loq[0]))
                    self.split.append((k, kh, r))

            def enter(self):
                self.load_to(self.at + 2)
                self.split_to(self.at + 1)
                self.load_to(self.at + 3)
                self.split_to(self.at + 2)
                k, kh, r = self.split[self.at]
                self.at += 1
                self.cur = (k, kh)
                return whi[kh], wlo[k], r

            def leave(self, *cur):
                k, kh = cur
                wring.give(k, PE.t)
                hring.give(kh, PE.t)

        def mm3(out_, lh, ll, rh, rl, start, stop, inc=False):
            mm(out_, lh, rh, start, False)
            mm(out_, lh, rl, False, False)
            mm(out_, ll, rh, False, stop, inc=inc)

        srcs = []
        for which, nm in ((0, "w_o_mla_2"), (1, "w_o_rwkv_2")):
            srcs += [A[nm].rearrange("(j p) n -> p j n", p=P)]
        srcs += [A["w_out_2"][:, n * 512:n * 512 + 512].rearrange("(j p) n -> p j n", p=P) for n in range(2)]
        srcs += [A["w_query_2"][:, n * 512:n * 512 + 512].rearrange("(j p) n -> p j n", p=P) for n in range(4)]
        srcs += [A["down"][u] for u in range(NE_)]
        for i in range(NU - NE_):
            srcs += [A["down"][NE_ + i]]
            srcs += [A["up"][i]]
            srcs += [A["up"][NE_ + i]]
        ws_ = Stream(srcs)

        def jn(ap):
            return ap.rearrange("p (j n) -> p j n", j=NJ)

        def up_chunk(wh, wl, m, ht=()):
            b = Bank()
            PE.wait(*b.w)
            for j in range(NJ):
                if ht:
                    PE.wait(ht[j])
                c = slice(m * P, (m + 1) * P)
                mm3(b.ap, wh[:, j, c], wl[:, j, c], hTh[:, j, :], hTl[:, j, :], j == 0, j == NJ - 1,
                    inc=(j == NJ - 1))
            return b

        def jn(ap):
            return ap.rearrange("p (j n) -> p j n", j=NJ)

        def jproj(wh, wl, t_, lh, ll, n, ht=()):
            b = Bank()
            PE.wait(*b.w)
            c = slice(t_ * P, (t_ + 1) * P)
            for j in range(n):
                if ht:
                    PE.wait(ht[j])
                mm3(b.ap, lh[:, j, c], ll[:, j, c], wh[:, j, :], wl[:, j, :], j == 0, j == n - 1, inc=(j == n - 1))
            return b

        for _ in gates_left:
            pass
        t_gt = [(x[0], x[1]) for x in lngt]
        wring.give(kup, PE.t, *t_gt)
        ws_.load_to(2)
        for piece in tail_pieces(NT - 1):
            piece()
        bt = [*barrier(), t_y[0], *t_gt]
        if stop == "rwkv":
            return finish(nc, ctx, (PE, V, S, G, SP), ldone)

        ph = Space(high[:, :], NT * 512, hi_at - nlow - NT * 512)
        xt = ph.get(NT, D)
        mix = ph.get(NT, D)
        orr = ph.get(NT, 512)
        assert ph.at == a_at - nlow + 4096
        oT = [ph.get(4, 512) for _ in range(2)]
        oTl = [rview(a_at + 4096 + 2048 * i, 4, 512) for i in range(2)]
        oTh = [rview(nlow, 4, 512), rview(a_at + 2048, 4, 512)]
        ss3 = ph.get(16)
        gates_ = [xt, Space(high[:, :], hi_at - nlow, 4096).get(NT, D)]
        t_gt = [load(gates_[i], A["gt"][i], *bt, ln=next(lines)) for i in range(2)]
        t_or = load(orr, oro.rearrange("(t p) d -> p t d", p=P), *bt, q=G, ln=next(lines))
        ot = [[], []]
        for which, src, w_ in ((0, omla, ()), (1, orr, (t_or,))):
            tk = []
            for j in range(4):
                b = Bank()
                PE.wait(*b.w, *w_)
                for t_ in range(NT):
                    tr(b.ap[:, t_ * P:(t_ + 1) * P], src[:, t_, j * P:(j + 1) * P], inc=(t_ == NT - 1))
                q = V if j % 2 else S
                tk.append(cp(q, oT[which][:, j, :], b.ap, PE.t))
                b.give(q.t)
            for j in range(4):
                ot[which].append(split_ops(oT[which][:, j, :], oTh[which][:, j, :], oTl[which][:, j, :],
                                           [tk[j], PE.t], (), V))
            wh, wl, r = ws_.enter()
            cur = ws_.cur
            PE.wait(*r, *ot[which])
            wh, wl = [x.rearrange("p (j n) -> p j n", j=4) for x in (wh, wl)]
            for n in range(2):
                nc_ = slice(n * 512, n * 512 + 512)
                for t_ in range(NT):
                    b = jproj(wh[:, :, nc_], wl[:, :, nc_], t_, oTh[which], oTl[which], 4)
                    dst, gate = mix[:, t_, nc_], gates_[which][:, t_, nc_]
                    if which == 0:
                        stt(dst, gate, 1.0, b.ap, ADD, MUL, PE.t, t_gt[0])
                        b.give(V.t)
                    else:
                        stt(gate, gate, 1.0, b.ap, ADD, MUL, PE.t, t_gt[1])
                        b.give(V.t)
                        tt(G, dst, dst, gate, ADD, V.t)
            ws_.leave(*cur)
        t_x2 = load(xt, A["xs"].rearrange("(t p) d -> p t d", p=P), V.t, G.t, q=G, ln=next(lines))
        t_h1 = PE.t
        mtok = transpose_into_hT(mix, NJ, (G.t, V.t))
        ht = [split_ops(hT[:, j, :], hTh[:, j, :], hTl[:, j, :], mtok, (t_h1,), V) for j in range(NJ)]
        x3t, xd3 = [], []
        for n in range(2):
            wh, wl, r = ws_.enter()
            cur = ws_.cur
            PE.wait(*r)
            nc_ = slice(n * 512, n * 512 + 512)
            for t_ in range(NT):
                b = jproj(jn(wh), jn(wl), t_, hTh, hTl, NJ, ht if n == t_ == 0 else ())
                stt(mix[:, t_, nc_], b.ap, 0.5, gt1_2[:, nc_], MUL, MUL, PE.t)
                b.give(V.t)
                t_x3 = tt(G, xt[:, t_, nc_], xt[:, t_, nc_], mix[:, t_, nc_], ADD, V.t, t_x2)
                if n == 1 and t_:
                    xd3.append(normalise_tile(xt, t_ - 1, (mix, ss3), x3t[-1]))
                x3t.append(t_x3)
            ws_.leave(*cur)
        xd3.append(normalise_tile(xt, NT - 1, (mix, ss3), x3t[-1]))
        dbg("x2", xt, t_x3)
        t_xsp = load(A["xs"].rearrange("(t p) d -> p t d", p=P), xt, t_x3, ln=next(lines))
        hready = make_hT(xt, (t_x3,), 32, t_col3, (mix, ss3), (), xd3)
        dbg("h3T", hT, *hready)
        bt = barrier()
        for q in QS:
            q.wait(t_xsp)

        ph = Space(high[:, :], 0, hi_at - nlow)
        loq[0] = G
        hkT = ph.get(3, 512)
        ust = [ph.get(512) for _ in range(2)]
        early0 = ph.at
        early = ph.rest()

        ht = [split_ops(hT[:, j, :], hTh[:, j, :], hTl[:, j, :], hready, (), V) for j in range(NJ)]
        sk = early.get(2, P)
        qT = early.get(16, 512)
        ln8 = next(lines)
        load(sk[:, 0, :], A["sub_keys1_2"], *bt, t_xsp, q=G, ln=ln8)
        t_sk = load(sk[:, 1, :], A["sub_keys2_2"], q=G, ln=ln8)

        for n in range(4):
            wh, wl, r = ws_.enter()
            cur = ws_.cur
            PE.wait(*r)
            for m in range(4):
                b = up_chunk(jn(wh), jn(wl), m, ht if n == m == 0 else ())
                cp(S, qT[:, 4 * n + m, :], b.ap, PE.t)
                b.give(S.t)
            ws_.leave(*cur)
        t_qT = S.t

        usr = Ring(2)
        lnu = [line(f"u{i}") for i in range(2)]
        st_ = {}

        def early_piece(u, m):
            if m == 0:
                wh, wl, r = ws_.enter()
                PE.wait(*r)
                st_["w"] = (jn(wh), jn(wl), ws_.cur)
            wh, wl, cur = st_["w"]
            b = up_chunk(wh, wl, m)
            if m == 3:
                ws_.leave(*cur)
            kx, wx = usr.take()
            act(ust[kx], b.ap, ACT.Gelu_apprx_tanh, PE.t, *wx)
            b.give(S.t)
            t = load(A["au"][u][:, m * 512:m * 512 + 512], ust[kx], S.t, ln=lnu[kx])
            usr.give(kx, t)

        for u in range(NE_):
            for m in range(4):
                side.append(lambda u=u, m=m: early_piece(u, m))
        side_every[0] = 1
        sb_ = early.get(2, 16, P)
        sbr = Ring(2)
        v16 = early.get(16, 16)
        i16 = early.get(16, 16).bitcast(U32)
        if16 = early.get(16, 16)
        cand = early.get(H, 256)
        cv = early.get(H, 16)
        ci = early.get(H, 16).bitcast(U32)
        cif = early.get(4, H, 16)
        eq = cand.rearrange("p h (a b) -> p h a b", a=16)
        e3 = early.get(3, P)
        NEGF = -3.0e38
        s_free = []

        def top16(n, src, vals, idx):
            def mx(m, o):
                s_, v_ = src(m), vals(m)[:, o:o + 8]
                return V.do(lambda e: e.max(v_, s_), tk[m])

            def ix(m, o):
                s_, v_, i_ = src(m), vals(m)[:, o:o + 8], idx(m)[:, o:o + 8]
                return V.do(lambda e: e.max_index(i_, v_, s_), tk[m])

            def rp(m, o):
                s_, v_ = src(m), vals(m)[:, 0:8]
                return V.do(lambda e: e.match_replace(s_, v_, s_, NEGF), tk[m])

            tk = [V.t] * n
            for f, o in ((mx, 0), (ix, 0), (rp, 0), (mx, 8), (ix, 8)):
                tk = [f(m, o) for m in range(n)]
                fill()

        def scores(t_):
            kx, wx = sbr.take()
            sc = sb_[:, kx]
            for n in range(4):
                b = Bank()
                PE.wait(*b.w, t_qT, t_sk)
                for m in range(4):
                    mm(b.ap[:, m * P:(m + 1) * P], qT[:, 4 * n + m, t_ * P:(t_ + 1) * P], sk[:, m % 2, :], True, True,
                       inc=(m == 3))
                cp(S, sc[:, 4 * n:4 * n + 4, :], b.v(4, P), PE.t, *wx)
                b.give(S.t)
            return kx, S.t

        nxt_sc = scores(0)
        for t_ in range(NT):
            kx, t_sc = nxt_sc
            sc = sb_[:, kx]
            if t_ + 1 < NT:
                nxt_sc = scores(t_ + 1)
            fill()
            V.wait(t_sc)
            top16(16, lambda m: sc[:, m, :], lambda m: v16[:, m, :], lambda m: i16[:, m, :])
            sbr.give(kx, V.t)
            cp(V, if16, i16, V.t)
            vv = v16.rearrange("p (h w) k -> p h w k", w=2)
            ii = if16.rearrange("p (h w) k -> p h w k", w=2)
            tcd = V.t
            for h in range(H):
                cd = cand[:, h, :].rearrange("p (a b) -> p a b", a=16)
                tt(V, cd, bx(vv[:, h, 0], 2, (P, 16, 16)), bx(vv[:, h, 1], 1, (P, 16, 16)), ADD, tcd)
            top16(8, lambda h: cand[:, h, :], lambda h: cv[:, h, :], lambda h: ci[:, h, :])
            cu = cif[:, 3].bitcast(U32)
            V.do(lambda e: e.tensor_scalar(cu, ci, 4, None, ALU.logical_shift_right), V.t)
            cp(V, cif[:, 0], cu, V.t)
            V.do(lambda e: e.tensor_scalar(cu, ci, 15, None, ALU.bitwise_and), V.t)
            cp(V, cif[:, 1], cu, V.t)
            io = C["iota"][:, 0:16]
            for w_ in range(2):
                te0 = V.t
                te = [tt(V, eq[:, h], bx(cif[:, w_, h], 2, (P, 16, 16)), bx(io, 1, (P, 16, 16)), EQ, te0)
                      for h in range(H)]
                for h in range(H):
                    tt(V, eq[:, h], eq[:, h], bx(ii[:, h, w_], 1, (P, 16, 16)), MUL, te[h])
                red(e3[:, w_, :].rearrange("p (h k) -> p h k", h=H), eq, ADD, V.t, *s_free)
                fill()
            cpm = cif[:, 2, :, 0]
            cp(V, cpm, cv[:, :, 0], V.t)
            tt(V, cv, cv, bx(cpm, 2, (P, H, 16)), SUB, V.t)
            act(cv, cv, ACT.Exp, V.t)
            red(cpm, cv, ADD, S.t)
            V.do(lambda e: e.reciprocal(cpm, cpm), V.t)
            tt(V, e3[:, 2, :].rearrange("p (h k) -> p h k", h=H), cv, bx(cpm, 2, (P, H, 16)), MUL, V.t)
            b = Bank()
            PE.wait(*b.w, V.t)
            for w_ in range(3):
                tr(b.ap[:, w_ * P:(w_ + 1) * P], e3[:, w_, :], inc=(w_ == 2))
            s_free = [PE.t]
            cp(S, hkT[:, :, t_ * P:(t_ + 1) * P], b.ap[:, 0:384].rearrange("p (a b) -> p a b", a=3), PE.t)
            b.give(S.t)

        bt = barrier()
        TB, NTB = 32, 16
        ls = Space(high[:, :], early0, hi_at - nlow - early0)
        stg = [ls.get(P, TB) for _ in range(2)]
        oh = [ls.get(2, 4, P) for _ in range(8)]
        ohr = Ring(8)
        stgr = Ring(2)
        loq[0] = V
        gd_ = A["gd"]
        lng = [line("g2"), line("g3")]
        iota = C["iota"]
        qi = 0
        def onehots(tok):
            kx, wx = ohr.take()
            a = tt(V, oh[kx], bx(bx(iota, 1, (P, 4, P)), 1, (P, 2, 4, P)),
                   bx(hkT[:, 0:2, tok:tok + 4], 3, (P, 2, 4, P)), EQ, *wx)
            o1 = oh[kx][:, 0]
            return kx, tt(G, o1, o1, bx(hkT[:, 2, tok:tok + 4], 2, (P, 4, P)), MUL, a)

        ahead = [onehots(4 * i) for i in range(4)]
        for tb in range(NTB):
            ks, wst = stgr.take()
            for q4 in range(TB // 4):
                tok = tb * TB + q4 * 4
                if tok + 16 < 512:
                    ahead.append(onehots(tok + 16))
                qi += 1
                if qi % 8 == 3 and side:
                    side.pop(0)()
                b = Bank()
                kx, c = ahead.pop(0)
                o1, o2_ = oh[kx][:, 0], oh[kx][:, 1]
                PE.wait(*b.w, c)
                for u in range(4):
                    mm(b.ap[:, u * P:(u + 1) * P], o2_[:, u], o1[:, u], True, True, inc=(u == 3))
                ohr.give(kx, PE.t)
                src = b.v(4, P).rearrange("p u a -> p a u")
                cp(S, stg[ks][:, :, q4 * 4:q4 * 4 + 4], src, PE.t, *wst)
                b.give(S.t)
            t_g = SP.dma(lng[tb % 2], gd_[tb].rearrange("b a t -> b (a t)"), stg[ks].rearrange("p a t -> p (a t)"), S.t)
            stgr.give(ks, t_g)
        drain_side()
        t_gd = [(l[0], l[1]) for l in (*lng, *lnu)]
        for q in (V, G, S, SP):
            q.wait(*t_gd)
        bt = [q.t for q in QS]
        SP.wait(*bt)
        V.wait(*bt)
        G.wait(*bt)
        S.wait(*bt)

        ls = Space(high[:, :], 0, hi_at - nlow)
        Y = ls.get(NT, D)
        Gb = [ls.get(NTB, 4, TB) for _ in range(2)]
        NA = 4
        assert ls.at == a_at - nlow
        Ab = [ls.get(4, 512) for _ in range(NA)]
        Al = [rview(a_at + 2048 * i, 4, 512) for i in range(NA)]
        assert ls.at == m_at - nlow
        Ah = [rview(m_at + 2048 * i, 4, 512) for i in range(2)]
        Aring, mring, gring = Ring(NA), Ring(2), Ring(2)
        gline = [line("g0"), line("g1")]
        aline = [line(f"a{i}") for i in range(NA)]
        where, mtok_, gload, ytok = {}, {}, {}, {}

        def fetch(u):
            kg, wg = gring.take()
            gload[u] = (kg, G.dma(gline[kg], Gb[kg].rearrange("p b a t -> p b (a t)"),
                                  gd_[:, :, 4 * u:4 * u + 4, :].rearrange("b p a t -> p b (a t)"), *wg))
            if u < NE_:
                ka_, wa = Aring.take()
                where[u] = (ka_, [G.dma(aline[ka_], Ab[ka_].rearrange("p m t -> p (m t)"), A["au"][u], *wa)] * 4)

        def compute(u, spilled):
            wh, wl, r = ws_.enter()
            cur = ws_.cur
            gates(spilled)
            ka_, wa = Aring.take()
            toks = []
            PE.wait(*r)
            for m in range(4):
                b = up_chunk(jn(wh), jn(wl), m)
                toks.append(act(Ab[ka_][:, m, :], b.ap, ACT.Gelu_apprx_tanh, PE.t, *wa))
                b.give(S.t)
            ws_.leave(*cur)
            where[u] = (ka_, toks)

        def gates(u):
            kg, t = gload[u]
            ka_, toks = where[u]
            km, wm = mring.take()
            r = []
            for m in range(4):
                a = Ab[ka_][:, m, :].rearrange("p (b t) -> p b t", b=NTB)
                x = tt(V, a, a, Gb[kg][:, :, m, :], MUL, t, toks[m])
                r.append(split_ops(Ab[ka_][:, m, :], Ah[km][:, m, :], Al[ka_][:, m, :], [x], wm, V))
            gring.give(kg, V.t)
            mtok_[u] = (ka_, km, r)

        def down_sum(u):
            ka_, km, ta = mtok_[u]
            wh, wl, r = ws_.enter()
            cur = ws_.cur
            wh, wl = [x.rearrange("p (m n) -> p m n", m=4) for x in (wh, wl)]
            for t_ in range(NT):
                for n in range(2):
                    b = Bank()
                    PE.wait(*b.w, *ta, *r)
                    tc, nc_ = slice(t_ * P, (t_ + 1) * P), slice(n * 512, n * 512 + 512)
                    for m in range(4):
                        mm3(b.ap, Ah[km][:, m, tc], Al[ka_][:, m, tc], wh[:, m, nc_], wl[:, m, nc_],
                            m == 0, m == 3, inc=(m == 3))
                    y = Y[:, t_, nc_]
                    if (t_, n) in ytok:
                        ytok[t_, n] = tt(V, y, y, b.ap, ADD, PE.t, ytok[t_, n])
                    else:
                        ytok[t_, n] = cp(V, y, b.ap, PE.t)
                    b.give(V.t)
            ws_.leave(*cur)
            Aring.give(ka_, PE.t)
            mring.give(km, PE.t)

        for i in range(NU - NE_):
            if i == 0:
                fetch(0)
            fetch(NE_ + i)
            compute(NE_ + i, i)
            gates(NE_ + i)
            if i + 1 < NU - NE_:
                fetch(i + 1)
            down_sum(i)
            down_sum(NE_ + i)
        xo = Space(high[:, :], a_at - nlow, 4096).get(NT, D)
        lno = next(lines)
        t_xl = load(xo, A["xs"].rearrange("(t p) d -> p t d", p=P), PE.t, V.t, G.t, q=S, ln=next(lines))
        for t_ in range(NT):
            tt(V, Y[:, t_, :], Y[:, t_, :], gt2_2, MUL, V.t)
            tt(V, Y[:, t_, :], Y[:, t_, :], xo[:, t_, :], ADD, V.t, t_xl)
            to = SP.dma(lno, out[t_ * P:(t_ + 1) * P, :], Y[:, t_, :], V.t)
        ldone.append(to)
        return finish(nc, ctx, (PE, V, S, G, SP), ldone)


def finish(nc, ctx, queues, ldone):
    PE, V, S, G, SP = queues
    SP.wait(*ldone)
    block = ctx.enter_context(nc.Block())

    @block.sync
    def _(e):
        SP.emit(e)

    @block.gpsimd
    def _(e):
        G.emit(e)

    @block.scalar
    def _(e):
        S.emit(e)

    @block.vector
    def _(e):
        V.emit(e)

    @block.tensor
    def _(e):
        PE.emit(e)


def layout(inputs):
    f = lambda n: np.asarray(inputs[n])
    col = lambda a, n: np.ascontiguousarray(a.reshape(n, 128).T)
    m = {}
    m["cst"], m["c1"], m["c2"] = constants()
    m["x"] = f("x")[0]
    m["c"] = col(f("c")[0], 8)
    m["c_2"] = col(f("c_2")[0], 8)
    p1, p2 = f("positions")[0], f("positions_2")[0]
    ce = p1[31::16]
    ce = np.concatenate([ce, ce[-1:]])
    ce = np.concatenate([ce, ce, ce, ce])
    m["pos"] = np.ascontiguousarray(np.concatenate([p1.reshape(4, 128), ce[None], p2.reshape(4, 128)]).T)
    m["w_ada"], m["w_ada_2"] = f("w_ada")[0], f("w_ada_2")[0]
    m["b_ada_c"], m["b_ada_2_c"] = col(f("b_ada")[0], 24), col(f("b_ada_2")[0], 48)
    m["b_ada_r"], m["b_ada_2_r"] = f("b_ada")[0], f("b_ada_2")[0]
    for n in ("g_pre", "norm_mix_2", "norm_ffn_2"):
        m[n] = col(f(n)[0], 8)
    m["g_post"] = f("g_post")[0]
    for n in ("w_in", "w_out", "cmp_w1_k", "cmp_w1_v", "cmp_w2_k", "cmp_w2_v", "w_in_2", "w_uq_2", "w_ukv_2",
              "w_o_mla_2", "w_decay_up_2", "w_aaa_up_2", "w_gate_up_2", "w_o_rwkv_2", "w_out_2", "w_query_2",
              "mu_shift_2", "decay_base_2", "aaa_base_2", "k_k_2", "k_a_2", "ln_x_w_2", "ln_x_b_2",
              "q_norm_2", "k_norm_2"):
        m[n] = f(n)[0]
    m["r_k_2"] = f("r_k_2")[0].reshape(512)
    for n in ("cmp_pe_k", "cmp_pe_v"):
        m[n] = col(f(n)[0].reshape(-1), 16)
    m["q_a_norm_2"] = col(f("q_a_norm_2")[0], 2)
    m["kv_a_norm_2"] = col(f("kv_a_norm_2")[0], 1)
    for n in ("sub_keys1_2", "sub_keys2_2"):
        m[n] = f(n)[0].T
    m["down"] = f("expert_down_2")[0].reshape(32, 512, 8, 128).transpose(0, 3, 2, 1).reshape(32, 128, 4096)
    m["up"] = f("expert_up_2")[0].reshape(32, 4, 128, 1024).transpose(0, 2, 1, 3).reshape(32, 128, 4096)
    return {k: np.ascontiguousarray(v) for k, v in m.items()}


def program(nc, shapes, tap=None, stop=None):
    A = {}
    for name, (shape, dt) in shapes.items():
        A[name] = nc.dram_tensor("in_" + name, shape, dt, kind="ExternalInput").ap()
    for name, shape in (("xs", (512, D)), ("ps", (513, RW)), ("orw", (512, 512)), ("gd", (16, P, P, 32)), ("gt", (2, P, NT, D)), ("au", (NE_, P, 2048))):
        A[name] = nc.dram_tensor("scratch_" + name, shape, F32, kind="Internal").ap()
    out = nc.dram_tensor("out_0", (512, D), F32, kind="ExternalOutput").ap()
    build(nc, A, out, tap, stop)


def kernel(**inputs):
    import concourse.bacc as bacc
    from concourse.bass_utils import run_bass_kernel_spmd

    arrays = layout(inputs)
    nc = bacc.Bacc("TRN2", target_bir_lowering=False, num_devices=1)
    program(nc, {k: (v.shape, mybir.dt.from_np(v.dtype)) for k, v in arrays.items()})
    r = run_bass_kernel_spmd(nc, [{"in_" + k: v for k, v in arrays.items()}], core_ids=[0])
    return r.results[0]["out_0"].reshape(1, 512, 1024)
```
